# Optimizing a Trainium2 kernel written in Bass

```python
import math
import jax
import jax.numpy as jnp
from jax import lax
import numpy as np

D_MODEL = 2048
BATCH = 1
SEQ = 256
DEPTH = 2

N_A_LAYERS = DEPTH // 2
N_B_LAYERS = DEPTH - N_A_LAYERS

SSM_WIDTH = D_MODEL // 2
SSM_GROUP = 16
SSM_GROUPS = SSM_WIDTH // SSM_GROUP
SSM_STATE = 64
DT_MIN = 0.001
DT_MAX = 0.1

N_HEADS = 16
HEAD_DIM = 128
N_KV_HEADS = 4
HEADS_PER_KV = N_HEADS // N_KV_HEADS
ATTN_WIDTH = N_HEADS * HEAD_DIM
KV_WIDTH = N_KV_HEADS * HEAD_DIM
N_BRANCH = 3
CMP_BLOCK = 32
CMP_STRIDE = 16
SEL_BLOCK = 64
N_SELECT = 16
WINDOW = 512
Q_BLOCK = 64
B_IN_WIDTH = ATTN_WIDTH * (1 + N_BRANCH) + N_BRANCH * N_HEADS

LN_EPS = 1e-5
DEEPNORM_ALPHA = (2 * DEPTH) ** 0.25
DEEPNORM_BETA = (8 * DEPTH) ** -0.25
MASK_VALUE = -1e30
FORCE_SCORE = 1e6


def layer_norm(x, g, b):
    x32 = x.astype(jnp.float32)
    mu = jnp.mean(x32, axis=-1, keepdims=True)
    var = jnp.mean(jnp.square(x32 - mu), axis=-1, keepdims=True)
    return ((x32 - mu) * lax.rsqrt(var + LN_EPS) * g.astype(jnp.float32) + b.astype(jnp.float32)).astype(x.dtype)

def _complex_linear_combine(e1, e2):
    a1r, a1i, b1r, b1i = e1
    a2r, a2i, b2r, b2i = e2
    return (a2r * a1r - a2i * a1i,
            a2r * a1i + a2i * a1r,
            a2r * b1r - a2i * b1i + b2r,
            a2r * b1i + a2i * b1r + b2i)

def s5_mixer(x, w_in, lam_re, lam_im, log_dt, b_re, b_im, c_re, c_im, d_skip, w_glu, b_glu, w_out):
    bsz, seq, _ = x.shape
    f32 = jnp.float32
    u, z = jnp.split(x @ w_in, 2, axis=-1)
    lr = lam_re.astype(f32)
    li = lam_im.astype(f32)
    dt = jnp.exp(log_dt.astype(f32))[:, None]
    mag = jnp.exp(lr * dt)
    ar = mag * jnp.cos(li * dt)
    ai = mag * jnp.sin(li * dt)
    inv_abs2 = 1.0 / (lr * lr + li * li)
    cr = ((ar - 1.0) * lr + ai * li) * inv_abs2
    ci = (ai * lr - (ar - 1.0) * li) * inv_abs2
    br = b_re.astype(f32)
    bi = b_im.astype(f32)
    bbar_r = cr[..., None] * br - ci[..., None] * bi
    bbar_i = cr[..., None] * bi + ci[..., None] * br
    ug = jnp.swapaxes(u, 0, 1).astype(f32).reshape(seq, bsz, SSM_GROUPS, SSM_GROUP)
    bu_r = jnp.einsum('lbgc,gpc->lbgp', ug, bbar_r)
    bu_i = jnp.einsum('lbgc,gpc->lbgp', ug, bbar_i)
    a_shape = (seq, 1, SSM_GROUPS, SSM_STATE)
    _, _, h_r, h_i = lax.associative_scan(
        _complex_linear_combine,
        (jnp.broadcast_to(ar, a_shape), jnp.broadcast_to(ai, a_shape), bu_r, bu_i),
        axis=0)
    y = (jnp.einsum('gcp,lbgp->lbgc', c_re.astype(f32), h_r)
         - jnp.einsum('gcp,lbgp->lbgc', c_im.astype(f32), h_i))
    y = jnp.swapaxes(y.reshape(seq, bsz, SSM_WIDTH), 0, 1).astype(x.dtype) + d_skip * u
    g = jax.nn.gelu(y)
    y = g * jax.nn.sigmoid(g @ w_glu + b_glu)
    return (y * jax.nn.silu(z)) @ w_out

def shared_kv(h, kv_w, pos_k, w1_k, w2_k, pos_v, w1_v, w2_v):
    bsz, seq, _ = h.shape
    kv = (h @ kv_w).reshape(bsz, seq, 2 * N_BRANCH, N_KV_HEADS, HEAD_DIM)
    k_c, v_c, k_s, v_s, k_w, v_w = [kv[:, :, i] for i in range(2 * N_BRANCH)]
    n_cmp = (seq - CMP_BLOCK) // CMP_STRIDE + 1
    idx = jnp.arange(n_cmp)[:, None] * CMP_STRIDE + jnp.arange(CMP_BLOCK)[None, :]

    def compress(t, pos, w1, w2):
        blk = t[:, idx] + pos[None, None, :, None, :]
        blk = jnp.moveaxis(blk, 3, 2).reshape(bsz, n_cmp, N_KV_HEADS, CMP_BLOCK * HEAD_DIM)
        return jax.nn.gelu(blk @ w1) @ w2

    return (compress(k_c, pos_k, w1_k, w2_k), compress(v_c, pos_v, w1_v, w2_v), k_s, v_s, k_w, v_w)

def masked_softmax(s, valid):
    s = jnp.where(valid, s, MASK_VALUE)
    m = jnp.max(s, axis=-1, keepdims=True)
    e = jnp.where(valid, jnp.exp(s - m), 0.0)
    return e / jnp.maximum(jnp.sum(e, axis=-1, keepdims=True), 1e-30)

def nsa_attention(q, k_cmp, v_cmp, k_slc, v_slc, k_win, v_win):
    bsz, seq = q.shape[:2]
    dtype = q.dtype
    f32 = jnp.float32
    n_q = seq // Q_BLOCK
    n_cmp = k_cmp.shape[1]
    n_sblk = seq // SEL_BLOCK
    n_sel = min(N_SELECT, n_sblk)
    scale = HEAD_DIM ** -0.5
    cmp_start = jnp.arange(n_cmp) * CMP_STRIDE
    cmp_end = cmp_start + CMP_BLOCK - 1
    sel_start = jnp.arange(n_sblk) * SEL_BLOCK
    overlap = ((cmp_start[:, None] < sel_start[None, :] + SEL_BLOCK)
               & (cmp_end[:, None] >= sel_start[None, :])).astype(f32)
    kb_s = k_slc.reshape(bsz, n_sblk, SEL_BLOCK, N_KV_HEADS, HEAD_DIM).transpose(0, 3, 1, 2, 4)
    vb_s = v_slc.reshape(bsz, n_sblk, SEL_BLOCK, N_KV_HEADS, HEAD_DIM).transpose(0, 3, 1, 2, 4)
    k_w_pad = jnp.pad(k_win, ((0, 0), (WINDOW, 0), (0, 0), (0, 0)))
    v_w_pad = jnp.pad(v_win, ((0, 0), (WINDOW, 0), (0, 0), (0, 0)))
    qg = q.reshape(bsz, n_q, Q_BLOCK, N_KV_HEADS, HEADS_PER_KV, HEAD_DIM).transpose(1, 0, 2, 3, 4, 5)
    gather_blocks = jax.vmap(jax.vmap(lambda blocks, ids: blocks[ids]))
    blk_ids = jnp.arange(n_sblk)

    def block_fn(args):
        i, qb = args
        t = i * Q_BLOCK + jnp.arange(Q_BLOCK)
        qb = qb * scale
        s = jnp.einsum('bqghd,bngd->bghqn', qb, k_cmp).astype(f32)
        p_cmp = masked_softmax(s, cmp_end[None, :] <= t[:, None])
        o_cmp = jnp.einsum('bghqn,bngd->bqghd', p_cmp.astype(dtype), v_cmp)
        imp = jnp.einsum('bghqn,nj->bgqj', p_cmp, overlap)
        cur = t // SEL_BLOCK
        future = blk_ids[None, :] > cur[:, None]
        forced = ((blk_ids[None, :] == 0) | (blk_ids[None, :] == cur[:, None])
                  | (blk_ids[None, :] == cur[:, None] - 1))
        imp = jnp.where(future, MASK_VALUE, jnp.where(forced, FORCE_SCORE, imp))
        _, sel = lax.top_k(imp, n_sel)
        ks = gather_blocks(kb_s, sel).reshape(bsz, N_KV_HEADS, Q_BLOCK, n_sel * SEL_BLOCK, HEAD_DIM)
        vs = gather_blocks(vb_s, sel).reshape(bsz, N_KV_HEADS, Q_BLOCK, n_sel * SEL_BLOCK, HEAD_DIM)
        pos = (sel[..., None] * SEL_BLOCK + jnp.arange(SEL_BLOCK)).reshape(bsz, N_KV_HEADS, Q_BLOCK, n_sel * SEL_BLOCK)
        valid = (pos <= t[None, None, :, None])[:, :, None]
        s = jnp.einsum('bqghd,bgqkd->bghqk', qb, ks).astype(f32)
        p = masked_softmax(s, valid)
        o_slc = jnp.einsum('bghqk,bgqkd->bqghd', p.astype(dtype), vs)
        kw = lax.dynamic_slice_in_dim(k_w_pad, i * Q_BLOCK, WINDOW + Q_BLOCK, axis=1)
        vw = lax.dynamic_slice_in_dim(v_w_pad, i * Q_BLOCK, WINDOW + Q_BLOCK, axis=1)
        kpos = i * Q_BLOCK - WINDOW + jnp.arange(WINDOW + Q_BLOCK)
        valid = ((kpos[None, :] <= t[:, None]) & (kpos[None, :] > t[:, None] - WINDOW)
                 & (kpos[None, :] >= 0))
        s = jnp.einsum('bqghd,bkgd->bghqk', qb, kw).astype(f32)
        p = masked_softmax(s, valid)
        o_win = jnp.einsum('bghqk,bkgd->bqghd', p.astype(dtype), vw)
        return o_cmp, o_slc, o_win

    o_cmp, o_slc, o_win = lax.map(block_fn, (jnp.arange(n_q), qg))

    def unblock(o):
        return o.transpose(1, 0, 2, 3, 4, 5).reshape(bsz, seq, N_HEADS, HEAD_DIM)

    return (unblock(o_cmp), unblock(o_slc), unblock(o_win))

def nsa_mixer(x, w_in, w_out, shared):
    bsz, seq, _ = x.shape
    proj = x @ w_in
    q = proj[..., :ATTN_WIDTH].reshape(bsz, seq, N_HEADS, HEAD_DIM)
    z = proj[..., ATTN_WIDTH:ATTN_WIDTH * (1 + N_BRANCH)].reshape(bsz, seq, N_BRANCH, N_HEADS, HEAD_DIM)
    gate = jax.nn.sigmoid(proj[..., ATTN_WIDTH * (1 + N_BRANCH):].reshape(bsz, seq, N_BRANCH, N_HEADS))
    o = jnp.stack(nsa_attention(q, *shared), axis=2)
    y = jnp.sum(gate[..., None] * o * jax.nn.silu(z), axis=2).reshape(bsz, seq, ATTN_WIDTH)
    return y @ w_out

def first_inputs(seed: int = 0) -> dict:
    key = jax.random.key(seed)
    ks = jax.random.split(key, 24)
    nrm = jax.random.normal
    f32 = jnp.float32
    na, nb = N_A_LAYERS, N_B_LAYERS
    g, p, c, e = SSM_GROUPS, SSM_STATE, SSM_GROUP, SSM_WIDTH
    lam_im0 = math.pi * jnp.arange(p, dtype=f32)
    return {
        "x": nrm(ks[0], (BATCH, SEQ, D_MODEL), f32),
        "a_w_in": nrm(ks[1], (na, D_MODEL, 2 * e), f32) * D_MODEL ** -0.5,
        "a_lam_re": -0.5 + 0.01 * nrm(ks[2], (na, g, p), f32),
        "a_lam_im": lam_im0 + 0.01 * nrm(ks[3], (na, g, p), f32),
        "a_log_dt": jax.random.uniform(ks[4], (na, g), f32, math.log(DT_MIN), math.log(DT_MAX)),
        "a_b_re": nrm(ks[5], (na, g, p, c), f32) * (2 * c) ** -0.5,
        "a_b_im": nrm(ks[6], (na, g, p, c), f32) * (2 * c) ** -0.5,
        "a_c_re": nrm(ks[7], (na, g, c, p), f32) * p ** -0.5,
        "a_c_im": nrm(ks[8], (na, g, c, p), f32) * p ** -0.5,
        "a_d": nrm(ks[9], (na, e), f32),
        "a_w_glu": nrm(ks[10], (na, e, e), f32) * e ** -0.5,
        "a_b_glu": 0.01 * nrm(ks[11], (na, e), f32),
        "a_w_out": nrm(ks[12], (na, e, D_MODEL), f32) * e ** -0.5 * DEEPNORM_BETA,
        "kv_w": nrm(ks[13], (D_MODEL, 2 * N_BRANCH * KV_WIDTH), f32) * D_MODEL ** -0.5,
        "cmp_pos_k": 0.02 * nrm(ks[14], (CMP_BLOCK, HEAD_DIM), f32),
        "cmp_w1_k": nrm(ks[15], (CMP_BLOCK * HEAD_DIM, HEAD_DIM), f32) * (CMP_BLOCK * HEAD_DIM) ** -0.5,
        "cmp_w2_k": nrm(ks[16], (HEAD_DIM, HEAD_DIM), f32) * HEAD_DIM ** -0.5,
        "cmp_pos_v": 0.02 * nrm(ks[17], (CMP_BLOCK, HEAD_DIM), f32),
        "cmp_w1_v": nrm(ks[18], (CMP_BLOCK * HEAD_DIM, HEAD_DIM), f32) * (CMP_BLOCK * HEAD_DIM) ** -0.5,
        "cmp_w2_v": nrm(ks[19], (HEAD_DIM, HEAD_DIM), f32) * HEAD_DIM ** -0.5,
        "b_w_in": nrm(ks[20], (nb, D_MODEL, B_IN_WIDTH), f32) * D_MODEL ** -0.5,
        "b_w_out": nrm(ks[21], (nb, ATTN_WIDTH, D_MODEL), f32) * ATTN_WIDTH ** -0.5 * DEEPNORM_BETA,
        "ln_g": 1.0 + 0.01 * nrm(ks[22], (DEPTH, D_MODEL), f32),
        "ln_b": 0.01 * nrm(ks[23], (DEPTH, D_MODEL), f32),
    }

def first_block(x, a_w_in, a_lam_re, a_lam_im, a_log_dt, a_b_re, a_b_im, a_c_re, a_c_im, a_d,
              a_w_glu, a_b_glu, a_w_out, kv_w, cmp_pos_k, cmp_w1_k, cmp_w2_k, cmp_pos_v,
              cmp_w1_v, cmp_w2_v, b_w_in, b_w_out, ln_g, ln_b):
    shared = None
    for layer in range(DEPTH):
        if layer < N_A_LAYERS:
            i = layer
            y = s5_mixer(x, a_w_in[i], a_lam_re[i], a_lam_im[i], a_log_dt[i], a_b_re[i], a_b_im[i],
                         a_c_re[i], a_c_im[i], a_d[i], a_w_glu[i], a_b_glu[i], a_w_out[i])
        else:
            i = layer - N_A_LAYERS
            y = nsa_mixer(x, b_w_in[i], b_w_out[i], shared)
        x = layer_norm(DEEPNORM_ALPHA * x + y, ln_g[layer], ln_b[layer])
        if layer == N_A_LAYERS - 1:
            shared = shared_kv(x, kv_w, cmp_pos_k, cmp_w1_k, cmp_w2_k, cmp_pos_v, cmp_w1_v, cmp_w2_v)
    return x


DEPTH_2 = 1

DIFF_WIDTH = D_MODEL // 2
SB_WIDTH = D_MODEL - DIFF_WIDTH
DIFF_QK_DIM = 64
DIFF_V_DIM = 2 * DIFF_QK_DIM
DIFF_HEADS = DIFF_WIDTH // DIFF_V_DIM
SB_HEAD_DIM = 128
SB_HEADS = SB_WIDTH // SB_HEAD_DIM
D_FF = 4 * D_MODEL
ROPE_THETA = 500000.0
ROPE_FRACTION_DEN = 4
BLOCK_Q = 128
NORM_EPS = 1e-6
NEG_INF = -1e30
PROJ_SPLITS = (
    2 * DIFF_HEADS * DIFF_QK_DIM,
    2 * DIFF_HEADS * DIFF_QK_DIM,
    DIFF_HEADS * DIFF_V_DIM,
    SB_HEADS * SB_HEAD_DIM,
    SB_HEADS * SB_HEAD_DIM,
    SB_HEADS * SB_HEAD_DIM,
)
PROJ_WIDTH = sum(PROJ_SPLITS)


def rmsnorm(x, g):
    xf = x.astype(jnp.float32)
    y = xf * lax.rsqrt(jnp.mean(jnp.square(xf), axis=-1, keepdims=True) + NORM_EPS)
    return (y * g.astype(jnp.float32)).astype(x.dtype)

def partial_rotary(x, pos):
    d = x.shape[-1]
    rot = d // ROPE_FRACTION_DEN
    half = rot // 2
    inv_freq = ROPE_THETA ** (-jnp.arange(0, rot, 2, dtype=jnp.float32) / rot)
    ang = pos.astype(jnp.float32)[:, None] * inv_freq[None, :]
    cos = jnp.cos(ang)[None, :, None, :]
    sin = jnp.sin(ang)[None, :, None, :]
    xr = x[..., :rot].astype(jnp.float32)
    x1, x2 = xr[..., :half], xr[..., half:]
    rotated = jnp.concatenate([x1 * cos - x2 * sin, x2 * cos + x1 * sin], axis=-1)
    return jnp.concatenate([rotated.astype(x.dtype), x[..., rot:]], axis=-1)

def to_blocks(a):
    b, s = a.shape[0], a.shape[1]
    return jnp.swapaxes(a.reshape(b, s // BLOCK_Q, BLOCK_Q, *a.shape[2:]), 0, 1)

def from_blocks(a):
    a = jnp.swapaxes(a, 0, 1)
    return a.reshape(a.shape[0], a.shape[1] * a.shape[2], *a.shape[3:])

def differential_attention(q1, q2, k1, k2, v, lam):
    s_len = q1.shape[1]
    key_pos = jnp.arange(s_len)
    scale = DIFF_QK_DIM ** -0.5

    def block(args):
        qb1, qb2, qpos = args
        causal = key_pos[None, :] <= qpos[:, None]

        def probs(qb, k):
            sc = jnp.einsum("bqhd,bkhd->bhqk", qb, k,
                            preferred_element_type=jnp.float32) * scale
            return jax.nn.softmax(jnp.where(causal, sc, NEG_INF), axis=-1)

        w = probs(qb1, k1) - lam * probs(qb2, k2)
        return jnp.einsum("bhqk,bkhd->bqhd", w.astype(v.dtype), v)

    qpos = jnp.arange(s_len).reshape(-1, BLOCK_Q)
    out = lax.map(block, (to_blocks(q1), to_blocks(q2), qpos))
    return from_blocks(out)

def stick_breaking_attention(q, k, v):
    s_len = q.shape[1]
    key_pos = jnp.arange(s_len)
    scale = SB_HEAD_DIM ** -0.5

    def block(args):
        qb, qpos = args
        strict = key_pos[None, :] < qpos[:, None]
        z = jnp.einsum("bqhd,bkhd->bhqk", qb, k,
                       preferred_element_type=jnp.float32) * scale
        log_beta = jax.nn.log_sigmoid(z)
        log_one_minus = jnp.where(strict, jax.nn.log_sigmoid(-z), 0.0)
        log_stick = lax.cumsum(log_one_minus, axis=3, reverse=True) - log_one_minus
        a = jnp.where(strict, jnp.exp(log_beta + log_stick), 0.0)
        return jnp.einsum("bhqk,bkhd->bqhd", a.astype(v.dtype), v)

    qpos = jnp.arange(s_len).reshape(-1, BLOCK_Q)
    out = lax.map(block, (to_blocks(q), qpos))
    return from_blocks(out)

def second_inputs(seed: int = 0) -> dict:
    key = jax.random.key(seed)
    ks = jax.random.split(key, 16)
    f32 = jnp.float32

    def normal(k, shape, scale):
        return jax.random.normal(k, shape, f32) * scale

    return {
        "x": normal(ks[0], (BATCH, SEQ, D_MODEL), 1.0),
        "ln1": 1.0 + normal(ks[1], (DEPTH_2, D_MODEL), 0.02),
        "w_in": normal(ks[2], (DEPTH_2, D_MODEL, PROJ_WIDTH), D_MODEL ** -0.5),
        "lambda_q1": normal(ks[3], (DEPTH_2, DIFF_QK_DIM), 0.1),
        "lambda_k1": normal(ks[4], (DEPTH_2, DIFF_QK_DIM), 0.1),
        "lambda_q2": normal(ks[5], (DEPTH_2, DIFF_QK_DIM), 0.1),
        "lambda_k2": normal(ks[6], (DEPTH_2, DIFF_QK_DIM), 0.1),
        "diff_head_norm": 1.0 + normal(ks[7], (DEPTH_2, DIFF_V_DIM), 0.02),
        "sb_head_norm": 1.0 + normal(ks[8], (DEPTH_2, SB_HEAD_DIM), 0.02),
        "w_out": normal(ks[9], (DEPTH_2, DIFF_WIDTH + SB_WIDTH, D_MODEL), (DIFF_WIDTH + SB_WIDTH) ** -0.5),
        "ln2": 1.0 + normal(ks[10], (DEPTH_2, D_MODEL), 0.02),
        "w_mlp_in": normal(ks[11], (DEPTH_2, D_MODEL, D_FF), D_MODEL ** -0.5),
        "w_mlp_out": normal(ks[12], (DEPTH_2, D_FF, D_MODEL), 0.2 * D_FF ** -0.5),
        "ln_f": 1.0 + normal(ks[13], (D_MODEL,), 0.02),
    }

def second_block(x, ln1, w_in, lambda_q1, lambda_k1, lambda_q2, lambda_k2,
              diff_head_norm, sb_head_norm, w_out, ln2, w_mlp_in, w_mlp_out, ln_f):
    b, s_len, _ = x.shape
    pos = jnp.arange(s_len)
    split_points = list(np.cumsum(PROJ_SPLITS)[:-1])
    for l in range(DEPTH_2):
        lam_init = 0.8 - 0.6 * math.exp(-0.3 * l)

        h = rmsnorm(x, ln1[l])
        proj = h @ w_in[l]
        dq, dk, dv, sq, sk, sv = jnp.split(proj, split_points, axis=-1)

        dq = dq.reshape(b, s_len, DIFF_HEADS, 2, DIFF_QK_DIM)
        dk = dk.reshape(b, s_len, DIFF_HEADS, 2, DIFF_QK_DIM)
        q1 = partial_rotary(dq[..., 0, :], pos)
        q2 = partial_rotary(dq[..., 1, :], pos)
        k1 = partial_rotary(dk[..., 0, :], pos)
        k2 = partial_rotary(dk[..., 1, :], pos)
        dv = dv.reshape(b, s_len, DIFF_HEADS, DIFF_V_DIM)
        lam = (jnp.exp(jnp.sum(lambda_q1[l].astype(jnp.float32) * lambda_k1[l].astype(jnp.float32)))
               - jnp.exp(jnp.sum(lambda_q2[l].astype(jnp.float32) * lambda_k2[l].astype(jnp.float32)))
               + lam_init)
        diff_out = differential_attention(q1, q2, k1, k2, dv, lam)
        diff_out = rmsnorm(diff_out, diff_head_norm[l]) * (1.0 - lam_init)

        sq = sq.reshape(b, s_len, SB_HEADS, SB_HEAD_DIM)
        sk = sk.reshape(b, s_len, SB_HEADS, SB_HEAD_DIM)
        sv = sv.reshape(b, s_len, SB_HEADS, SB_HEAD_DIM)
        sb_out = rmsnorm(stick_breaking_attention(sq, sk, sv), sb_head_norm[l])

        mixed = jnp.concatenate([diff_out.reshape(b, s_len, DIFF_WIDTH),
                                 sb_out.reshape(b, s_len, SB_WIDTH)], axis=-1)
        x = x + mixed @ w_out[l]

        h = rmsnorm(x, ln2[l])
        x = x + jnp.square(jax.nn.relu(h @ w_mlp_in[l])) @ w_mlp_out[l]
    return rmsnorm(x, ln_f)


_first_inputs = second_inputs


def second_inputs(seed=0):
    import zlib

    import numpy as np

    out = dict(_first_inputs(seed))
    spreads = {}
    factors = {'ln1': 2.785,
     'lambda_q1': 4.798,
     'lambda_k1': 3.482,
     'lambda_q2': 8.0,
     'diff_head_norm': 6.236,
     'sb_head_norm': 5.155,
     'ln2': 8.0,
     'ln_f': 2.775}
    for name, (base, spread) in spreads.items():
        noise = np.random.default_rng([zlib.crc32(name.encode()), seed]).standard_normal(out[name].shape)
        drawn = base * np.exp(spread * noise) if base else spread * noise
        out[name] = jnp.asarray(drawn.astype(out[name].dtype))
    for name, factor in factors.items():
        out[name] = (out[name] * factor).astype(out[name].dtype)
    return out


_narrow_inputs = second_inputs


def second_inputs(seed=0):

    out = dict(_narrow_inputs(seed))
    wider = {'lambda_q2': 12.0, 'diff_head_norm': 3.85, 'sb_head_norm': 3.8, 'ln_f': 3.12}
    for name, times in wider.items():
        mean = out[name].mean()
        out[name] = (mean + times * (out[name] - mean)).astype(out[name].dtype)
    return out


def setup_inputs(seed=0):
    out = dict(first_inputs(seed))
    for name, value in second_inputs(seed + 1).items():
        if name != "x":
            out[name + "_2"] = value
    return out


def reference(
    x, a_w_in, a_lam_re, a_lam_im, a_log_dt, a_b_re, a_b_im, a_c_re, a_c_im, a_d, a_w_glu,
    a_b_glu, a_w_out, kv_w, cmp_pos_k, cmp_w1_k, cmp_w2_k, cmp_pos_v, cmp_w1_v, cmp_w2_v,
    b_w_in, b_w_out, ln_g, ln_b, ln1_2, w_in_2, lambda_q1_2, lambda_k1_2, lambda_q2_2,
    lambda_k2_2, diff_head_norm_2, sb_head_norm_2, w_out_2, ln2_2, w_mlp_in_2, w_mlp_out_2,
    ln_f_2,
):
    x = first_block(
        x, a_w_in, a_lam_re, a_lam_im, a_log_dt, a_b_re, a_b_im, a_c_re, a_c_im, a_d, a_w_glu,
        a_b_glu, a_w_out, kv_w, cmp_pos_k, cmp_w1_k, cmp_w2_k, cmp_pos_v, cmp_w1_v, cmp_w2_v,
        b_w_in, b_w_out, ln_g, ln_b,
    )
    return second_block(
        x, ln1_2, w_in_2, lambda_q1_2, lambda_k1_2, lambda_q2_2, lambda_k2_2, diff_head_norm_2,
        sb_head_norm_2, w_out_2, ln2_2, w_mlp_in_2, w_mlp_out_2, ln_f_2,
    )


_drawn_inputs = setup_inputs


def setup_inputs(seed=0):
    import zlib

    import numpy as np

    out = dict(_drawn_inputs(seed))
    spreads = {}
    factors = {'a_lam_re': 64.0,
     'a_b_re': 3.596,
     'a_b_im': 3.661,
     'a_c_re': 3.674,
     'a_c_im': 3.496,
     'a_b_glu': 38.178,
     'cmp_pos_k': 61.542,
     'cmp_pos_v': 8.0,
     'lambda_q1_2': 8.0,
     'lambda_k1_2': 8.0}
    for name, (base, spread) in spreads.items():
        noise = np.random.default_rng([zlib.crc32(name.encode()), seed]).standard_normal(out[name].shape)
        drawn = base * np.exp(spread * noise) if base else spread * noise
        out[name] = jnp.asarray(drawn.astype(out[name].dtype))
    for name, factor in factors.items():
        out[name] = (out[name] * factor).astype(out[name].dtype)
    return out
```

```python
import math

import numpy as np
import concourse.bass as bass
from concourse import mybir

F32 = mybir.dt.float32
F32R = mybir.dt.float32r
ALU = mybir.AluOpType
ACT = mybir.ActivationFunctionType
AX_X = mybir.AxisListType.X

P = 128
TOK = 256
NT = TOK // P
DM = 2048
KT = DM // P
COLS = 512
SLOTS = 8
SPLIT = 4
LEAD = 3

SSM_W = DM // 2
CB = SSM_W // P
NST = 32
CHUNK = 64
HEADS, KVH, HD = 16, 4, 128
NCMP, CSTRIDE, CBLOCK = 15, 16, 32
ZW = 2048
GATES = 48
DIFF_H, SB_H = 8, 8
DFF = 8192

ALPHA = 4.0 ** 0.25
MAGIC = 12582912.0
TWO_PI = 2.0 * math.pi
PI_A = 6.28125
PI_B = float(np.float32(TWO_PI - PI_A - (TWO_PI - PI_A) % (2.0 ** -20)))
PI_C = float(np.float32(TWO_PI - PI_A - PI_B))
NEG = -1e30
LN_EPS, NORM_EPS = 1e-5, 1e-6
LAM_INIT = 0.8 - 0.6 * math.exp(-0.3 * 0)
PARAM_DMAS = 11
GROUP_STEPS, QUARTER_STEPS = 55, 4

U_AIN, U_GLU, U_AOUT, U_KV, U_NSA = 0, 4, 5, 7, 14
U_BOUT, U_QKV, U_WOUT, U_MLP = 30, 34, 46, 50
G_AIN, G_GLU, G_AOUT, G_KV, G_NSA = 0, 4, 6, 10, 16
G_BOUT, G_QKV, G_WOUT, G_MLP = 32, 36, 48, 52
N_UNITS = 82


class Steps:

    def __init__(self, eng, sem):
        self.eng, self.sem, self.base, self.n = eng, sem, 0, 0

    def inc(self, ins):
        ins.then_inc(self.sem, 1)
        self.n += 1
        return self.base + self.n

    def wait(self, value=None):
        self.eng.wait_ge(self.sem, self.base + self.n if value is None else value)

    def link(self, ins):
        self.inc(ins)
        self.wait()


_CONST = {}
_at = 0
for _name, _width in [("ident", P), ("causal", P), ("rotate", P), ("strict", P), ("later", P), ("ones", P),
                      ("cos", TOK), ("sin", TOK), ("cmp_bias", NT * 16), ("cmp_valid", NT * 16),
                      ("steps", CHUNK), ("group_half", 2), ("state_half", 2)]:
    _CONST[_name] = (_at, _width)
    _at += _width
CONST_W = _at


def constants():
    c = np.zeros((P, CONST_W), np.float32)

    def put(name, value):
        at, width = _CONST[name]
        c[:, at:at + width] = value.reshape(P, width)

    row, col = np.arange(P)[:, None], np.arange(P)[None, :]
    put("ident", (row == col).astype(np.float32))
    put("causal", np.where(col <= row, 0.0, NEG).astype(np.float32))
    put("strict", (row < col).astype(np.float32))
    put("later", (row > col).astype(np.float32))
    put("ones", np.ones((P, P), np.float32))
    rot = np.zeros((P, P), np.float32)
    inv_freq = (np.float32(500000.0) ** (-np.arange(0, 16, 2, dtype=np.float32) / np.float32(16))).astype(np.float32)
    cos, sin = np.ones((P, TOK), np.float32), np.zeros((P, TOK), np.float32)
    pos = np.arange(TOK, dtype=np.float32)
    for d in range(P):
        if d % 64 < 8:
            rot[d + 8, d] = -1.0
        elif d % 64 < 16:
            rot[d - 8, d] = 1.0
        if d % 64 < 16:
            angle = pos * inv_freq[d % 8]
            cos[d], sin[d] = np.cos(angle), np.sin(angle)
    put("rotate", rot)
    put("cos", cos)
    put("sin", sin)
    t = np.arange(NT)[None, :, None] * P + np.arange(P)[:, None, None]
    n = np.arange(16)[None, None, :]
    valid = (n * CSTRIDE + CBLOCK - 1 <= t) & (n < NCMP)
    put("cmp_valid", valid.astype(np.float32))
    put("cmp_bias", np.where(valid, 0.0, NEG).astype(np.float32))
    put("steps", np.broadcast_to(np.arange(CHUNK, dtype=np.float32), (P, CHUNK)))
    half = (np.arange(P) // 16) % 2
    put("group_half", np.stack([half == 0, half == 1], 1).astype(np.float32))
    half = np.arange(P) // 64
    put("state_half", np.stack([half == 0, half == 1], 1).astype(np.float32))
    return c


def build(nc, ins, out):
    from contextlib import ExitStack

    ctx = ExitStack()
    base = 16640
    top = [base]

    def at(name, shape, dt, offset):
        return nc.alloc_sbuf_tensor_at(name, shape, dt, offset=offset)

    def sem(name):
        return ctx.enter_context(nc.semaphore(name))

    K1 = 1024
    RAW = at("raw", [P, SLOTS, 2, COLS], F32, base)
    WH = at("w_high", [P, SPLIT, 2, COLS], F32R, base + 32 * K1)
    WL = at("w_low", [P, SPLIT, 2, COLS], F32R, base + 48 * K1)
    XH = at("x_high", [P, KT, TOK], F32R, base + 64 * K1)
    XL = at("x_low", [P, KT, TOK], F32R, base + 80 * K1)
    X = at("x_rows", [P, NT, DM], F32, base + 96 * K1)
    HH = at("h_high", [P, KT, TOK], F32R, base + 112 * K1)
    HL = at("h_low", [P, KT, TOK], F32R, base + 128 * K1)

    def region(start, limit):
        place = [start]

        def take(name, shape, dt=F32):
            size = int(np.prod(shape[1:])) * 4
            t = at(name, shape, dt, base + place[0])
            place[0] += (size + 31) // 32 * 32
            assert place[0] <= limit, (name, place[0], limit)
            return t
        return take

    END = 207 * K1 + 500
    small = region(144 * K1, 157 * K1)
    CST = small("constants", [P, CONST_W])
    PR = small("param_rows", [P, 2, P])
    PT = small("param_cols", [P, 2, P])
    LDT = small("log_dt_rows", [P, 2])
    TMP = small("transposed_tmp", [P, 2, 2, TOK])

    def const(name):
        a, w = _CONST[name]
        return CST[:, a:a + w]

    ID = const("ident")
    CAUSAL_R = small("causal_rounded", [P, P], F32R)
    ID_R = small("ident_rounded", [P, P], F32R)
    STATS = small("ln_stats", [P, NT, 4, 6])
    MV = small("mean_var", [P, NT, 2])
    RSTD = small("rstd", [P, 8])
    MHALF = small("minus_half", [P, 8])
    TINY = small("tiny", [P, 2])
    MS = small("mean_squares", [P, 8])
    HNC = small("head_gains", [P, 2])

    ssm = region(157 * K1, END)
    UT = ssm("u_cols", [P, CB, TOK])
    ZT = ssm("z_gated", [P, CB, TOK])
    YT = ssm("y_cols", [P, CB, TOK])
    COS = ssm("cos_table", [P, NST, CHUNK])
    SIN = ssm("sin_table", [P, NST, CHUNK])
    DECAY = ssm("decay_table", [P, NST, CHUNK])
    SP = ssm("ssm_params", [P, 16, NST])
    CARRY = ssm("carry", [P, 4, 2, 8])
    CTMP = ssm("carry_tmp", [P, 4, 8])
    BT = at("b_rows", [P, CB, 2, P], F32, base + 96 * K1)
    CT = at("c_rows", [P, CB, 2, P], F32, base + 104 * K1)
    prep = region(112 * K1, 144 * K1)
    BN = prep("b_natural", [P, 2, NST, 16])
    CN = prep("c_natural", [P, 2, CB, 64])
    BB = prep("b_bar", [P, 2, NST, 16])
    BTMP = prep("b_tmp", [P, 2, NST, 16])
    BBLK = prep("b_block", [P, 2, NST, 2, 16])
    CBLK = prep("c_block", [P, 2, CB, 2, 64])
    tab = region(112 * K1, 144 * K1)
    TA = tab("tab_whole", [P, NST, CHUNK])
    TB = tab("tab_high", [P, NST, CHUNK])
    TC = tab("tab_low", [P, NST, CHUNK])
    TD = tab("tab_sum", [P, NST, CHUNK])
    core = region(112 * K1, 144 * K1)
    BU = core("bu", [P, 2, 2, 8, CHUNK])
    QP = core("q_products", [P, 2, 2, 8, CHUNK])
    PP = core("p_products", [P, 2, 8, CHUNK])
    G = core("rotated_states", [P, 2, 8, CHUNK])
    HP = core("h_products", [P, 2, 8, CHUNK])
    XP = core("x_products", [P, 2, 8, CHUNK])

    kv = region(157 * K1, END)
    KS = kv("k_slc_cols", [P, KVH, TOK])
    KW = kv("k_win_cols", [P, KVH, TOK])
    VS = kv("v_slc_rows", [P, NT, COLS])
    VW = kv("v_win_rows", [P, NT, COLS])
    KC = kv("k_cmp_cols", [P, 16, KVH])
    VC = kv("v_cmp_rows", [P, KVH, HD])
    kv_end = (157 + 16) * K1 + 256 + 2048
    comp = region(kv_end, END)
    KVC = [comp("kv_cmp_high", [P, 2, KVH, TOK], F32R), comp("kv_cmp_low", [P, 2, KVH, TOK], F32R)]
    GB = comp("gain_bias_half", [P, 2, DM // 2])
    PSR = [comp("pos_high", [P, 2, 32, 2], F32R), comp("pos_low", [P, 2, 32, 2], F32R)]
    HC = comp("cmp_hidden", [P, 2, 16, KVH])
    W2 = comp("cmp_w2", [P, 2, HD])
    PB = comp("cmp_pos_bias", [P, 2])
    nsa = region(kv_end, END)
    OB = nsa("branch_out", [P, 3, NT, COLS])
    ZB = nsa("z_tmp", [P, NT, COLS])
    QT = nsa("q_cols", [P, 4, TOK])
    PB_ = nsa("probs", [P, 2, 384])
    PTB = nsa("probs_cols", [P, 2, 384])
    CP = nsa("cmp_probs", [P, 2, 4, 16])
    GATE = nsa("gates", [P, NT, GATES])
    NM = nsa("neg_max", [P, 2, 8])
    RS = nsa("row_sum", [P, 2, 8])
    OS = nsa("out_scale", [P, 2, 8])
    YB = OB[:, 0, :, :]
    PTC = nsa("cmp_probs_cols", [P, 2, COLS])
    GW = at("gate_w", [P, KT, GATES], F32, base + kv_end)
    GWS = [at("gate_w_high", [P, KT, GATES], F32R, base + kv_end + 3 * K1),
           at("gate_w_low", [P, KT, GATES], F32R, base + kv_end + 6 * K1)]

    blk2 = region(157 * K1, END)
    GB2 = blk2("gain_bias", [P, 2, DM])
    HN = blk2("normed_rows", [P, NT, DM])
    att = region(157 * K1, END)
    DQ = att("diff_q_cols", [P, 4, TOK])
    DK = att("diff_k_cols", [P, 4, TOK])
    DV = att("diff_v_rows", [P, NT, COLS])
    SQ = att("sb_q_cols", [P, 4, TOK])
    SK = att("sb_k_cols", [P, 4, TOK])
    SV = att("sb_v_rows", [P, NT, COLS])
    P1 = att("probs_first", [P, 2, 384])
    P2 = att("probs_second", [P, 2, 384])
    PT2 = att("mixed_cols", [P, 2, 384])
    SA = att("stick_a", [P, 2, 384])
    SB = att("stick_b", [P, 2, 384])
    SC = att("stick_c", [P, 2, 384])
    RT = att("rotary_tmp", [P, 2, TOK])
    ON = att("head_rows", [P, 2, NT, HD])
    JUNK = att("squares", [P, NT, HD])
    SM = att("head_small", [P, 2, 24])
    LAM4 = at("lambda_rows", [P, 4, 64], F32, base + 206 * K1)
    LSM = at("lambda_small", [P, 8], F32, base + 207 * K1)
    mlp = region(157 * K1, END)
    REL = mlp("relu_tmp", [P, 2, COLS])
    HID = mlp("hidden_tmp", [P, 2, COLS])
    GF = mlp("last_gain", [P, DM])

    ACC = [ctx.enter_context(nc.psum_tensor(f"acc{i}", [P, NT, COLS], F32)) for i in range(2)]
    BK = [ctx.enter_context(nc.psum_tensor(f"bank{i}", [P, COLS], F32)) for i in range(4)]

    raw_in = [sem(f"raw_in{i}") for i in range(SLOTS)]
    hi_ready = sem("hi_ready")
    lo_ready = sem("lo_ready")
    slot_used = sem("slot_used")
    acc_free = sem("acc_free")
    act_part = sem("act_part")
    h_ready = sem("h_ready")
    tr_full = sem("tr_full")
    tr_tmp = sem("tr_tmp")
    split_done = sem("split_done")
    x_loaded = sem("x_loaded")
    const_in, params_in = sem("const_in"), sem("params_in")
    bc_in, kvp_in, gain_in = sem("bc_in"), sem("kvp_in"), sem("gain_in")
    dve_steps, act_steps, pool_steps = sem("dve_steps"), sem("act_steps"), sem("pool_steps")
    params_full, params_done = sem("params_full"), sem("params_done")
    rows_ready = sem("rows_ready")
    out_ready = sem("out_ready")
    stored = sem("stored")

    rows_set = sem("rows_set")
    blk_ready = sem("blk_ready")
    bc_full, bc_done = sem("bc_full"), sem("bc_done")
    bu_full, bu_evac = sem("bu_full"), sem("bu_evac")
    bu_half = sem("bu_half")
    in_used = sem("in_used")
    q_ready, w_ready = sem("q_ready"), sem("w_ready")
    g_ready, xp_ready = sem("g_ready"), sem("xp_ready")
    hs_ready, y_full, y_read = sem("hs_ready"), sem("y_full"), sem("y_read")
    tab_pool, tab_dve, tab_act = sem("tab_pool"), sem("tab_dve"), sem("tab_act")
    comp_full, comp_act, comp_dve = sem("comp_full"), sem("comp_act"), sem("comp_dve")
    gate_split, gate_full, gate_tanh, gate_ready = sem("gate_split"), sem("gate_full"), sem("gate_tanh"), sem("gate_ready")
    gw_in = sem("gw_in")
    s_full, nm_ready, p_ready = sem("s_full"), sem("nm_ready"), sem("p_ready")
    t_full, pt_ready, o_full, o_read = sem("t_full"), sem("pt_ready"), sem("o_full"), sem("o_read")
    z_tanh, z_used = sem("z_tanh"), sem("z_used")
    rot_raw, rot_full = sem("rot_raw"), sem("rot_full")
    a_full, b_full, c_full = sem("a_full"), sem("b_full"), sem("c_full")
    a_dve, a_act, w_dve = sem("a_dve"), sem("a_act"), sem("w_dve")
    b_act, ss_act, ms_dve, r_pool, on_dve = sem("b_act"), sem("ss_act"), sem("ms_dve"), sem("r_pool"), sem("on_dve")
    sb_full = sem("sb_full")
    f_dve, f_pool = sem("f_dve"), sem("f_pool")
    sb_abs, sb_act = sem("sb_abs"), sem("sb_act")
    x_rows = sem("x_rows")
    row_squares = sem("row_squares")
    ms_rows, rstd_rows = sem("ms_rows"), sem("rstd_rows")
    lam_in, hn_in = sem("lam_in"), sem("hn_in")
    lam_dve, lam_act = sem("lam_dve"), sem("lam_act")
    hid_act, hid_dve, hid_high, hid_relu = sem("hid_act"), sem("hid_dve"), sem("hid_high"), sem("hid_relu")
    natural_done = sem("natural_done")

    def rows_cols(w, row0, col0):
        return w[bass.ds(row0, 2 * P), bass.ds(col0, COLS)].rearrange("(k p) n -> p k n", p=P)

    A_IN, A_GLU, A_OUT, KV_W = ins["a_w_in"][0], ins["a_w_glu"][0], ins["a_w_out"][0], ins["kv_w"]
    B_IN, B_OUT = ins["b_w_in"][0], ins["b_w_out"][0]
    QKV_W, OUT_W, M_IN, M_OUT = ins["w_in_2"][0], ins["w_out_2"][0], ins["w_mlp_in_2"][0], ins["w_mlp_out_2"][0]
    KV_COL = [0, 1, 2, None, 3, 4, 5]

    block = ctx.enter_context(nc.Block())

    @block.sync
    def _(sp):
        def slot(unit, s, src, view=None):
            if not isinstance(unit, int) or unit > 0:
                sp.wait_ge(lo_ready, unit * SLOTS - SLOTS + s + 1)
            dst = RAW[:, s, :, :] if view is None else view
            sp.dma_start(dst, src).then_inc(raw_in[s], 16)

        def unit_wide(unit, w, col0, row0=0):
            for s in range(SLOTS):
                slot(unit, s, rows_cols(w, row0 + 2 * P * s, col0))

        def unit_half(unit, w, col0):
            for s in range(SLOTS):
                slot(unit, s, rows_cols(w, 2 * P * (s % 4), col0 + COLS * (s // 4)))

        x_in = ins["x"][0].rearrange("(t p) d -> p t d", p=P)
        sp.dma_start(CST[:, :], ins["consts"]).then_inc(const_in, 16)
        for t in range(NT):
            sp.dma_start(X[:, t, :], x_in[:, t, :]).then_inc(x_loaded, 16)
        for u in range(4):
            unit_wide(U_AIN + u, A_IN, COLS * u)
        unit_half(U_GLU, A_GLU, 0)
        sp.wait_ge(y_full, 16)
        sp.wait_ge(x_loaded, 16 * NT)
        sp.dma_start(X[:, :, :], x_in).then_inc(x_loaded, 16)
        for u in range(2):
            unit_half(U_AOUT + u, A_OUT, 2 * COLS * u)
        for u, c in enumerate(KV_COL):
            if c is not None:
                unit_wide(U_KV + u, KV_W, COLS * c)
                continue
            for s in range(SLOTS):
                w1 = ins["cmp_w1_k" if s < 4 else "cmp_w1_v"]
                src = w1[bass.ds(1024 * (s % 4), 1024), :].rearrange("(i d) e -> d i e", d=HD)
                slot(U_KV + u, s, src, RAW[:, s, :, :].rearrange("p k (i e) -> p (k i) e", e=HD))
        unit_wide(U_NSA, B_IN, 0)
        with sp.Fori(0, 3) as g:
            for j in range(3):
                unit_wide(g * 4 + (U_NSA + 1 + j), B_IN, g * COLS + ZW * (1 + j))
            unit_wide(g * 4 + (U_NSA + 4), B_IN, g * COLS + COLS)
        for j in range(3):
            unit_wide(U_NSA + 13 + j, B_IN, 3 * COLS + ZW * (1 + j))
        for u in range(4):
            unit_wide(U_BOUT + u, B_OUT, COLS * u)
        for n in range(12):
            half, kind = divmod(n, 6)
            unit_wide(U_QKV + n, QKV_W, 1024 * kind + COLS * half)
        for u in range(4):
            unit_wide(U_WOUT + u, OUT_W, COLS * u)
        with sp.Fori(0, 4) as q:
            for j in range(4):
                unit_wide(q * 8 + (U_MLP + j), M_IN, q * 2048 + COLS * j)
            for j in range(4):
                unit_wide(q * 8 + (U_MLP + 4 + j), M_OUT, COLS * j, q * 2048)
        for t in range(NT):
            sp.wait_ge(out_ready, t + 1)
            sp.dma_start(out[0].rearrange("(t p) d -> p t d", p=P)[:, t, :], X[:, t, :]).then_inc(stored, 16)
        sp.wait_ge(stored, 16 * NT)

    S_ITS = [(c, q) for c in range(TOK // CHUNK) for q in range(4)]
    TR_X, TR_X1, TR_Y, TR_H, TR_MIX, TR_H2 = 0, 8, 16, 24, 32, 48

    @block.tensor
    def _(pe):
        def tick(tau, s, mode, pair, kt, start, stop, xh, xl):
            k = s % SPLIT
            pe.wait_ge(lo_ready, tau + 1)
            for j in range(2):
                first, last = start and j == 0, stop and j == 1
                for n, (xa, wa) in enumerate(((xh, WH), (xh, WL), (xl, WH))):
                    if mode == "rows":
                        for t in range(NT):
                            ins_ = nc.tensor.matmul(ACC[pair][:, t, :], xa[:, kt + j, t * P:(t + 1) * P], wa[:, k, j, :],
                                                    start=first and n == 0, stop=last and n == 2)
                    else:
                        for m in range(4):
                            ins_ = nc.tensor.matmul(ACC[pair][:, m // 2, (m % 2) * TOK:(m % 2 + 1) * TOK],
                                                    wa[:, k, j, m * P:(m + 1) * P], xa[:, kt + j, :],
                                                    start=first and n == 0 and m % 2 == 0, stop=last and n == 2,
                                                    skip_group_check=True)
            ins_.then_inc(slot_used, 1)

        def gemm(unit, group, mode, xh=XH, xl=XL, ready=None, extras=None, s0=0, s1=SLOTS, kt0=0, parity=None):
            g2 = group if parity is None else parity
            if not isinstance(group, int) or group >= 2:
                pe.wait_ge(acc_free, group - 1)
            for s in range(s0, s1):
                if ready is not None:
                    ready(s)
                tick(unit * SLOTS + s, s, mode, g2 % 2, kt0 + 2 * (s - s0), s == s0, s == s1 - 1, xh, xl)
                if extras is not None:
                    extras(s)

        def split_ready(first):
            return lambda s: pe.wait_ge(split_done, first + s + 1)

        def transposes(first, rows, ready=None):
            for i in range(8):
                n = first + i
                if ready is not None:
                    ready(i)
                if i >= 4:
                    pe.wait_ge(tr_tmp, n - 3)
                for j in range(2):
                    for t in range(NT):
                        kt = 2 * i + j
                        ins_ = nc.tensor.transpose(BK[i % 4][:, (j * NT + t) * P:(j * NT + t + 1) * P],
                                                   rows[:, t, kt * P:(kt + 1) * P], ID)
                ins_.then_inc(tr_full, 1)

        pe.wait_ge(const_in, 16)
        pe.wait_ge(rows_set, 1)
        for i in range(2):
            ins_ = nc.tensor.transpose(BK[i][:, 0:P], PR[:, i, :], ID)
        ins_.then_inc(params_full, 1)
        pe.wait_ge(params_done, 1)
        pe.wait_ge(x_loaded, 16 * NT)
        transposes(TR_X, X)
        gemm(U_AIN, G_AIN, "cols", ready=split_ready(TR_X))
        pe.wait_ge(blk_ready, 1)
        for n in range(8):
            if n < 4:
                pe.wait_ge(tr_tmp, 8)
            else:
                pe.wait_ge(bc_done, n - 3)
            src = BBLK if n < 4 else CBLK
            for j in range(4):
                cb, ri = 2 * (n % 4) + j // 2, j % 2
                if n < 4:
                    m_in = BBLK[:, ri, 4 * cb:4 * cb + 4, :, :].rearrange("p s w c -> p (s w c)")
                else:
                    m_in = CBLK[:, ri, cb, :, :].rearrange("p w n -> p (w n)")
                ins_ = nc.tensor.transpose(BK[n % 4][:, j * P:(j + 1) * P], m_in, ID)
            ins_.then_inc(bc_full, 1)
        gemm(U_AIN + 1, G_AIN + 1, "cols")

        def bu(it):
            c, q = S_ITS[it]
            pe.wait_ge(bc_done, 8)
            pe.wait_ge(acc_free, 2)
            if it:
                pe.wait_ge(bu_evac, 2 * it - 1)
            for s4 in range(4):
                n = 2 * it + s4 % 2
                if s4 >= 2:
                    pe.wait_ge(bu_half, n + 1)
                for ri in range(2):
                    for cbl in range(2):
                        at_ = ((ri * 2 + cbl) * 2 + s4 // 2) * CHUNK
                        cb = 2 * q + cbl
                        ins_ = nc.tensor.matmul(BK[n % 3][:, at_:at_ + CHUNK], BT[32 * s4:32 * s4 + 32, cb, ri, :],
                                                UT[32 * s4:32 * s4 + 32, cb, c * CHUNK:(c + 1) * CHUNK],
                                                start=True, stop=True)
                ins_.then_inc(bu_half if s4 < 2 else bu_full, 1)

        def y(it):
            c, q = S_ITS[it]
            pe.wait_ge(hs_ready, it + 1)
            if it:
                pe.wait_ge(y_read, it)
            for cbl in range(2):
                for s4 in range(4):
                    for ri in range(2):
                        ins_ = nc.tensor.matmul(BK[3][32 * s4:32 * s4 + 32, (q * 2 + cbl) * CHUNK:(q * 2 + cbl + 1) * CHUNK],
                                                CT[:, 2 * q + cbl, ri, 32 * s4:32 * s4 + 32], HP[:, ri, 4 * cbl + s4, :],
                                                start=ri == 0, stop=ri == 1)
            ins_.then_inc(y_full, 1)

        bu(0)
        for zu in range(2):
            def mix(s, zu=zu):
                it = 8 * zu + s
                if it + 1 < len(S_ITS):
                    bu(it + 1)
                if it >= 1:
                    y(it - 1)
            gemm(U_AIN + 2 + zu, G_AIN + 2 + zu, "cols", extras=mix)
        y(len(S_ITS) - 1)

        for c in range(2):
            gemm(U_GLU, G_GLU + c, "cols", HH, HL, s0=4 * c, s1=4 * c + 4,
                 ready=lambda s, c=c: pe.wait_ge(h_ready, s + 1) if c == 0 else None)
        for c in range(4):
            gemm(U_AOUT + c // 2, G_AOUT + c, "rows", HH, HL, s0=4 * (c % 2), s1=4 * (c % 2) + 4, kt0=CB,
                 ready=lambda s, c=c: pe.wait_ge(h_ready, 4 + s + 1) if c == 0 else None)
        transposes(TR_X1, X, lambda i: pe.wait_ge(rows_ready, 1) if i == 0 else None)

        gemm(U_KV, G_KV, "cols", ready=split_ready(TR_X1))
        gemm(U_KV + 1, G_KV + 1, "cols")
        gemm(U_KV + 2, G_KV + 2, "cols")
        pe.wait_ge(comp_dve, 2)
        for kv_ in range(2):
            for s4 in range(4):
                s = 4 * kv_ + s4
                pe.wait_ge(lo_ready, (U_KV + 3) * SLOTS + s + 1)
                for i8 in range(8):
                    i = 8 * s4 + i8
                    first, last = i == 0, i == 31
                    for n, (xi, wa) in enumerate(((0, WH), (0, WL), (1, WH))):
                        w = wa[:, s % SPLIT, :, :].rearrange("p k (i e) -> p (k i) e", e=HD)[:, i8, :]
                        r = KVC[xi][:, kv_, :, i:i + CSTRIDE * (NCMP - 1) + 1:CSTRIDE].rearrange("p h n -> p n h")
                        nc.tensor.matmul(BK[kv_][:, 0:NCMP * KVH].rearrange("p (n h) -> p n h", h=KVH), w, r,
                                         start=first and n == 0, stop=last and n == 2)
                        ins_ = nc.tensor.matmul(BK[2 + kv_][:, 0:2], w, PSR[xi][:, kv_, i, :],
                                                start=first and n == 0, stop=last and n == 2)
                ins_.then_inc(slot_used, 1)
        gemm(U_KV + 4, G_KV + 3, "rows")
        pe.wait_ge(kvp_in, 32)
        pe.wait_ge(comp_act, 2)
        nc.tensor.matmul(BK[0][:, 0:NCMP * KVH], W2[:, 0, :], HC[:, 0, 0:NCMP, :].rearrange("p n h -> p (n h)"),
                         start=True, stop=True)
        for h in range(KVH):
            ins_ = nc.tensor.matmul(BK[1][0:NCMP, h * HD:(h + 1) * HD], HC[:, 1, 0:NCMP, h], W2[:, 1, :],
                                    start=True, stop=True)
        ins_.then_inc(comp_full, 1)
        gemm(U_KV + 5, G_KV + 4, "cols")
        gemm(U_KV + 6, G_KV + 5, "rows")

        gemm(U_NSA, G_NSA, "cols")
        pe.wait_ge(gate_split, 1)
        pe.wait_ge(comp_dve, 4)
        for t in range(NT):
            for kt in range(KT):
                for n, (xa, wi) in enumerate(((XH, 0), (XH, 1), (XL, 0))):
                    ins_ = nc.tensor.matmul(BK[0][:, t * GATES:(t + 1) * GATES], xa[:, kt, t * P:(t + 1) * P],
                                            GWS[wi][:, kt, :], start=kt == 0 and n == 0, stop=kt == KT - 1 and n == 2)
        ins_.then_inc(gate_full, 1)
        pe.wait_ge(gate_tanh, 1)

        def group(g, more):
            def scores(n):
                if n == 0:
                    pe.wait_ge(acc_free, g * 4 + (G_NSA + 1))
                if n >= 2:
                    pe.wait_ge(p_ready, g * 10 + (n - 1))
                bank = BK[n % 2]
                if n < 2:
                    for h in range(4):
                        ins_ = nc.tensor.matmul(bank[:, h * 16:(h + 1) * 16], QT[:, h, n * P:(n + 1) * P],
                                                KC[:, :, bass.ds(g, 1)].rearrange("p n o -> p (n o)"), start=True, stop=True)
                else:
                    h, keys = (n - 2) % 4, KS if n < 6 else KW
                    for t in range(NT):
                        lo, w = (0, P) if t == 0 else (P, TOK)
                        nc.tensor.matmul(bank[:, lo:lo + w], QT[:, h, t * P:(t + 1) * P],
                                         keys[:, bass.ds(g, 1), 0:w].rearrange("p o k -> p (o k)"), start=True, stop=False)
                        d = lo + w - P
                        ins_ = nc.tensor.matmul(bank[:, d:d + P], ID_R[:, :], CAUSAL_R[:, :], start=False, stop=True)
                ins_.then_inc(s_full, 1)

            def turn(n):
                pe.wait_ge(p_ready, g * 10 + (n + 1))
                if n:
                    pe.wait_ge(pt_ready, g * 10 + n)
                if n < 2:
                    for h in range(4):
                        ins_ = nc.tensor.transpose(BK[2][0:16, h * P:(h + 1) * P], CP[:, n, h, :], ID)
                else:
                    for b in range(3):
                        ins_ = nc.tensor.transpose(BK[2][:, b * P:(b + 1) * P], PB_[:, n % 2, b * P:(b + 1) * P], ID)
                ins_.then_inc(t_full, 1)

            def values(n):
                pe.wait_ge(pt_ready, g * 10 + (n + 1))
                if n:
                    pe.wait_ge(o_read, g * 10 + n)
                if n < 2:
                    for h in range(4):
                        ins_ = nc.tensor.matmul(BK[3][:, h * P:(h + 1) * P], PTC[:, n % 2, h * P:(h + 1) * P],
                                                VC[:, bass.ds(g, 1), :].rearrange("p o d -> p (o d)"), start=True, stop=True)
                else:
                    v = VS if n < 6 else VW
                    for b, (t, k) in enumerate(((0, 0), (1, 0), (1, 1))):
                        ins_ = nc.tensor.matmul(BK[3][:, t * P:(t + 1) * P], PTB[:, n % 2, b * P:(b + 1) * P],
                                                v[:, k, bass.ds(g * HD, HD)], start=b < 2, stop=b != 1)
                ins_.then_inc(o_full, 1)

            for j in range(3):
                def attend(s, j=j):
                    i = 8 * j + s
                    if 2 <= i < 12:
                        values(i - 2)
                    if 1 <= i < 11:
                        turn(i - 1)
                    if i < 10:
                        scores(i)
                gemm(g * 4 + (U_NSA + 1 + j), g * 4 + (G_NSA + 1 + j), "rows", extras=attend, parity=1 + j)
            if more:
                gemm(g * 4 + (U_NSA + 4), g * 4 + (G_NSA + 4), "cols", parity=0)
            pe.wait_ge(rows_ready, g + 2)
            for i in range(2):
                for j in range(2):
                    for t in range(NT):
                        h = 2 * i + j
                        ins_ = nc.tensor.transpose(BK[i][:, (j * NT + t) * P:(j * NT + t + 1) * P],
                                                   YB[:, t, h * P:(h + 1) * P], ID)
                ins_.then_inc(tr_full, 1)
            pe.wait_ge(tr_tmp, g * 2 + (TR_Y + 2))

        with pe.Fori(0, 3) as g:
            group(g, True)
        group(3, False)

        for u in range(4):
            gemm(U_BOUT + u, G_BOUT + u, "rows", HH, HL,
                 ready=(lambda s: pe.wait_ge(split_done, TR_Y + s + 1)) if u == 0 else None)
        transposes(TR_H, HN, lambda i: pe.wait_ge(rows_ready, 6) if i == 0 else None)

        def rotate(n):
            pair = [G_QKV, G_QKV + 1, G_QKV + 6, G_QKV + 7][n] % 2
            dst = (DQ, DK)[n % 2]
            for b in range(2):
                pe.wait_ge(rot_raw, 2 * n + b + 1)
                ins_ = nc.tensor.matmul(ACC[pair][:, b, :], const("rotate"),
                                        dst[:, 2 * b:2 * b + 2, :].rearrange("p m t -> p (m t)"), start=True, stop=True)
                ins_.then_inc(rot_full, 1)

        def diff_scores(n):
            h = n % 4
            if h == 0:
                pe.wait_ge(acc_free, G_QKV + 6 * (n // 4) + 3)
            if n:
                pe.wait_ge(a_act, 2 * n)
            if n == 4:
                pe.wait_ge(f_dve, 8)
            for m in range(2):
                for t in range(NT):
                    lo, w = (0, P) if t == 0 else (P, TOK)
                    nc.tensor.matmul(BK[m][:, lo:lo + w], DQ[64 * m:64 * m + 64, h, t * P:(t + 1) * P],
                                     DK[64 * m:64 * m + 64, h, 0:w], start=True, stop=False)
                    d = lo + w - P
                    ins_ = nc.tensor.matmul(BK[m][:, d:d + P], ID_R[:, :], CAUSAL_R[:, :], start=False, stop=True)
                ins_.then_inc(a_full, 1)

        def diff_turn(n):
            pe.wait_ge(w_dve, n + 1)
            pe.wait_ge(tr_tmp, TR_MIX + 8 * (n // 4) + n % 4)
            for b in range(3):
                ins_ = nc.tensor.transpose(BK[2][:, b * P:(b + 1) * P], P1[:, n % 2, b * P:(b + 1) * P], ID)
            ins_.then_inc(b_full, 1)

        def weigh(order, cols, ready, v, h):
            pe.wait_ge(*ready)
            if order:
                pe.wait_ge(on_dve, order)
            for b, (t, k) in enumerate(((0, 0), (1, 0), (1, 1))):
                ins_ = nc.tensor.matmul(BK[3][:, t * P:(t + 1) * P], cols[:, b * P:(b + 1) * P],
                                        v[:, k, h * HD:(h + 1) * HD], start=b < 2, stop=b != 1)
            ins_.then_inc(c_full, 1)

        def head_turn(order, turned):
            pe.wait_ge(on_dve, order + 1)
            pe.wait_ge(b_act, turned)
            if order:
                pe.wait_ge(tr_tmp, TR_MIX + order)
            for t in range(NT):
                ins_ = nc.tensor.transpose(BK[2][:, t * P:(t + 1) * P], ON[:, order % 2, t, :], ID)
            ins_.then_inc(tr_full, 1)

        def sb_scores(n):
            h = n % 4
            if h == 0:
                pe.wait_ge(acc_free, G_QKV + 6 * (n // 4) + 6)
                pe.wait_ge(a_act, 8 * (n // 4) + 8)
            else:
                pe.wait_ge(f_dve, 2 * n)
            nc.tensor.matmul(BK[0][:, 0:TOK], SK[:, h, 0:P], SQ[:, h, :], start=True, stop=True)
            nc.tensor.matmul(BK[0][:, TOK:TOK + P], SK[:, h, P:TOK], SQ[:, h, P:TOK], start=True, stop=True).then_inc(sb_full, 1)

        def sb_sums(n):
            pe.wait_ge(f_dve, 2 * n + 1)
            if n % 4 == 0:
                pe.wait_ge(a_act, 8 * (n // 4) + 8)
            c = SC[:, n % 2, :]
            nc.tensor.matmul(BK[1][:, 0:384], const("later"), c, start=True, stop=False, skip_group_check=True)
            nc.tensor.matmul(BK[1][:, P:TOK], const("ones"), c[:, TOK:384], start=False, stop=True,
                             skip_group_check=True).then_inc(sb_full, 1)

        def second_stage(kind, j, i):
            for h in range(4):
                n = 4 * j + h
                order = 8 * j + (0 if kind == "diff" else 4) + h
                if kind == "diff":
                    if i == 4 * h:
                        diff_scores(n)
                    if i == 4 * h + 1:
                        diff_turn(n)
                    if i == 4 * h + 2:
                        weigh(order, PT2[:, n % 2, :], (b_act, n + 1), DV, h)
                    if i == 4 * h + 5:
                        head_turn(order, n + 1)
                else:
                    if i == 4 * h:
                        sb_scores(n)
                    if i == 4 * h + 2:
                        sb_sums(n)
                    if i == 4 * h + 4:
                        weigh(order, SA[:, n % 2, :], (f_pool, n + 1), SV, h)
                    if i == 4 * h + 7:
                        head_turn(order, 4 * j + 4)

        for n in range(12):
            j, kind = divmod(n, 6)

            def beside(s, n=n, j=j, kind=kind):
                if s == 1 and kind in (1, 2):
                    rotate(2 * j + kind - 1)
                if kind >= 3:
                    second_stage("diff", j, 8 * (kind - 3) + s)
                elif j:
                    second_stage("sb", j - 1, 8 * kind + s)
            gemm(U_QKV + n, G_QKV + n, "rows" if kind in (2, 5) else "cols",
                 ready=split_ready(TR_H) if n == 0 else None, extras=beside)
        for i in range(24):
            second_stage("sb", 1, i)
        need = [2, 4, 10, 12, 12, 12, 14, 16]
        for u in range(4):
            gemm(U_WOUT + u, G_WOUT + u, "rows", HH, HL,
                 ready=(lambda s: pe.wait_ge(split_done, TR_MIX + need[s])) if u == 0 else None)
        transposes(TR_H2, HN, lambda i: pe.wait_ge(rows_ready, 7) if i == 0 else None)

        def quarter(q, first):
            for j in range(4):
                gemm(q * 8 + (U_MLP + j), q * 8 + (G_MLP + j), "cols", parity=j,
                     ready=split_ready(TR_H2) if first and j == 0 else None)
            for j in range(4):
                gemm(q * 8 + (U_MLP + 4 + j), q * 8 + (G_MLP + 4 + j), "rows", HH, HL, parity=j,
                     ready=(lambda s: pe.wait_ge(h_ready, q * 8 + (8 + s + 1))) if j == 0 else None)

        quarter(0, True)
        with pe.Fori(1, 4) as q:
            quarter(q, False)

    SINK = 6.283185

    @block.scalar
    def _(act):
        steps = Steps(act, act_steps)
        seen = [0]

        def high(base_, n=1):
            for _ in range(n):
                p = seen[0]
                seen[0] += 1
                s = p % SLOTS
                act.wait_ge(raw_in[s], base_ * 2 + 16 * (p // SLOTS + 1))
                if not isinstance(base_, int) or base_ + p >= SPLIT:
                    act.wait_ge(slot_used, base_ + (p - SPLIT + 1))
                nc.scalar.activation(WH[:, s % SPLIT, :, :], RAW[:, s, :, :], ACT.Copy).then_inc(hi_ready, 1)

        def unit(base_=0, first=None, extras=None, ticks=SLOTS):
            for s in range(ticks):
                high(base_)
                if s == 0 and first is not None:
                    first()
                if extras is not None:
                    extras(s)

        def done(ticks, base_=0):
            act.wait_ge(slot_used, base_ + ticks)

        def turned(first, gain=None, bias=None, n=8):
            for i in range(n):
                m = first + i
                act.wait_ge(tr_full, m + 1)
                if not isinstance(m, int) or m >= 2:
                    act.wait_ge(split_done, m - 1)
                if gain is None:
                    nc.scalar.activation(TMP[:, i % 2, :, :], BK[i % 4].rearrange("p (j t) -> p j t", j=2)[:, :, :], ACT.Copy).then_inc(tr_tmp, 1)
                    continue
                for j in range(2):
                    kt = 2 * i + j
                    ins_ = nc.scalar.activation(TMP[:, i % 2, j, :], BK[i % 4][:, j * TOK:(j + 1) * TOK], ACT.Identity,
                                                scale=PT[:, 0, gain + kt:gain + kt + 1],
                                                bias=0.0 if bias is None else PT[:, 0, bias + kt:bias + kt + 1])
                ins_.then_inc(tr_tmp, 1)

        act.wait_ge(params_full, 1)
        for i in range(2):
            ins_ = nc.scalar.activation(PT[:, i, :], BK[i][:, 0:P], ACT.Copy)
        ins_.then_inc(params_done, 1)
        high(0, LEAD)
        turned(TR_X)

        act.wait_ge(params_done, 1)
        nc.scalar.activation(SP[:, 0, :], PT[:, 1, 64:96], ACT.Exp).then_inc(tab_act, 1)
        high(0, 2)
        act.wait_ge(tab_dve, 1)
        nc.scalar.activation(SP[:, 1, :], SP[:, 3, :], ACT.Exp).then_inc(tab_act, 1)
        high(0)
        act.wait_ge(tab_dve, 2)
        nc.scalar.activation(SP[:, 4:6, :], SP[:, 4:6, :], ACT.Sin, scale=SINK).then_inc(tab_act, 1)
        high(0)
        act.wait_ge(tab_dve, 3)
        nc.scalar.activation(SP[:, 6:8, :], SP[:, 6:8, :], ACT.Sin, scale=SINK).then_inc(tab_act, 1)
        high(0, 4)
        for n in range(8):
            act.wait_ge(bc_full, n + 1)
            dst = BT if n < 4 else CT
            i = 2 * (n % 4)
            nc.scalar.activation(dst[:, i:i + 2, :, :].rearrange("p c r n -> p (c r n)"), BK[n % 4][:, :], ACT.Copy).then_inc(bc_done, 1)

        def u_copy(zu):
            done(SLOTS * (zu + 1))
            nc.scalar.activation(UT[:, 4 * zu:4 * zu + 2, :].rearrange("p m t -> p (m t)"), ACC[zu][:, 0, :], ACT.Copy).then_inc(act_part, 1)

        unit(first=lambda: u_copy(0))
        act.wait_ge(tab_dve, 4)
        nc.scalar.activation(SIN[:, :, :], TD[:, :, :], ACT.Sin, scale=SINK).then_inc(tab_act, 1)
        act.wait_ge(tab_dve, 5)
        nc.scalar.activation(COS[:, :, :], TA[:, :, :], ACT.Sin, scale=SINK).then_inc(tab_act, 1)

        def bu_copy(it):
            for b in range(2):
                n = 2 * it + b
                act.wait_ge(bu_full, n + 1)
                if it >= 2:
                    act.wait_ge(in_used, it - 1)
                    act.wait_ge(q_ready, it - 1)
                elif it == 0:
                    act.wait_ge(tab_act, 6)
                dst = BU[:, it % 2, :, :, :].rearrange("p r (c h b) t -> p (r c) h b t", c=2, h=2)[:, :, :, b, :]
                nc.scalar.activation(dst, BK[n % 3].rearrange("p (a h t) -> p a h t", a=4, h=2)[:, :, :, :], ACT.Copy).then_inc(bu_evac, 1)

        def z_epilogue(zu):
            for b in range(2):
                if b == 0:
                    done(SLOTS * (zu + 3))
                nc.scalar.activation(ZT[:, 4 * zu + 2 * b:4 * zu + 2 * b + 2, :].rearrange("p m t -> p (m t)"),
                                     ACC[zu][:, b, :], ACT.Tanh, scale=0.5).then_inc(act_part, 1)

        for zu in range(2):
            def beside(s, zu=zu):
                it = 8 * zu + s
                if it == 0:
                    u_copy(1)
                    bu_copy(0)
                if it + 1 < len(S_ITS):
                    bu_copy(it + 1)
                if it == 10:
                    z_epilogue(0)
            unit(extras=beside)
        z_epilogue(1)
        for b in range(4):
            act.wait_ge(y_read, len(S_ITS))
            yb = YT[:, 2 * b:2 * b + 2, :]
            nc.scalar.activation(yb, yb, ACT.Gelu_apprx_tanh).then_inc(hid_act, 1)
        unit(ticks=8)
        for c in range(2):
            done(SLOTS * U_GLU + 4 * (c + 1))
            for m in range(4):
                bias = PT[:, 0, 72 + 4 * c + m:73 + 4 * c + m]
                if c == 0 and m == 0:
                    act.wait_ge(tab_dve, 6)
                nc.scalar.activation(ACC[c][:, m // 2, (m % 2) * TOK:(m % 2 + 1) * TOK], ACC[c][:, m // 2, (m % 2) * TOK:(m % 2 + 1) * TOK],
                                     ACT.Tanh, scale=0.5, bias=bias).then_inc(act_part, 1)
        unit()
        unit()
        turned(TR_X1, gain=0, bias=16)

        def half_copy(unit_, group, dst, scale=1.0):
            done(SLOTS * (unit_ + 1))
            nc.scalar.activation(dst, ACC[group % 2][:, 0, :], ACT.Copy, scale=scale).then_inc(act_part, 1)

        def flat(x):
            return x.rearrange("p m t -> p (m t)")

        def kvc_high(n):
            done(SLOTS * (U_KV + n + 1))
            for b in range(2):
                nc.scalar.activation(flat(KVC[0][:, n, 2 * b:2 * b + 2, :]), ACC[(G_KV + n) % 2][:, b, :], ACT.Copy).then_inc(act_part, 1)

        unit()
        unit(first=lambda: kvc_high(0))
        unit(first=lambda: kvc_high(1))
        unit(first=lambda: half_copy(U_KV + 2, G_KV + 2, flat(KS[:, 0:2, :])))
        unit()
        act.wait_ge(slot_used, SLOTS * (U_KV + 4))
        act.wait_ge(comp_dve, 3)
        for i in range(2):
            nc.scalar.activation(HC[:, i, 0:NCMP, :].rearrange("p n h -> p (n h)"), BK[i][:, 0:NCMP * KVH],
                                 ACT.Gelu_apprx_tanh, bias=PB[:, i:i + 1]).then_inc(comp_act, 1)
        unit(first=lambda: half_copy(U_KV + 4, G_KV + 3, VS[:, 0, :]))
        unit(first=lambda: half_copy(U_KV + 5, G_KV + 4, flat(KW[:, 0:2, :])))
        unit(first=lambda: half_copy(U_KV + 6, G_KV + 5, VW[:, 0, :]))
        act.wait_ge(gate_full, 1)
        nc.scalar.activation(GATE[:, :, :].rearrange("p t n -> p (t n)"), BK[0][:, 0:NT * GATES], ACT.Tanh, scale=0.5).then_inc(gate_tanh, 1)

        def group(g, more, base_):
            def probs(n):
                act.wait_ge(nm_ready, g * 10 + (n + 1))
                if n >= 2:
                    act.wait_ge(t_full, g * 10 + (n - 1))
                if n < 2:
                    nc.scalar.activation(CP[:, n, :, :], CP[:, n, :, :], ACT.Exp).then_inc(p_ready, 1)
                    return
                for t in range(NT):
                    lo, w = (0, P) if t == 0 else (P, TOK)
                    ins_ = nc.scalar.activation(PB_[:, n % 2, lo:lo + w], BK[n % 2][:, lo:lo + w], ACT.Exp,
                                                bias=NM[:, n % 2, t:t + 1], accum_out=RS[:, n % 2, t:t + 1])
                ins_.then_inc(p_ready, 1)

            def turned_probs(n):
                act.wait_ge(t_full, g * 10 + (n + 1))
                if n >= 2:
                    act.wait_ge(o_full, g * 10 + (n - 1))
                if n < 2:
                    nc.scalar.activation(PTC[0:16, n, :], BK[2][0:16, :], ACT.Copy).then_inc(pt_ready, 1)
                else:
                    nc.scalar.activation(PTB[:, n % 2, :], BK[2][:, 0:384], ACT.Copy).then_inc(pt_ready, 1)

            def z_tanh_(j):
                act.wait_ge(slot_used, g * 32 + SLOTS * (U_NSA + 2 + j))
                if j:
                    act.wait_ge(z_used, g * 3 + j)
                for t in range(NT):
                    nc.scalar.activation(ZB[:, t, :], ACC[(1 + j) % 2][:, t, :], ACT.Tanh, scale=0.5).then_inc(z_tanh, 1)

            for j in range(3 + more):
                def beside(s, j=j):
                    i = 8 * j + s
                    if 1 <= i < 11:
                        turned_probs(i - 1)
                    if i < 10:
                        probs(i)
                unit(base_, first=(lambda j=j: z_tanh_(j - 1)) if j else None, extras=beside)
            if not more:
                z_tanh_(2)
            else:
                q_epilogue(g)
            for i in range(2):
                m = g * 2 + (TR_Y + i)
                act.wait_ge(tr_full, m + 1)
                act.wait_ge(split_done, m - 1)
                nc.scalar.activation(TMP[:, i, :, :], BK[i].rearrange("p (j t) -> p j t", j=2)[:, :, :], ACT.Copy).then_inc(tr_tmp, 1)

        def q_epilogue(g):
            act.wait_ge(slot_used, g * 32 + SLOTS * (U_NSA + 5))
            nc.scalar.activation(flat(QT[:, 0:2, :]), ACC[0][:, 0, :], ACT.Copy, scale=HD ** -0.5).then_inc(act_part, 1)

        nc.scalar.activation(flat(QT[:, 0:2, :]), ACC[0][:, 0, :], ACT.Copy, scale=HD ** -0.5).then_inc(act_part, 1)
        first_tick = SLOTS * (U_NSA + 1)
        assert seen[0] == first_tick + LEAD, (seen[0], first_tick)
        with act.Fori(0, 3) as g:
            seen[0] = LEAD
            group(g, True, g * 32 + first_tick)
        seen[0] = first_tick + 96 + LEAD
        group(3, False, 0)

        for u in range(4):
            unit()
        for t in range(NT):
            act.wait_ge(x_rows, 1 + t)
            nc.scalar.activation(HN[:, t, :], X[:, t, :], ACT.Square, accum_out=MV[:, t, 0:1]).then_inc(row_squares, 1)
        turned(TR_H, gain=32)
        act.wait_ge(lam_dve, 1)
        nc.scalar.activation(LSM[:, 0:2], LSM[:, 0:2], ACT.Exp).then_inc(lam_act, 1)

        def raw_epilogue(n):
            unit_ = U_QKV + [0, 1, 6, 7][n]
            dst = (DQ, DK)[n % 2]
            done(SLOTS * (unit_ + 1))
            if n >= 2:
                act.wait_ge(a_full, 8)
            for b in range(2):
                nc.scalar.activation(flat(dst[:, 2 * b:2 * b + 2, :]), ACC[n % 2][:, b, :], ACT.Copy,
                                     scale=64 ** -0.5 if n % 2 == 0 else 1.0).then_inc(rot_raw, 1)

        def qkv_epilogue(n):
            j, kind = divmod(n, 6)
            if kind < 2:
                raw_epilogue(2 * j + kind)
                return
            dst = {2: DV[:, 0, :], 3: flat(SQ[:, 0:2, :]), 4: flat(SK[:, 0:2, :]), 5: SV[:, 0, :]}[kind]
            if j and kind == 2:
                act.wait_ge(c_full, 4)
            if j and kind == 3:
                act.wait_ge(c_full, 8)
            half_copy(U_QKV + n, G_QKV + n, dst, HD ** -0.5 if kind == 3 else 1.0)

        def norm_squares(order):
            act.wait_ge(c_full, order + 1)
            for t in range(NT):
                ins_ = nc.scalar.activation(JUNK[:, t, :], BK[3][:, t * P:(t + 1) * P], ACT.Square,
                                            accum_out=SM[:, order % 2, 8 + t:9 + t])
            ins_.then_inc(ss_act, 1)

        def head_copy(kind, order):
            act.wait_ge(tr_full, TR_MIX + order + 1)
            act.wait_ge(split_done, TR_MIX + order - 1)
            nc.scalar.activation(TMP[:, order % 2, 0, :], BK[2][:, 0:TOK], ACT.Identity, bias=0.0,
                                 scale=HNC[:, kind:kind + 1]).then_inc(tr_tmp, 1)

        def second_stage(kind, j, i):
            for h in range(4):
                n = 4 * j + h
                order = 8 * j + (0 if kind == "diff" else 4) + h
                if kind == "diff":
                    if i == 4 * h:
                        for m in range(2):
                            dst = (P1, P2)[m]
                            act.wait_ge(a_dve, 2 * n + m + 1)
                            if n >= 2:
                                act.wait_ge(b_full, n - 1)
                            for t in range(NT):
                                lo, w = (0, P) if t == 0 else (P, TOK)
                                ins_ = nc.scalar.activation(dst[:, n % 2, lo:lo + w], BK[m][:, lo:lo + w], ACT.Exp,
                                                            bias=SM[:, n % 2, 2 * m + t:2 * m + t + 1],
                                                            accum_out=SM[:, n % 2, 4 + 2 * m + t:5 + 2 * m + t])
                            ins_.then_inc(a_act, 1)
                    if i == 4 * h + 1:
                        act.wait_ge(b_full, n + 1)
                        if n >= 2:
                            act.wait_ge(c_full, 8 * ((n - 2) // 4) + (n - 2) % 4 + 1)
                        nc.scalar.activation(PT2[:, n % 2, :], BK[2][:, 0:384], ACT.Copy).then_inc(b_act, 1)
                    if i == 4 * h + 2:
                        norm_squares(order)
                    if i == 4 * h + 5:
                        head_copy(0, order)
                else:
                    if i == 4 * h:
                        act.wait_ge(sb_abs, n + 1)
                        a = SA[:, n % 2, :]
                        nc.scalar.activation(a, a, ACT.Exp).then_inc(sb_act, 1)
                        act.wait_ge(sb_act, 3 * n + 1)
                        nc.scalar.activation(a, a, ACT.Ln, bias=1.0).then_inc(sb_act, 1)
                    if i == 4 * h + 2:
                        act.wait_ge(f_dve, 2 * n + 2)
                        nc.scalar.activation(SA[:, n % 2, :], SB[:, n % 2, :], ACT.Exp).then_inc(sb_act, 1)
                    if i == 4 * h + 4:
                        norm_squares(order)
                    if i == 4 * h + 7:
                        head_copy(1, order)

        for n in range(12):
            j, kind = divmod(n, 6)

            def beside(s, n=n, j=j, kind=kind):
                if kind >= 3:
                    second_stage("diff", j, 8 * (kind - 3) + s)
                elif j:
                    second_stage("sb", j - 1, 8 * kind + s)
            unit(first=(lambda n=n: qkv_epilogue(n - 1)) if n else None, extras=beside)
        qkv_epilogue(11)
        for i in range(24):
            second_stage("sb", 1, i)
        for u in range(4):
            unit()
        for t in range(NT):
            act.wait_ge(acc_free, G_WOUT + 4)
            nc.scalar.activation(HN[:, t, :], X[:, t, :], ACT.Square, accum_out=MV[:, t, 0:1]).then_inc(row_squares, 1)
        turned(TR_H2, gain=48)

        def hidden(q, j):
            act.wait_ge(slot_used, q * 64 + SLOTS * (U_MLP + j + 1))
            for b in range(2):
                if j:
                    act.wait_ge(hid_dve, q * 8 + (2 * j - 1 + b))
                nc.scalar.activation(REL[:, b, :], ACC[j % 2][:, b, :], ACT.Relu).then_inc(hid_relu, 1)
            for b in range(2):
                act.wait_ge(hid_dve, q * 8 + (2 * j + b + 1))
                kt = 4 * j + 2 * b
                nc.scalar.activation(flat(HH[:, kt:kt + 2, :]), HID[:, b, :], ACT.Copy).then_inc(hid_high, 1)

        def quarter(q, base_, last):
            for j in range(8):
                ticks = SLOTS - LEAD if last and j == 7 else SLOTS
                unit(base_, first=(lambda j=j: hidden(q, j - 1)) if 1 <= j <= 4 else None, ticks=ticks)

        base_ = SLOTS * U_MLP
        with act.Fori(0, 3) as q:
            seen[0] = LEAD
            quarter(q, q * 64 + base_, False)
        seen[0] = base_ + 192 + LEAD
        quarter(3, 0, True)
        for t in range(NT):
            act.wait_ge(acc_free, G_MLP + 32)
            nc.scalar.activation(HN[:, t, :], X[:, t, :], ACT.Square, accum_out=MV[:, t, 0:1]).then_inc(row_squares, 1)

    @block.vector
    def _(v):
        steps = Steps(v, dve_steps)
        seen = [0]
        V = nc.vector

        def low(base_, n=1):
            for _ in range(n):
                p = seen[0]
                seen[0] += 1
                v.wait_ge(hi_ready, base_ + (p + 1))
                k = p % SPLIT
                V.tensor_tensor(WL[:, k, :, :], RAW[:, p % SLOTS, :, :], WH[:, k, :, :].bitcast(F32), ALU.subtract).then_inc(lo_ready, 1)

        def unit(base_=0, first=None, extras=None, ticks=SLOTS):
            for s in range(ticks):
                low(base_)
                if s == 0 and first is not None:
                    first()
                if extras is not None:
                    extras(s)

        def flat(x):
            return x.rearrange("p m t -> p (m t)")

        def f32(x):
            return x.bitcast(F32)

        parts = [0]

        def part():
            parts[0] += 1
            v.wait_ge(act_part, parts[0])

        def split(m, high, low_, src, sem_=None):
            V.tensor_copy(high, src).then_inc(dve_steps, 1)
            steps.n += 1
            steps.wait()
            V.tensor_tensor(low_, src, f32(high), ALU.subtract).then_inc(sem_ or split_done, 1)

        def split_turned(first, n=8):
            for i in range(n):
                v.wait_ge(tr_tmp, first + i + 1)
                split(first + i, XH[:, 2 * i:2 * i + 2, :], XL[:, 2 * i:2 * i + 2, :], TMP[:, i % 2, :, :])

        v.wait_ge(const_in, 16)
        v.wait_ge(params_in, PARAM_DMAS * 16)
        V.tensor_copy(PR[64:96, 1, :].rearrange("s (w p) -> s w p", w=2), LDT[64:96, :].unsqueeze(2).to_broadcast([32, 2, 64])).then_inc(rows_set, 1)
        V.tensor_copy(CAUSAL_R[:, :], const("causal")).then_inc(dve_steps, 1)
        V.tensor_copy(ID_R[:, :], const("ident")).then_inc(dve_steps, 1)
        V.memset(MHALF[:, :], -0.5).then_inc(dve_steps, 1)
        V.memset(TINY[:, :], 0.0).then_inc(dve_steps, 1)
        steps.n += 4
        low(0, LEAD)
        split_turned(TR_X)

        v.wait_ge(tab_act, 1)
        dt, mag, theta, a_, red, w2_ = (SP[:, i, :] for i in (0, 1, 2, 3, 8, 9))
        lr, li = PT[:, 1, 0:32], PT[:, 1, 32:64]
        V.tensor_tensor(SP[:, 3, :], lr, dt, ALU.mult).then_inc(tab_dve, 1)
        low(0, 2)
        TT = lambda o, a, b, op: steps.link(V.tensor_tensor(o, a, b, op))
        TS = lambda o, a, s1, s2, o1, o2: steps.link(V.tensor_scalar(o, a, s1, s2, o1, o2))
        TT(theta, li, dt, ALU.mult)
        TS(w2_, theta, 1.0 / TWO_PI, MAGIC, ALU.mult, ALU.add)
        TS(w2_, w2_, -MAGIC, None, ALU.add, ALU.bypass)
        steps.link(V.scalar_tensor_tensor(red, w2_, -PI_A, theta, ALU.mult, ALU.add))
        steps.link(V.scalar_tensor_tensor(red, w2_, -PI_B, red, ALU.mult, ALU.add))
        steps.link(V.scalar_tensor_tensor(red, w2_, -PI_C, red, ALU.mult, ALU.add))
        r_, rh, rl = SP[:, 10, :], SP[:, 11, :], SP[:, 12, :]
        TS(r_, red, 1.0 / TWO_PI, None, ALU.mult, ALU.bypass)
        TS(rh, r_, 4096.0, MAGIC, ALU.mult, ALU.add)
        TS(rh, rh, -MAGIC, 1.0 / 4096.0, ALU.add, ALU.mult)
        TT(rl, r_, rh, ALU.subtract)

        def turns(whole, high, low_, sin_, cos_, between=lambda: None):
            TS(sin_, whole, MAGIC, -MAGIC, ALU.add, ALU.add)
            between()
            TT(sin_, high, sin_, ALU.subtract)
            TT(sin_, sin_, low_, ALU.add)
            between()
            TS(cos_, whole, 0.25, MAGIC, ALU.add, ALU.add)
            between()
            TS(cos_, cos_, -MAGIC, -0.25, ALU.add, ALU.add)
            TT(cos_, high, cos_, ALU.subtract)
            between()
            TT(cos_, cos_, low_, ALU.add)
            between()
            TS(cos_, cos_, 0.5, -0.5, ALU.min, ALU.max)
            return lambda: V.tensor_scalar(sin_, sin_, 0.5, -0.5, ALU.min, ALU.max)

        turns(r_, rh, rl, SP[:, 4, :], SP[:, 5, :])().then_inc(tab_dve, 1)
        low(0)
        TS(SP[:, 13, :], r_, float(CHUNK), None, ALU.mult, ALU.bypass)
        TS(SP[:, 14, :], rh, float(CHUNK), None, ALU.mult, ALU.bypass)
        TS(SP[:, 15, :], rl, float(CHUNK), None, ALU.mult, ALU.bypass)
        turns(SP[:, 13, :], SP[:, 14, :], SP[:, 15, :], SP[:, 6, :], SP[:, 7, :])().then_inc(tab_dve, 1)
        low(0)
        v.wait_ge(tab_act, 4)
        low(0, 4)
        TT(SP[:, 4:6, :], SP[:, 4:6, :], mag.unsqueeze(1).to_broadcast([P, 2, NST]), ALU.mult)
        TT(SP[:, 6:8, :], SP[:, 6:8, :], mag.unsqueeze(1).to_broadcast([P, 2, NST]), ALU.mult)
        ai, ar = SP[:, 4, :], SP[:, 5, :]
        cr, ci, inv, t0, t1 = (SP[:, i, :] for i in (8, 9, 13, 14, 15))
        TT(t0, lr, lr, ALU.mult)
        TT(t1, li, li, ALU.mult)
        TT(t0, t0, t1, ALU.add)
        steps.link(V.reciprocal(inv, t0))
        TS(ar, ar, -1.0, None, ALU.add, ALU.bypass)
        TT(t0, ar, lr, ALU.mult)
        TT(t1, ai, li, ALU.mult)
        TT(t0, t0, t1, ALU.add)
        TT(cr, t0, inv, ALU.mult)
        TT(t0, ai, lr, ALU.mult)
        TT(t1, ar, li, ALU.mult)
        TT(t0, t0, t1, ALU.subtract)
        TT(ci, t0, inv, ALU.mult)
        v.wait_ge(bc_in, 64)
        v.wait_ge(pool_steps, 1)
        crb, cib = (x.unsqueeze(2).to_broadcast([P, NST, 16]) for x in (cr, ci))
        for ri, (m, n, op) in enumerate((((crb, 0), (cib, 1), ALU.subtract), ((crb, 1), (cib, 0), ALU.add))):
            TT(BB[:, ri, :, :], BN[:, m[1], :, :], m[0], ALU.mult)
            TT(BTMP[:, ri, :, :], BN[:, n[1], :, :], n[0], ALU.mult)
            for w in range(2):
                h = slice(64 * w, 64 * w + 64)
                TT(BBLK[h, ri, :, w, :], BB[h, ri, :, :], BTMP[h, ri, :, :], op)
        for ri in range(2):
            for w in range(2):
                ins_ = V.tensor_scalar(CBLK[:, ri, :, w, :], CN[:, ri, :, :], const("group_half")[:, w:w + 1],
                                       1.0 if ri == 0 else -1.0, ALU.mult, ALU.mult)
                (steps.link if (ri, w) != (1, 1) else (lambda x: x.then_inc(blk_ready, 1)))(ins_)

        def u_copy(zu):
            part()
            v.wait_ge(slot_used, SLOTS * (zu + 1))
            V.tensor_copy(flat(UT[:, 4 * zu + 2:4 * zu + 4, :]), ACC[zu][:, 1, :]).then_inc(acc_free, 1)

        v.wait_ge(bc_full, 8)
        full = [P, NST, CHUNK]
        tt = const("steps").unsqueeze(1).to_broadcast(full)
        TT(TA[:, :, :], r_.unsqueeze(2).to_broadcast(full), tt, ALU.mult)
        low(0)
        u_copy(0)
        TT(TB[:, :, :], rh.unsqueeze(2).to_broadcast(full), tt, ALU.mult)
        low(0)
        TT(TC[:, :, :], rl.unsqueeze(2).to_broadcast(full), tt, ALU.mult)
        low(0)
        turns(TA[:, :, :], TB[:, :, :], TC[:, :, :], TD[:, :, :], TA[:, :, :], between=lambda: low(0))().then_inc(tab_dve, 1)
        V.tensor_scalar(PT[:, 0, 72:80], PT[:, 0, 72:80], 0.5, None, ALU.mult, ALU.bypass).then_inc(tab_dve, 1)
        V.tensor_copy(DECAY[:, :, :], mag.unsqueeze(2).to_broadcast(full)).then_inc(tab_dve, 1)
        v.wait_ge(tab_dve, 6)
        steps.link(V.memset(DECAY[:, :, 0:1], 0.0))

        def inputs(it):
            c, q = S_ITS[it]
            st = slice(8 * q, 8 * q + 8)
            bur, bui = BU[:, it % 2, 0, :, :], BU[:, it % 2, 1, :, :]
            v.wait_ge(bu_evac, 2 * it + 2)
            steps.inc(V.tensor_tensor(PP[:, 0, :, :], COS[:, st, :], bur, ALU.mult))
            V.tensor_tensor(PP[:, 1, :, :], COS[:, st, :], bui, ALU.mult).then_inc(in_used, 1)

        def states(it):
            v.wait_ge(xp_ready, it + 1)
            v.wait_ge(o_steps[it][0], o_steps[it][1])
            steps.link(V.tensor_tensor(HP[:, 0, :, :], HP[:, 0, :, :], XP[:, 0, :, :], ALU.subtract))
            V.tensor_tensor(HP[:, 1, :, :], HP[:, 1, :, :], XP[:, 1, :, :], ALU.add).then_inc(hs_ready, 1)

        def rotated(it):
            c, q = S_ITS[it]
            st = slice(8 * q, 8 * q + 8)
            v.wait_ge(q_ready, it + 1)
            v.wait_ge(in_used, it + 1)
            QR = QP[:, it % 2, :, :, :]
            i1 = steps.inc(V.tensor_tensor(PP[:, 0, :, :], PP[:, 0, :, :], QR[:, 0, :, :], ALU.add))
            i2 = steps.inc(V.tensor_tensor(PP[:, 1, :, :], PP[:, 1, :, :], QR[:, 1, :, :], ALU.subtract))
            if c:
                for ri in range(2):
                    steps.wait(i1 if ri == 0 else i2)
                    steps.inc(V.tensor_tensor(PP[:, ri, :, 0:1], PP[:, ri, :, 0:1], CARRY[:, q, ri, :].unsqueeze(2), ALU.add))
            for ri in range(2):
                steps.wait()
                ins_ = V.tensor_tensor_scan(G[:, ri, :, :].rearrange("p s t -> p (s t)"),
                                            DECAY[:, st, :].rearrange("p s t -> p (s t)"),
                                            PP[:, ri, :, :].rearrange("p s t -> p (s t)"), 0.0, ALU.mult, ALU.add)
                ins_.then_inc(g_ready, 1)
            v.wait_ge(g_ready, 2 * it + 2)
            if it:
                v.wait_ge(y_full, it)
            steps.inc(V.tensor_tensor(HP[:, 0, :, :], COS[:, st, :], G[:, 0, :, :], ALU.mult))
            v_ = steps.inc(V.tensor_tensor(HP[:, 1, :, :], COS[:, st, :], G[:, 1, :, :], ALU.mult))
            o_steps.append((dve_steps, v_))
            if c < 3:
                er, ei = G[:, 0, :, CHUNK - 1:CHUNK], G[:, 1, :, CHUNK - 1:CHUNK]
                ms_, mc = (SP[:, i, st].unsqueeze(2) for i in (6, 7))
                ct = [CTMP[:, i, :].unsqueeze(2) for i in range(4)]
                for o, a, b in ((ct[0], er, mc), (ct[1], ei, ms_), (ct[2], ei, mc), (ct[3], er, ms_)):
                    steps.inc(V.tensor_tensor(o, a, b, ALU.mult))
                steps.wait()
                steps.inc(V.tensor_tensor(CARRY[:, q, 0, :].unsqueeze(2), ct[0], ct[1], ALU.subtract))
                steps.link(V.tensor_tensor(CARRY[:, q, 1, :].unsqueeze(2), ct[2], ct[3], ALU.add))

        def y_copy(it):
            c, q = S_ITS[it]
            v.wait_ge(y_full, it + 1)
            for cbl in range(2):
                cb = 2 * q + cbl
                ins_ = V.scalar_tensor_tensor(YT[:, cb, c * CHUNK:(c + 1) * CHUNK], UT[:, cb, c * CHUNK:(c + 1) * CHUNK],
                                              PT[:, 0, 64 + cb:65 + cb], BK[3][:, (q * 2 + cbl) * CHUNK:(q * 2 + cbl + 1) * CHUNK],
                                              ALU.mult, ALU.add)
            ins_.then_inc(y_read, 1)

        def z_epilogue(zu):
            for b in range(2):
                part()
                zt = flat(ZT[:, 4 * zu + 2 * b:4 * zu + 2 * b + 2, :])
                ins_ = V.scalar_tensor_tensor(zt, zt, 1.0, ACC[zu][:, b, :], ALU.add, ALU.mult)
                if b:
                    ins_.then_inc(acc_free, 1)
                else:
                    steps.inc(ins_)

        o_steps = []
        v.wait_ge(tab_act, 6)
        for zu in range(2):
            def beside(s, zu=zu):
                it = 8 * zu + s
                if it == 0:
                    u_copy(1)
                inputs(it)
                if it:
                    states(it - 1)
                if it >= 2:
                    y_copy(it - 2)
                rotated(it)
                if it == 10:
                    z_epilogue(0)
            unit(extras=beside)
        last = len(S_ITS) - 1
        states(last)
        y_copy(last - 1)
        y_copy(last)
        z_epilogue(1)
        for b in range(4):
            v.wait_ge(hid_act, b + 1)
            split(None, HH[:, 2 * b:2 * b + 2, :], HL[:, 2 * b:2 * b + 2, :], YT[:, 2 * b:2 * b + 2, :], h_ready)
        unit()
        for c in range(2):
            for b in range(2):
                part()
                part()
                g_ = flat(YT[:, 4 * c + 2 * b:4 * c + 2 * b + 2, :])
                z_ = flat(ZT[:, 4 * c + 2 * b:4 * c + 2 * b + 2, :])
                ins_ = V.scalar_tensor_tensor(g_, ACC[c][:, b, :], 1.0, g_, ALU.add, ALU.mult)
                if b:
                    ins_.then_inc(acc_free, 1)
                    v.wait_ge(acc_free, G_GLU + c + 1)
                else:
                    steps.link(ins_)
                steps.link(V.scalar_tensor_tensor(g_, g_, 0.25, z_, ALU.mult, ALU.mult))
                kt = CB + 4 * c + 2 * b
                split(None, HH[:, kt:kt + 2, :], HL[:, kt:kt + 2, :], YT[:, 4 * c + 2 * b:4 * c + 2 * b + 2, :], h_ready)

        def residual(unit_done, pair, chunk, alpha=None):
            v.wait_ge(slot_used, unit_done)
            for t in range(NT):
                xr = X[:, t, chunk * COLS:(chunk + 1) * COLS] if isinstance(chunk, int) else None
                if alpha is None:
                    ins_ = V.tensor_tensor(xr, xr, ACC[pair][:, t, :], ALU.add)
                else:
                    ins_ = V.scalar_tensor_tensor(xr, xr, alpha, ACC[pair][:, t, :], ALU.mult, ALU.add)
                if t:
                    ins_.then_inc(acc_free, 1)
                else:
                    steps.inc(ins_)

        def chunk_stats(chunk, group):
            v.wait_ge(acc_free, group + 1)
            for t in range(NT):
                steps.inc(V.bn_stats(STATS[:, t, chunk, :], X[:, t, chunk * COLS:(chunk + 1) * COLS]))

        def whiten(n, rows_sem):
            steps.wait()
            for t in range(NT):
                steps.inc(V.bn_aggr(MV[:, t, :], STATS[:, t, :, :]))
            steps.wait()
            V.tensor_scalar(MS[:, 0:NT], MV[:, :, 1:2].rearrange("p t o -> p (t o)"), LN_EPS, None, ALU.add, ALU.bypass).then_inc(ms_rows, 1)
            v.wait_ge(rstd_rows, n)
            for t in range(NT):
                ins_ = V.tensor_scalar(X[:, t, :], X[:, t, :], MV[:, t, 0:1], RSTD[:, t:t + 1], ALU.subtract, ALU.mult)
                if t:
                    ins_.then_inc(rows_sem, 1)
                else:
                    steps.inc(ins_)

        v.wait_ge(x_loaded, 16 * (NT + 1))
        for c in range(4):
            if c % 2 == 0:
                low(0, SLOTS)
            residual(SLOTS * (U_AOUT + c // 2) + 4 * (c % 2) + 4, (G_AOUT + c) % 2, c, ALPHA)
            chunk_stats(c, G_AOUT + c)
        whiten(1, rows_ready)
        split_turned(TR_X1)

        def half_copy(unit_, group, dst, scale=1.0):
            part()
            v.wait_ge(slot_used, SLOTS * (unit_ + 1))
            ins_ = V.tensor_scalar(dst, ACC[group % 2][:, 1, :], scale, None, ALU.mult, ALU.bypass)
            ins_.then_inc(acc_free, 1)

        def kvc_low(n):
            for b in range(2):
                part()
                ins_ = V.tensor_tensor(flat(KVC[1][:, n, 2 * b:2 * b + 2, :]), ACC[(G_KV + n) % 2][:, b, :],
                                       f32(flat(KVC[0][:, n, 2 * b:2 * b + 2, :])), ALU.subtract)
                if b:
                    ins_.then_inc(acc_free, 1)
                else:
                    steps.inc(ins_)

        unit()
        unit(first=lambda: kvc_low(0))

        def positions():
            kvc_low(1)
            v.wait_ge(acc_free, G_KV + 2)
            for i, src in enumerate((PT[:, 0, 80:112], PT[:, 1, 96:128])):
                hi_ = PSR[0][:, i, :, :]
                src = src.unsqueeze(2).to_broadcast([P, 32, 2])
                steps.link(V.tensor_copy(hi_, src))
                V.tensor_tensor(PSR[1][:, i, :, :], src, f32(hi_), ALU.subtract).then_inc(comp_dve, 1)

        unit(first=positions)
        unit(first=lambda: half_copy(U_KV + 2, G_KV + 2, flat(KS[:, 2:4, :])))
        unit()
        v.wait_ge(slot_used, SLOTS * (U_KV + 4))
        for i in range(2):
            ins_ = V.tensor_copy(PB[:, i:i + 1], BK[2 + i][:, 0:1])
            (steps.inc if i == 0 else (lambda x: x.then_inc(comp_dve, 1)))(ins_)
        unit(first=lambda: half_copy(U_KV + 4, G_KV + 3, VS[:, 1, :]))
        steps.inc(V.memset(KC[:, NCMP:16, :], 0.0))
        steps.inc(V.memset(VC[:, :, :], 0.0))
        steps.wait()
        v.wait_ge(comp_full, 1)
        steps.inc(V.tensor_copy(KC[:, 0:NCMP, :].rearrange("p n h -> p (n h)"), BK[0][:, 0:NCMP * KVH]))
        V.tensor_copy(VC[0:NCMP, :, :].rearrange("p h d -> p (h d)"), BK[1][0:NCMP, :]).then_inc(comp_dve, 1)
        unit(first=lambda: half_copy(U_KV + 5, G_KV + 4, flat(KW[:, 2:4, :])))
        unit(first=lambda: half_copy(U_KV + 6, G_KV + 5, VW[:, 1, :]))
        v.wait_ge(natural_done, 1)
        v.wait_ge(gw_in, 16)
        steps.link(V.tensor_copy(GWS[0][:, :, :], GW[:, :, :]))
        V.tensor_tensor(GWS[1][:, :, :], GW[:, :, :], f32(GWS[0][:, :, :]), ALU.subtract).then_inc(gate_split, 1)

        steps.inc(V.memset(PTC[:, :, :], 0.0))
        v.wait_ge(gate_tanh, 1)
        steps.link(V.tensor_scalar(GATE[:, :, :], GATE[:, :, :], 1.0, 0.25, ALU.add, ALU.mult))
        for t in range(NT):
            steps.inc(V.tensor_scalar(GATE[:, t, 0:HEADS], GATE[:, t, 0:HEADS], const("cmp_valid")[:, 16 * t:16 * t + 1],
                                      None, ALU.mult, ALU.bypass))
        steps.wait()

        def group(g, more, base_):
            def maxima(n):
                v.wait_ge(s_full, g * 10 + (n + 1))
                if n < 2:
                    c = CP[:, n, :, :]
                    bias = const("cmp_bias")[:, 16 * n:16 * n + 16].unsqueeze(1).to_broadcast([P, 4, 16])
                    steps.link(V.tensor_tensor(c, BK[n][:, 0:64].rearrange("p (h n) -> p h n", h=4), bias, ALU.add))
                    steps.link(V.tensor_reduce(NM[:, n, 0:4], c, AX_X, ALU.max))
                    V.tensor_tensor(c, c, NM[:, n, 0:4].unsqueeze(2).to_broadcast([P, 4, 16]), ALU.subtract).then_inc(nm_ready, 1)
                    return
                for t in range(NT):
                    lo, w = (0, P) if t == 0 else (P, TOK)
                    ins_ = V.tensor_reduce(NM[:, n % 2, t:t + 1], BK[n % 2][:, lo:lo + w], AX_X, ALU.max, negate=True)
                    if t:
                        ins_.then_inc(nm_ready, 1)
                    else:
                        steps.inc(ins_)

            def scales(n):
                v.wait_ge(p_ready, g * 10 + (n + 1))
                w = 4 if n < 2 else 2
                rs, os = RS[:, n % 2, 0:w], OS[:, n % 2, 0:w]
                if n < 2:
                    steps.link(V.tensor_reduce(rs, CP[:, n, :, :], AX_X, ALU.add))
                    gate = GATE[:, n, bass.ds(g * 4, 4)]
                else:
                    branch, h = (1 if n < 6 else 2), (n - 2) % 4
                    gate = GATE[:, :, bass.ds(g * 4 + (branch * HEADS + h), 1)].rearrange("p t o -> p (t o)")
                steps.link(V.reciprocal(rs, rs))
                steps.inc(V.tensor_tensor(os, rs, gate, ALU.mult))

            def outputs(n):
                steps.wait()
                v.wait_ge(o_full, g * 10 + (n + 1))
                for m in range(4 if n < 2 else 2):
                    branch, t, h = (0, n, m) if n < 2 else (1 if n < 6 else 2, m, (n - 2) % 4)
                    ins_ = V.tensor_scalar(OB[:, branch, t, h * HD:(h + 1) * HD], BK[3][:, m * P:(m + 1) * P],
                                           OS[:, n % 2, m:m + 1], None, ALU.mult, ALU.bypass)
                    if m == (3 if n < 2 else 1):
                        ins_.then_inc(o_read, 1)
                    else:
                        steps.inc(ins_)

            def z_epilogue(j):
                v.wait_ge(o_read, g * 10 + (2, 6, 10)[j])
                for t in range(NT):
                    v.wait_ge(z_tanh, g * 6 + (2 * j + t + 1))
                    z_ = ZB[:, t, :]
                    ins_ = V.scalar_tensor_tensor(z_, z_, 1.0, ACC[(1 + j) % 2][:, t, :], ALU.add, ALU.mult)
                    if t:
                        ins_.then_inc(acc_free, 1)
                        v.wait_ge(acc_free, g * 4 + (G_NSA + 2 + j))
                    else:
                        steps.link(ins_)
                if j == 0:
                    V.tensor_tensor(YB[:, :, :], ZB[:, :, :], OB[:, 0, :, :], ALU.mult).then_inc(z_used, 1)
                    return
                steps.link(V.tensor_tensor(ZB[:, :, :], ZB[:, :, :], OB[:, j, :, :], ALU.mult))
                v.wait_ge(z_used, g * 3 + j)
                ins_ = V.tensor_tensor(YB[:, :, :], YB[:, :, :], ZB[:, :, :], ALU.add)
                ins_.then_inc(z_used, 1)
                if j == 2:
                    v.wait_ge(z_used, g * 3 + 3)
                    V.tensor_copy(TINY[:, 0:1], TINY[:, 1:2]).then_inc(rows_ready, 1)

            for j in range(3 + more):
                def beside(s, j=j):
                    i = 8 * j + s
                    if 2 <= i < 12:
                        outputs(i - 2)
                    if i < 10:
                        maxima(i)
                    if i < 10:
                        scales(i)
                unit(base_, first=(lambda j=j: z_epilogue(j - 1)) if j else None, extras=beside)
            if more:
                q_epilogue(g, g + (parts[0] + 1))
            else:
                z_epilogue(2)
            for i in range(2):
                v.wait_ge(tr_tmp, g * 2 + (TR_Y + i + 1))
                kt = bass.ds(g * 4 + 2 * i, 2)
                split(None, HH[:, kt, :], HL[:, kt, :], TMP[:, i, :, :])

        def q_epilogue(g, share):
            v.wait_ge(act_part, share)
            v.wait_ge(slot_used, g * 32 + SLOTS * (U_NSA + 5))
            V.tensor_scalar(flat(QT[:, 2:4, :]), ACC[0][:, 1, :], HD ** -0.5, None, ALU.mult, ALU.bypass).then_inc(acc_free, 1)

        parts[0] += 1
        q_epilogue(-1, parts[0])
        first_tick = SLOTS * (U_NSA + 1)
        assert seen[0] == first_tick + LEAD, (seen[0], first_tick)
        n0, per = steps.n, GROUP_STEPS
        with v.Fori(0, 3) as g:
            seen[0], steps.base, steps.n = LEAD, g * per + n0, 0
            group(g, True, g * 32 + first_tick)
            assert steps.n == per, steps.n
        seen[0], steps.base, steps.n = first_tick + 96 + LEAD, 0, n0 + 3 * per
        parts[0] += 3
        group(3, False, 0)

        for c in range(4):
            low(0, SLOTS)
            residual(SLOTS * (U_BOUT + c + 1), (G_BOUT + c) % 2, c, ALPHA)
            chunk_stats(c, G_BOUT + c)
        whiten(2, dve_steps)
        steps.n += 1
        v.wait_ge(gain_in, 96)
        for t in range(NT):
            steps.wait()
            steps.link(V.tensor_tensor(X[:, t, :], X[:, t, :], GB2[:, 0, :], ALU.mult))
            V.tensor_tensor(X[:, t, :], X[:, t, :], GB2[:, 1, :], ALU.add).then_inc(x_rows, 1)

        def root_mean_squares(n, squares, dst):
            v.wait_ge(row_squares, squares)
            V.tensor_scalar(MS[:, 0:NT], MV[:, :, 0:1].rearrange("p t o -> p (t o)"), 1.0 / DM, NORM_EPS,
                            ALU.mult, ALU.add).then_inc(ms_rows, 1)
            v.wait_ge(rstd_rows, n)
            for t in range(NT):
                ins_ = V.tensor_scalar(dst[:, t, :], X[:, t, :], RSTD[:, t:t + 1], None, ALU.mult, ALU.bypass)
                if t and dst is HN:
                    ins_.then_inc(rows_ready, 1)
                else:
                    steps.inc(ins_)

        v.wait_ge(x_rows, 2)
        root_mean_squares(3, 2, HN)
        split_turned(TR_H)
        v.wait_ge(lam_in, 64)
        steps.link(V.tensor_tensor(LAM4[:, 0:4:2, :], LAM4[:, 0:4:2, :], LAM4[:, 1:4:2, :], ALU.mult))
        V.tensor_reduce(LSM[:, 0:2], LAM4[:, 0:4:2, :], AX_X, ALU.add).then_inc(lam_dve, 1)
        v.wait_ge(lam_act, 1)
        steps.link(V.tensor_tensor(LSM[:, 2:3], LSM[:, 1:2], LSM[:, 0:1], ALU.subtract))
        steps.inc(V.tensor_scalar(LSM[:, 3:4], LSM[:, 2:3], -LAM_INIT, None, ALU.add, ALU.bypass))
        v.wait_ge(hn_in, 32)
        steps.link(V.tensor_scalar(HNC[:, 0:1], HNC[:, 0:1], 1.0 - LAM_INIT, None, ALU.mult, ALU.bypass))

        def rotary(n):
            group = [G_QKV, G_QKV + 1, G_QKV + 6, G_QKV + 7][n]
            dst = (DQ, DK)[n % 2]
            for b in range(2):
                v.wait_ge(rot_full, 2 * n + b + 1)
                d = dst[:, 2 * b:2 * b + 2, :]
                wide = [P, 2, TOK]
                ins_ = V.tensor_tensor(RT[:, :, :], ACC[group % 2][:, b, :].rearrange("p (m t) -> p m t", m=2),
                                       const("sin").unsqueeze(1).to_broadcast(wide), ALU.mult)
                steps.inc(ins_)
                steps.link(V.tensor_tensor(d, d, const("cos").unsqueeze(1).to_broadcast(wide), ALU.mult))
                ins_ = V.tensor_tensor(d, d, RT[:, :, :], ALU.add)
                if b:
                    ins_.then_inc(acc_free, 1)
                else:
                    steps.link(ins_)

        def qkv_epilogue(n):
            j, kind = divmod(n, 6)
            if kind < 2:
                return
            dst = {2: DV[:, 1, :], 3: flat(SQ[:, 2:4, :]), 4: flat(SK[:, 2:4, :]), 5: SV[:, 1, :]}[kind]
            half_copy(U_QKV + n, G_QKV + n, dst, HD ** -0.5 if kind == 3 else 1.0)

        def mean_square(order):
            v.wait_ge(ss_act, order + 1)
            r = order % 2
            V.tensor_scalar(SM[:, r, 18:20], SM[:, r, 8:10], 1.0 / HD, NORM_EPS, ALU.mult, ALU.add).then_inc(ms_dve, 1)

        def normed(order):
            v.wait_ge(r_pool, order + 1)
            for t in range(NT):
                ins_ = V.tensor_scalar(ON[:, order % 2, t, :], BK[3][:, t * P:(t + 1) * P],
                                       SM[:, order % 2, 20 + t:21 + t], None, ALU.mult, ALU.bypass)
                if t:
                    ins_.then_inc(on_dve, 1)
                else:
                    steps.inc(ins_)

        def head_split(order, kt):
            v.wait_ge(tr_tmp, TR_MIX + order + 1)
            split(None, HH[:, kt, :], HL[:, kt, :], TMP[:, order % 2, 0, :])

        def diagonal(x):
            return x.rearrange("p (b q) -> p b q", b=3)[:, 0:3:2, :]

        def second_stage(kind, j, i):
            for h in range(4):
                n = 4 * j + h
                r = n % 2
                order = 8 * j + (0 if kind == "diff" else 4) + h
                if kind == "diff":
                    if i == 4 * h:
                        for m in range(2):
                            v.wait_ge(a_full, 2 * n + m + 1)
                            for t in range(NT):
                                lo, w = (0, P) if t == 0 else (P, TOK)
                                ins_ = V.tensor_reduce(SM[:, r, 2 * m + t:2 * m + t + 1], BK[m][:, lo:lo + w], AX_X, ALU.max, negate=True)
                                if t:
                                    ins_.then_inc(a_dve, 1)
                                else:
                                    steps.inc(ins_)
                        v.wait_ge(a_act, 2 * n + 2)
                        steps.link(V.reciprocal(SM[:, r, 12:16], SM[:, r, 4:8]))
                        steps.link(V.tensor_scalar(SM[:, r, 16:18], SM[:, r, 14:16], LSM[:, 3:4], None, ALU.mult, ALU.bypass))
                        for t in range(NT):
                            lo, w = (0, P) if t == 0 else (P, TOK)
                            p1, p2 = P1[:, r, lo:lo + w], P2[:, r, lo:lo + w]
                            steps.link(V.tensor_scalar(p1, p1, SM[:, r, 12 + t:13 + t], None, ALU.mult, ALU.bypass))
                            ins_ = V.scalar_tensor_tensor(p1, p2, SM[:, r, 16 + t:17 + t], p1, ALU.mult, ALU.add)
                            if t:
                                ins_.then_inc(w_dve, 1)
                            else:
                                steps.inc(ins_)
                    if i == 4 * h + 3:
                        mean_square(order)
                    if i == 4 * h + 4:
                        normed(order)
                    if i == 4 * h + 6:
                        head_split(order, 4 * j + h)
                else:
                    if i == 4 * h:
                        v.wait_ge(sb_full, 2 * n + 1)
                        s_ = BK[0][:, 0:384]
                        a, b, c = SA[:, r, :], SB[:, r, :], SC[:, r, :]
                        steps.link(V.tensor_scalar(b, s_, 0.0, None, ALU.min, ALU.bypass))
                        V.scalar_tensor_tensor(a, b, 2.0, s_, ALU.mult, ALU.subtract).then_inc(sb_abs, 1)
                        v.wait_ge(sb_act, 3 * n + 2)
                        steps.link(V.tensor_tensor(b, b, a, ALU.subtract))
                        steps.link(V.tensor_tensor(c, b, s_, ALU.subtract))
                        V.tensor_tensor(diagonal(c), diagonal(c), const("strict").unsqueeze(1).to_broadcast([P, 2, P]),
                                        ALU.mult).then_inc(f_dve, 1)
                    if i == 4 * h + 2:
                        v.wait_ge(sb_full, 2 * n + 2)
                        b = SB[:, r, :]
                        V.tensor_tensor(b, b, BK[1][:, 0:384], ALU.add).then_inc(f_dve, 1)
                    if i == 4 * h + 5:
                        mean_square(order)
                    if i == 4 * h + 6:
                        normed(order)
                    if i == 4 * h + 8:
                        head_split(order, 8 + 4 * j + h)

        for n in range(12):
            j, kind = divmod(n, 6)

            def beside(s, n=n, j=j, kind=kind):
                if s == 1 and kind in (1, 2):
                    rotary(2 * j + kind - 1)
                if kind >= 3:
                    second_stage("diff", j, 8 * (kind - 3) + s)
                elif j:
                    second_stage("sb", j - 1, 8 * kind + s)
            unit(first=(lambda n=n: qkv_epilogue(n - 1)) if n else None, extras=beside)
        qkv_epilogue(11)
        for i in range(24):
            second_stage("sb", 1, i)

        for c in range(4):
            low(0, SLOTS)
            residual(SLOTS * (U_WOUT + c + 1), (G_WOUT + c) % 2, c)
        v.wait_ge(acc_free, G_WOUT + 4)
        root_mean_squares(4, 4, HN)
        split_turned(TR_H2)

        def hidden(q, j):
            for b in range(2):
                v.wait_ge(hid_relu, q * 8 + (2 * j + b + 1))
                if j:
                    v.wait_ge(hid_high, q * 8 + (2 * j + b - 1))
                V.scalar_tensor_tensor(HID[:, b, :], ACC[j % 2][:, b, :], 0.0, REL[:, b, :], ALU.max, ALU.mult).then_inc(hid_dve, 1)
            v.wait_ge(hid_dve, q * 8 + (2 * j + 2))
            V.tensor_copy(TINY[:, 0:1], TINY[:, 1:2]).then_inc(acc_free, 1)
            for b in range(2):
                kt = 4 * j + 2 * b
                v.wait_ge(hid_high, q * 8 + (2 * j + b + 1))
                V.tensor_tensor(flat(HL[:, kt:kt + 2, :]), HID[:, b, :], f32(flat(HH[:, kt:kt + 2, :])), ALU.subtract).then_inc(h_ready, 1)

        def quarter(q, base_, last):
            for j in range(8):
                def first(j=j):
                    if j <= 4:
                        hidden(q, j - 1)
                    else:
                        residual(q * 64 + SLOTS * (U_MLP + j), (j - 1) % 2, j - 5)
                ticks = SLOTS - LEAD if last and j == 7 else SLOTS
                unit(base_, first=first if j else None, ticks=ticks)
            residual(q * 64 + SLOTS * (U_MLP + 8), 1, 3)

        base_ = SLOTS * U_MLP
        n0, per = steps.n, QUARTER_STEPS
        with v.Fori(0, 3) as q:
            seen[0], steps.base, steps.n = LEAD, q * per + n0, 0
            quarter(q, q * 64 + base_, False)
            assert steps.n == per, steps.n
        seen[0], steps.base, steps.n = base_ + 192 + LEAD, 0, n0 + 3 * per
        quarter(3, 0, True)
        v.wait_ge(acc_free, G_MLP + 32)
        root_mean_squares(5, 6, X)
        steps.wait()
        v.wait_ge(gain_in, 112)
        for t in range(NT):
            V.tensor_tensor(X[:, t, :], X[:, t, :], GF[:, :], ALU.mult).then_inc(out_ready, 1)

    @block.gpsimd
    def _(pool):
        GP = nc.gpsimd
        steps = Steps(pool, pool_steps)
        GP.memset(BBLK[:, :, :, :, :], 0.0).then_inc(pool_steps, 1)
        GP.memset(PR[:, 0, :], 0.0).then_inc(pool_steps, 1)
        pool.wait_ge(pool_steps, 2)
        tiles = lambda w: w.rearrange("(k p) -> k p", p=P)
        rows = [(PR[0:16, 0, :], tiles(ins["ln_g"][0])), (PR[16:32, 0, :], tiles(ins["ln_b"][0])),
                (PR[32:48, 0, :], tiles(ins["ln1_2"][0])), (PR[48:64, 0, :], tiles(ins["ln2_2"][0])),
                (PR[64:72, 0, :], tiles(ins["a_d"][0])), (PR[72:80, 0, :], tiles(ins["a_b_glu"][0])),
                (PR[80:112, 0, :], ins["cmp_pos_k"]), (PR[96:128, 1, :], ins["cmp_pos_v"]),
                (PR[0:32, 1, :], ins["a_lam_re"][0].rearrange("(s w) p -> s (w p)", w=2)),
                (PR[32:64, 1, :], ins["a_lam_im"][0].rearrange("(s w) p -> s (w p)", w=2)),
                (LDT[64:96, :], ins["a_log_dt"][0].rearrange("(s w) -> s w", w=2))]
        assert len(rows) == PARAM_DMAS
        for dst, src in rows:
            pool.dma_start(dst, src).then_inc(params_in, 16)
        for i, name in enumerate(("a_b_re", "a_b_im")):
            pool.dma_start(BN[:, i, :, :], ins[name][0].rearrange("(s w) p c -> (w p) s c", w=2)).then_inc(bc_in, 16)
        for i, name in enumerate(("a_c_re", "a_c_im")):
            pool.dma_start(CN[:, i, :, :], ins[name][0].rearrange("(k r) c p -> (r c) k p", r=8)).then_inc(bc_in, 16)
        for i, name in enumerate(("diff_head_norm_2", "sb_head_norm_2")):
            pool.dma_start(HNC[:, i:i + 1], ins[name][0].rearrange("(p o) -> p o", o=1)).then_inc(hn_in, 16)

        def q_products(it):
            c, q = S_ITS[it]
            st = slice(8 * q, 8 * q + 8)
            pool.wait_ge(bu_evac, 2 * it + 2)
            if it >= 2:
                pool.wait_ge(g_ready, 2 * it - 2)
            for i in range(2):
                ins_ = GP.tensor_tensor(QP[:, it % 2, i, :, :], SIN[:, st, :], BU[:, it % 2, 1 - i, :, :], ALU.mult)
            ins_.then_inc(q_ready, 1)

        def x_products(it):
            c, q = S_ITS[it]
            st = slice(8 * q, 8 * q + 8)
            pool.wait_ge(g_ready, 2 * it + 2)
            if it:
                pool.wait_ge(hs_ready, it)
            for i in range(2):
                ins_ = GP.tensor_tensor(XP[:, i, :, :], SIN[:, st, :], G[:, 1 - i, :, :], ALU.mult)
            ins_.then_inc(xp_ready, 1)

        pool.wait_ge(tab_act, 6)
        q_products(0)
        for it in range(len(S_ITS)):
            if it + 1 < len(S_ITS):
                q_products(it + 1)
            x_products(it)

        def rsqrt(n):
            pool.wait_ge(ms_rows, n)
            GP.tensor_tensor(RSTD[:, 0:NT], MS[:, 0:NT], MHALF[:, 0:NT], ALU.pow).then_inc(rstd_rows, 1)

        def gains(dst, name, layer, cols):
            src = ins[name][layer] if layer is not None else ins[name]
            return dst, src[cols].partition_broadcast(P)

        pool.wait_ge(h_ready, 8)
        pool.wait_ge(y_full, 16)
        for i, name in enumerate(("cmp_w2_k", "cmp_w2_v")):
            pool.dma_start(W2[:, i, :], ins[name]).then_inc(kvp_in, 16)
        for half in range(2):
            cols = slice(half * DM // 2, (half + 1) * DM // 2)
            if half:
                pool.wait_ge(pool_steps, steps.n)
            for i, name in enumerate(("ln_g", "ln_b")):
                pool.dma_start(GB[:, i, :], ins[name][0][cols].partition_broadcast(P)).then_inc(gain_in, 16)
            if half == 0:
                rsqrt(1)
                pool.wait_ge(tr_full, TR_X1 + 8)
            pool.wait_ge(gain_in, 32 * (half + 1))
            if half == 0:
                steps.n = 2
            for t in range(NT):
                steps.link(GP.tensor_tensor(X[:, t, cols], X[:, t, cols], GB[:, 0, :], ALU.mult))
                ins_ = GP.tensor_tensor(X[:, t, cols], X[:, t, cols], GB[:, 1, :], ALU.add)
                if half and t:
                    ins_.then_inc(natural_done, 1)
                else:
                    steps.inc(ins_)
        pool.wait_ge(comp_dve, 4)
        pool.dma_start(GW[:, :, :], B_IN[:, ZW * 4:ZW * 4 + GATES].rearrange("(k p) n -> p k n", p=P)).then_inc(gw_in, 16)
        pool.wait_ge(rows_ready, 5)
        pool.wait_ge(o_read, 40)
        for i, name in enumerate(("ln_g", "ln_b")):
            pool.dma_start(GB2[:, i, :], ins[name][1].partition_broadcast(P)).then_inc(gain_in, 16)
        for i, name in enumerate(("lambda_q1_2", "lambda_k1_2", "lambda_q2_2", "lambda_k2_2")):
            pool.dma_start(LAM4[:, i, :], ins[name][0].partition_broadcast(P)).then_inc(lam_in, 16)
        rsqrt(2)
        rsqrt(3)

        def head_rsqrt(order):
            pool.wait_ge(ms_dve, order + 1)
            r = order % 2
            GP.tensor_tensor(SM[:, r, 20:22], SM[:, r, 18:20], MHALF[:, 0:2], ALU.pow).then_inc(r_pool, 1)

        def second_stage(kind, j, i):
            for h in range(4):
                n = 4 * j + h
                order = 8 * j + (0 if kind == "diff" else 4) + h
                if kind == "diff":
                    if i == 4 * h + 3:
                        head_rsqrt(order)
                else:
                    if i == 4 * h + 3:
                        pool.wait_ge(sb_act, 3 * n + 3)
                        d = SA[:, n % 2, :].rearrange("p (b q) -> p b q", b=3)[:, 0:3:2, :]
                        GP.tensor_tensor(d, d, const("strict").unsqueeze(1).to_broadcast([P, 2, P]), ALU.mult).then_inc(f_pool, 1)
                    if i == 4 * h + 5:
                        head_rsqrt(order)

        for j in range(2):
            for kind in ("diff", "sb"):
                for i in range(24):
                    second_stage(kind, j, i)
        pool.wait_ge(split_done, TR_MIX + 16)
        pool.dma_start(GF[:, :], ins["ln_f_2"].partition_broadcast(P)).then_inc(gain_in, 16)
        rsqrt(4)
        rsqrt(5)

    ctx.close()


NAMES = ["x", "a_w_in", "a_lam_re", "a_lam_im", "a_log_dt", "a_b_re", "a_b_im", "a_c_re", "a_c_im", "a_d", "a_w_glu",
         "a_b_glu", "a_w_out", "kv_w", "cmp_pos_k", "cmp_w1_k", "cmp_w2_k", "cmp_pos_v", "cmp_w1_v", "cmp_w2_v",
         "b_w_in", "b_w_out", "ln_g", "ln_b", "ln1_2", "w_in_2", "lambda_q1_2", "lambda_k1_2", "lambda_q2_2",
         "lambda_k2_2", "diff_head_norm_2", "sb_head_norm_2", "w_out_2", "ln2_2", "w_mlp_in_2", "w_mlp_out_2", "ln_f_2"]


def kernel(**inputs):
    import numpy as _np
    import concourse.bacc as _bacc
    from concourse import mybir as _mybir
    from concourse.bass_utils import run_bass_kernel_spmd as _run

    nc = _bacc.Bacc("TRN2", target_bir_lowering=False, num_devices=1)
    arrays, aps = {}, {}
    for name in NAMES + ["consts"]:
        a = constants() if name == "consts" else _np.ascontiguousarray(inputs[name])
        arrays[f"in_{name}"] = a
        aps[name] = nc.dram_tensor(f"in_{name}", a.shape, _mybir.dt.from_np(a.dtype), kind="ExternalInput").ap()
    out = nc.dram_tensor("out", (1, TOK, DM), F32, kind="ExternalOutput").ap()
    build(nc, aps, out)
    r = _run(nc, [arrays], core_ids=[0])
    return r.results[0]["out"]
```

```python
import math

import numpy as np
import concourse.bass as bass
from concourse import mybir

F32 = mybir.dt.float32
F32R = mybir.dt.float32r
ALU = mybir.AluOpType
ACT = mybir.ActivationFunctionType
AX_X = mybir.AxisListType.X

P = 128
TOK = 256
NT = TOK // P
DM = 2048
KT = DM // P
COLS = 512
SLOTS = 8
SPLIT = 4
LEAD = 3

SSM_W = DM // 2
CB = SSM_W // P
NST = 32
CHUNK = 64
HEADS, KVH, HD = 16, 4, 128
NCMP, CSTRIDE, CBLOCK = 15, 16, 32
ZW = 2048
GATES = 48
DIFF_H, SB_H = 8, 8
DFF = 8192

ALPHA = 4.0 ** 0.25
MAGIC = 12582912.0
TWO_PI = 2.0 * math.pi
PI_A = 6.28125
PI_B = float(np.float32(TWO_PI - PI_A - (TWO_PI - PI_A) % (2.0 ** -20)))
PI_C = float(np.float32(TWO_PI - PI_A - PI_B))
NEG = -1e30
LN_EPS, NORM_EPS = 1e-5, 1e-6
LAM_INIT = 0.8 - 0.6 * math.exp(-0.3 * 0)
PARAM_DMAS = 7
GROUP_STEPS, QUARTER_STEPS = 55, 4

U_AIN, U_GLU, U_AOUT, U_KV, U_NSA = 0, 4, 5, 7, 14
U_BOUT, U_QKV, U_WOUT, U_MLP = 30, 34, 46, 50
G_AIN, G_GLU, G_AOUT, G_KV, G_NSA = 0, 4, 6, 10, 16
G_BOUT, G_QKV, G_WOUT, G_MLP = 32, 36, 48, 52
N_UNITS = 82


OUT_ORDER = ([(c, k) for c in range(2) for k in range(6)] + [(c, k) for c in range(2) for k in (6, 7)]
             + [(c, k) for c in (2, 3) for k in range(SLOTS)])
OUT_DONE = [14, 16, 24, 32]


class Steps:

    def __init__(self, eng, sem):
        self.eng, self.sem, self.base, self.n = eng, sem, 0, 0

    def inc(self, ins):
        ins.then_inc(self.sem, 1)
        self.n += 1
        return self.base + self.n

    def wait(self, value=None):
        self.eng.wait_ge(self.sem, self.base + self.n if value is None else value)

    def link(self, ins):
        self.inc(ins)
        self.wait()


_CONST = {}
_at = 0
for _name, _width in [("ident", P), ("causal", P), ("rotate", P), ("strict", P), ("later", P), ("ones", P),
                      ("cos", TOK), ("sin", TOK), ("cmp_bias", NT * 16), ("cmp_valid", NT * 16),
                      ("steps", CHUNK), ("not_first", CHUNK), ("group_half", 2), ("group_minus", 2)]:
    _CONST[_name] = (_at, _width)
    _at += _width
CONST_W = _at


def constants():
    c = np.zeros((P, CONST_W), np.float32)

    def put(name, value):
        at, width = _CONST[name]
        c[:, at:at + width] = value.reshape(P, width)

    row, col = np.arange(P)[:, None], np.arange(P)[None, :]
    put("ident", (row == col).astype(np.float32))
    put("causal", np.where(col <= row, 0.0, NEG).astype(np.float32))
    put("strict", (row < col).astype(np.float32))
    put("later", (row > col).astype(np.float32))
    put("ones", np.ones((P, P), np.float32))
    rot = np.zeros((P, P), np.float32)
    inv_freq = (np.float32(500000.0) ** (-np.arange(0, 16, 2, dtype=np.float32) / np.float32(16))).astype(np.float32)
    cos, sin = np.ones((P, TOK), np.float32), np.zeros((P, TOK), np.float32)
    pos = np.arange(TOK, dtype=np.float32)
    for d in range(P):
        if d % 64 < 8:
            rot[d + 8, d] = -1.0
        elif d % 64 < 16:
            rot[d - 8, d] = 1.0
        if d % 64 < 16:
            angle = pos * inv_freq[d % 8]
            cos[d], sin[d] = np.cos(angle), np.sin(angle)
    put("rotate", rot)
    put("cos", cos)
    put("sin", sin)
    t = np.arange(NT)[None, :, None] * P + np.arange(P)[:, None, None]
    n = np.arange(16)[None, None, :]
    valid = (n * CSTRIDE + CBLOCK - 1 <= t) & (n < NCMP)
    put("cmp_valid", valid.astype(np.float32))
    put("cmp_bias", np.where(valid, 0.0, NEG).astype(np.float32))
    put("steps", np.broadcast_to(np.arange(CHUNK, dtype=np.float32), (P, CHUNK)))
    put("not_first", np.broadcast_to(np.arange(CHUNK) > 0, (P, CHUNK)).astype(np.float32))
    half = (np.arange(P) // 16) % 2
    put("group_half", np.stack([half == 0, half == 1], 1).astype(np.float32))
    put("group_minus", -np.stack([half == 0, half == 1], 1).astype(np.float32))
    return c


def build(nc, ins, out):
    from contextlib import ExitStack

    ctx = ExitStack()
    base = 16640
    top = [base]

    def at(name, shape, dt, offset):
        return nc.alloc_sbuf_tensor_at(name, shape, dt, offset=offset)

    def sem(name):
        return ctx.enter_context(nc.semaphore(name))

    K1 = 1024
    RAW = at("raw", [P, SLOTS, 2, COLS], F32, base)
    WH = at("w_high", [P, SPLIT, 2, COLS], F32R, base + 32 * K1)
    WL = at("w_low", [P, SPLIT, 2, COLS], F32R, base + 48 * K1)
    XH = at("x_high", [P, KT, TOK], F32R, base + 64 * K1)
    XL = at("x_low", [P, KT, TOK], F32R, base + 80 * K1)
    X = at("x_rows", [P, NT, DM], F32, base + 96 * K1)
    HH = at("h_high", [P, KT, TOK], F32R, base + 112 * K1)
    HL = at("h_low", [P, KT, TOK], F32R, base + 128 * K1)

    placed = {}

    def region(start, limit):
        place = [start]

        def take(name, shape, dt=F32):
            size = int(np.prod(shape[1:])) * 4
            t = at(name, shape, dt, base + place[0])
            placed[name] = base + place[0]
            place[0] += (size + 31) // 32 * 32
            assert place[0] <= limit, (name, place[0], limit)
            return t
        return take

    END = 207 * K1 + 500
    small = region(144 * K1, 157 * K1)
    CST = small("constants", [P, CONST_W])
    PR = small("param_rows", [P, 2, P])
    PT = small("param_cols", [P, 2, P])
    LDT = small("log_dt_rows", [P, 2])
    TMP = small("transposed_tmp", [P, 2, 2, TOK])

    def const(name):
        a, w = _CONST[name]
        return CST[:, a:a + w]

    ID = const("ident")
    CAUSAL_R = small("causal_rounded", [P, P], F32R)
    ID_R = small("ident_rounded", [P, P], F32R)
    STATS = at("ln_stats", [P, NT, 4, 6], F32, placed["param_rows"])
    CS = at("chunk_squares", [P, NT, 4], F32, placed["param_rows"] + 256)
    MV = small("mean_var", [P, NT, 2])
    RSTD = small("rstd", [P, 8])
    MHALF = small("minus_half", [P, 8])
    TINY = small("tiny", [P, 2])
    MS = small("mean_squares", [P, 8])
    HNC = small("head_gains", [P, 2])

    ssm = region(157 * K1, END)
    UT = ssm("u_cols", [P, CB, TOK])
    HX1 = ssm("state_products_b", [P, 4, 8, CHUNK])
    ZT = UT
    YT = ssm("y_cols", [P, CB, TOK])
    COS = ssm("cos_table", [P, NST, CHUNK])
    SIN = ssm("sin_table", [P, NST, CHUNK])
    DECAY = ssm("decay_table", [P, NST, CHUNK])
    SP = ssm("ssm_params", [P, 16, NST])
    CARRY = ssm("carry", [P, 4, 2, 8])
    CTMP = ssm("carry_tmp", [P, 4, 8])
    BT = at("b_rows", [P, CB, 2, P], F32, base + 96 * K1)
    CT = at("c_rows", [P, CB, 2, P], F32, base + 104 * K1)
    prep = region(112 * K1, 144 * K1)
    BN = prep("b_natural", [P, 2, NST, 16])
    CN = prep("c_natural", [P, 2, CB, 64])
    BB = prep("b_bar", [P, 2, NST, 16])
    BTMP = prep("b_tmp", [P, 2, NST, 16])
    BBLK = prep("b_block", [P, 2, NST, 2, 16])
    CBLK = prep("c_block", [P, 2, CB, 2, 64])
    core = region(112 * K1, 144 * K1)
    BU = core("bu", [P, 2, 2, 8, CHUNK])
    QP = core("q_products", [P, 2, 2, 8, CHUNK])
    PP = [core("rotated_inputs", [P, 2, 8, CHUNK]),
          at("rotated_inputs_b", [P, 2, 8, CHUNK], F32, placed["transposed_tmp"])]
    G = core("rotated_states", [P, 2, 8, CHUNK])
    HX = [core("state_products", [P, 4, 8, CHUNK]), HX1]

    kv = region(157 * K1, END)
    KS = kv("k_slc_cols", [P, KVH, TOK])
    KW = kv("k_win_cols", [P, KVH, TOK])
    VS = kv("v_slc_rows", [P, NT, COLS])
    VW = kv("v_win_rows", [P, NT, COLS])
    KC = kv("k_cmp_cols", [P, 16, KVH])
    VC = kv("v_cmp_rows", [P, KVH, HD])
    kv_end = (157 + 16) * K1 + 256 + 2048
    comp = region(kv_end, END)
    KVC = comp("kv_cmp", [P, 2, 2, KVH + 1, TOK], F32R)
    GB = comp("gain_bias_half", [P, 2, DM // 2])
    HS = comp("cmp_sums", [P, 2, NCMP, KVH + 1])
    HC = comp("cmp_hidden", [P, 2, 16, KVH])
    W2 = comp("cmp_w2", [P, 2, HD])
    nsa = region(kv_end, END)
    OB = nsa("branch_out", [P, 3, NT, COLS])
    ZB = nsa("z_tmp", [P, NT, COLS])
    QT = nsa("q_cols", [P, 4, TOK])
    PB_ = nsa("probs", [P, 2, 384])
    PTB = nsa("probs_cols", [P, 2, 384])
    CP = nsa("cmp_probs", [P, 2, 4, 16])
    GATE = nsa("gates", [P, NT, GATES])
    NM = nsa("neg_max", [P, 2, 8])
    RS = nsa("row_sum", [P, 2, 8])
    OS = nsa("out_scale", [P, 2, 8])
    YB = OB[:, 0, :, :]
    PTC = nsa("cmp_probs_cols", [P, 2, COLS])
    GT = at("gate_cols", [P, TOK], F32, placed["probs"])
    GW = at("gate_w", [P, KT, GATES], F32, base + kv_end)
    GWS = [at("gate_w_high", [P, KT, GATES], F32R, base + kv_end + 3 * K1),
           at("gate_w_low", [P, KT, GATES], F32R, base + kv_end + 6 * K1)]

    blk2 = region(157 * K1, END)
    GB2 = blk2("gain_bias", [P, 2, DM])
    HN = blk2("normed_rows", [P, NT, DM])
    att = region(157 * K1, END)
    DQ = att("diff_q_cols", [P, 4, TOK])
    DK = att("diff_k_cols", [P, 4, TOK])
    DV = att("diff_v_rows", [P, NT, COLS])
    SQ = att("sb_q_cols", [P, 4, TOK])
    SK = att("sb_k_cols", [P, 4, TOK])
    SV = att("sb_v_rows", [P, NT, COLS])
    P1 = att("probs_first", [P, 2, 384])
    P2 = att("probs_second", [P, 2, 384])
    PT2 = att("mixed_cols", [P, 2, 384])
    SA = att("stick_a", [P, 2, 384])
    SB = att("stick_b", [P, 2, 384])
    SC = att("stick_c", [P, 2, 384])
    RT = att("rotary_tmp", [P, 2, TOK])
    ON = att("head_rows", [P, 2, NT, HD])
    JUNK = att("squares", [P, NT, HD])
    SM = att("head_small", [P, 2, 24])
    LAM4 = at("lambda_rows", [P, 4, 64], F32, base + 206 * K1)
    LSM = at("lambda_small", [P, 8], F32, base + 207 * K1)
    mlp = region(157 * K1, END)
    REL = mlp("relu_tmp", [P, 2, COLS])
    HID = mlp("hidden_tmp", [P, 2, COLS])
    GF = mlp("last_gain", [P, DM])

    ACC = [ctx.enter_context(nc.psum_tensor(f"acc{i}", [P, NT, COLS], F32)) for i in range(2)]
    BK = [ctx.enter_context(nc.psum_tensor(f"bank{i}", [P, COLS], F32)) for i in range(4)]

    raw_in = [sem(f"raw_in{i}") for i in range(SLOTS)]
    hi_ready = sem("hi_ready")
    lo_ready = sem("lo_ready")
    slot_used = sem("slot_used")
    acc_free = sem("acc_free")
    act_part = sem("act_part")
    h_ready = sem("h_ready")
    tr_full = sem("tr_full")
    tr_tmp = sem("tr_tmp")
    split_done = sem("split_done")
    x_loaded = sem("x_loaded")
    x_rounded, x_low = sem("x_rounded"), sem("x_low")
    const_in, params_in, ssm_in = sem("const_in"), sem("params_in"), sem("ssm_in")
    x_first = [sem("x_first0"), sem("x_first1")]
    bc_in, kvp_in, gain_in = sem("bc_in"), sem("kvp_in"), sem("gain_in")
    dve_steps, pool_steps = sem("dve_steps"), sem("pool_steps")
    params_full, params_done = sem("params_full"), sem("params_done")
    rows_ready = sem("rows_ready")
    out_ready = sem("out_ready")
    stored = sem("stored")

    c_ready = sem("c_ready")
    coef_ready, b_products = sem("coef_ready"), sem("b_products")
    rows_set = sem("rows_set")
    blk_ready = sem("blk_ready")
    bc_full, bc_done = sem("bc_full"), sem("bc_done")
    bu_full, bu_evac = sem("bu_full"), sem("bu_evac")
    bu_half = sem("bu_half")
    q_ready = sem("q_ready")
    g_ready, xp_ready = sem("g_ready"), sem("xp_ready")
    hs_ready, y_full, y_read = sem("hs_ready"), sem("y_full"), sem("y_read")
    skip_done = sem("skip_done")
    tab_pool, tab_dve, tab_act = sem("tab_pool"), sem("tab_dve"), sem("tab_act")
    comp_full, comp_act, comp_dve = sem("comp_full"), sem("comp_act"), sem("comp_dve")
    gate_split, gate_full, gate_tanh = sem("gate_split"), sem("gate_full"), sem("gate_tanh")
    gw_in = sem("gw_in")
    s_full, nm_ready, p_ready = sem("s_full"), sem("nm_ready"), sem("p_ready")
    t_full, pt_ready, o_full, o_read = sem("t_full"), sem("pt_ready"), sem("o_full"), sem("o_read")
    z_tanh, z_used = sem("z_tanh"), sem("z_used")
    rot_raw, rot_full = sem("rot_raw"), sem("rot_full")
    a_full, b_full, c_full = sem("a_full"), sem("b_full"), sem("c_full")
    a_dve, a_act, w_dve = sem("a_dve"), sem("a_act"), sem("w_dve")
    b_act, ss_act, ms_dve, r_pool, on_dve = sem("b_act"), sem("ss_act"), sem("ms_dve"), sem("r_pool"), sem("on_dve")
    sb_full, sb_summed = sem("sb_full"), sem("sb_summed")
    f_dve, f_pool = sem("f_dve"), sem("f_pool")
    sb_abs, sb_act = sem("sb_abs"), sem("sb_act")
    x_rows = sem("x_rows")
    row_squares = sem("row_squares")
    ms_rows, rstd_rows = sem("ms_rows"), sem("rstd_rows")
    lam_in, hn_in = sem("lam_in"), sem("hn_in")
    lam_dve, lam_act = sem("lam_dve"), sem("lam_act")
    gelu_done, hid_dve, hid_high, hid_relu = sem("gelu_done"), sem("hid_dve"), sem("hid_high"), sem("hid_relu")
    natural_done = sem("natural_done")

    def rows_cols(w, row0, col0):
        return w[bass.ds(row0, 2 * P), bass.ds(col0, COLS)].rearrange("(k p) n -> p k n", p=P)

    A_IN, A_GLU, A_OUT, KV_W = ins["a_w_in"][0], ins["a_w_glu"][0], ins["a_w_out"][0], ins["kv_w"]
    B_IN, B_OUT = ins["b_w_in"][0], ins["b_w_out"][0]
    QKV_W, OUT_W, M_IN, M_OUT = ins["w_in_2"][0], ins["w_out_2"][0], ins["w_mlp_in_2"][0], ins["w_mlp_out_2"][0]
    KV_COL = [0, 1, 2, None, 3, 4, 5]

    block = ctx.enter_context(nc.Block())

    @block.sync
    def _(sp):
        def slot(unit, s, src, view=None):
            if not isinstance(unit, int) or unit > 0:
                sp.wait_ge(lo_ready, unit * SLOTS - SLOTS + s + 1)
            dst = RAW[:, s, :, :] if view is None else view
            sp.dma_start(dst, src).then_inc(raw_in[s], 16)

        def unit_wide(unit, w, col0, row0=0):
            for s in range(SLOTS):
                slot(unit, s, rows_cols(w, row0 + 2 * P * s, col0))

        def unit_half(unit, w, col0):
            for s in range(SLOTS):
                slot(unit, s, rows_cols(w, 2 * P * (s % 4), col0 + COLS * (s // 4)))

        x_in = ins["x"][0].rearrange("(t p) d -> p t d", p=P)
        sp.dma_start(CST[:, :], ins["consts"]).then_inc(const_in, 16)
        for i in range(2):
            cols = slice(i * DM // 2, (i + 1) * DM // 2)
            sp.dma_start(X[:, :, cols], x_in[:, :, cols]).then_inc(x_first[i], 16)
        for u in range(4):
            unit_wide(U_AIN + u, A_IN, COLS * u)
        unit_half(U_GLU, A_GLU, 0)
        sp.wait_ge(y_full, 16)
        sp.dma_start(X[:, :, :], x_in).then_inc(x_loaded, 16)
        for u in range(2):
            unit_half(U_AOUT + u, A_OUT, 2 * COLS * u)
        for u, c in enumerate(KV_COL):
            if c is not None:
                unit_wide(U_KV + u, KV_W, COLS * c)
                continue
            for s in range(SLOTS):
                w1 = ins["cmp_w1_k" if s < 4 else "cmp_w1_v"]
                src = w1[bass.ds(1024 * (s % 4), 1024), :].rearrange("(i d) e -> d i e", d=HD)
                slot(U_KV + u, s, src, RAW[:, s, :, :].rearrange("p k (i e) -> p (k i) e", e=HD))
        unit_wide(U_NSA, B_IN, 0)
        with sp.Fori(0, 3) as g:
            for j in range(3):
                unit_wide(g * 4 + (U_NSA + 1 + j), B_IN, g * COLS + ZW * (1 + j))
            unit_wide(g * 4 + (U_NSA + 4), B_IN, g * COLS + COLS)
        for j in range(3):
            unit_wide(U_NSA + 13 + j, B_IN, 3 * COLS + ZW * (1 + j))
        for u in range(4):
            unit_wide(U_BOUT + u, B_OUT, COLS * u)
        for n in range(12):
            half, kind = divmod(n, 6)
            unit_wide(U_QKV + n, QKV_W, 1024 * kind + COLS * half)
        for n, (c, k) in enumerate(OUT_ORDER):
            slot(U_WOUT + n // SLOTS, n % SLOTS, rows_cols(OUT_W, 2 * P * k, COLS * c))
        with sp.Fori(0, 4) as q:
            for j in range(4):
                unit_wide(q * 8 + (U_MLP + j), M_IN, q * 2048 + COLS * j)
            for j in range(4):
                unit_wide(q * 8 + (U_MLP + 4 + j), M_OUT, COLS * j, q * 2048)
        for c in range(4):
            cols = slice(c * COLS, (c + 1) * COLS)
            sp.wait_ge(out_ready, NT * (c + 1))
            sp.dma_start(out[0].rearrange("(t p) d -> p t d", p=P)[:, :, cols], X[:, :, cols]).then_inc(stored, 16)
        sp.wait_ge(stored, 16 * 4)

    S_ITS = [(c, q) for q in range(4) for c in range(TOK // CHUNK)]
    S_TICK = 16
    S_END = 4 * SLOTS - S_TICK
    B_TICK = 9
    TR_X, TR_X1, TR_Y, TR_H, TR_MIX, TR_H2 = 0, 8, 16, 24, 32, 48

    @block.tensor
    def _(pe):
        def tick(tau, s, mode, pair, kt, start, stop, xh, xl):
            k = s % SPLIT
            pe.wait_ge(lo_ready, tau + 1)
            for j in range(2):
                first, last = start and j == 0, stop and j == 1
                for n, (xa, wa) in enumerate(((xh, WH), (xh, WL), (xl, WH))):
                    if mode == "rows":
                        for t in range(NT):
                            ins_ = nc.tensor.matmul(ACC[pair][:, t, :], xa[:, kt + j, t * P:(t + 1) * P], wa[:, k, j, :],
                                                    start=first and n == 0, stop=last and n == 2)
                    else:
                        for m in range(4):
                            ins_ = nc.tensor.matmul(ACC[pair][:, m // 2, (m % 2) * TOK:(m % 2 + 1) * TOK],
                                                    wa[:, k, j, m * P:(m + 1) * P], xa[:, kt + j, :],
                                                    start=first and n == 0 and m % 2 == 0, stop=last and n == 2,
                                                    skip_group_check=True)
            ins_.then_inc(slot_used, 1)

        def gemm(unit, group, mode, xh=XH, xl=XL, ready=None, extras=None, s0=0, s1=SLOTS, kt0=0, parity=None):
            g2 = group if parity is None else parity
            if not isinstance(group, int) or group >= 2:
                pe.wait_ge(acc_free, group - 1)
            for s in range(s0, s1):
                if ready is not None:
                    ready(s)
                tick(unit * SLOTS + s, s, mode, g2 % 2, kt0 + 2 * (s - s0), s == s0, s == s1 - 1, xh, xl)
                if extras is not None:
                    extras(s)

        def split_ready(first):
            return lambda s: pe.wait_ge(split_done, first + s + 1)

        def transposes(first, rows, ready=None):
            for i in range(8):
                n = first + i
                if ready is not None:
                    ready(i)
                if i >= 4:
                    pe.wait_ge(tr_tmp, n - 3)
                for j in range(2):
                    for t in range(NT):
                        kt = 2 * i + j
                        ins_ = nc.tensor.transpose(BK[i % 4][:, (j * NT + t) * P:(j * NT + t + 1) * P],
                                                   rows[:, t, kt * P:(kt + 1) * P], ID)
                ins_.then_inc(tr_full, 1)

        pe.wait_ge(const_in, 16)
        transposes(TR_X, X, lambda i: pe.wait_ge(x_first[i // 4], 16) if i % 4 == 0 else None)

        def params_turn(s):
            if s == 0:
                pe.wait_ge(rows_set, 1)
                pe.wait_ge(tr_tmp, TR_X + 5)
                nc.tensor.transpose(BK[0][:, 0:P], PR[:, 1, :], ID).then_inc(params_full, 1)

        gemm(U_AIN, G_AIN, "cols", ready=split_ready(TR_X), extras=params_turn)

        def block_turns():
            pe.wait_ge(blk_ready, 1)
            pe.wait_ge(c_ready, 1)
            for n in range(8):
                if n < 4:
                    pe.wait_ge(tr_tmp, 8)
                    pe.wait_ge(params_done, 1)
                else:
                    pe.wait_ge(bc_done, n - 3)
                src = BBLK if n < 4 else CBLK
                for j in range(4):
                    cb, ri = 2 * (n % 4) + j // 2, j % 2
                    if n < 4:
                        m_in = BBLK[:, ri, 4 * cb:4 * cb + 4, :, :].rearrange("p s w c -> p (s w c)")
                    else:
                        m_in = CBLK[:, ri, cb, :, :].rearrange("p w n -> p (w n)")
                    ins_ = nc.tensor.transpose(BK[n % 4][:, j * P:(j + 1) * P], m_in, ID)
                ins_.then_inc(bc_full, 1)
            pe.wait_ge(params_in, 16 * PARAM_DMAS)
            pe.wait_ge(bc_done, 5)
            nc.tensor.transpose(BK[0][:, 0:P], PR[:, 0, :], ID).then_inc(params_full, 1)

        def bu(it):
            c, q = S_ITS[it]
            if it == 0:
                pe.wait_ge(bc_done, 8)
                pe.wait_ge(params_done, 2)
                pe.wait_ge(acc_free, 1)
            elif it == 8:
                pe.wait_ge(acc_free, 2)
            if it:
                pe.wait_ge(bu_evac, 2 * it - 1)
            for h in range(2):
                if h:
                    pe.wait_ge(bu_half, it + 1)
                for ri in range(2):
                    for cbl in range(2):
                        for b in range(2):
                            at_ = ((ri * 2 + cbl) * 2 + h) * CHUNK
                            cb, rows = 2 * q + cbl, slice(64 * h + 32 * b, 64 * h + 32 * b + 32)
                            ins_ = nc.tensor.matmul(BK[(2 * it + b) % 3][:, at_:at_ + CHUNK], BT[rows, cb, ri, :],
                                                    UT[rows, cb, c * CHUNK:(c + 1) * CHUNK], start=True, stop=True)
                ins_.then_inc(bu_full if h else bu_half, 1)

        def y(it):
            c, q = S_ITS[it]
            pe.wait_ge(hs_ready, it + 1)
            pe.wait_ge(xp_ready, it + 1)
            if it:
                pe.wait_ge(y_read, it)
            for cbl in range(2):
                for s4 in range(4):
                    for n in (0, 2):
                        ins_ = nc.tensor.matmul(BK[3][32 * s4:32 * s4 + 32, (q * 2 + cbl) * CHUNK:(q * 2 + cbl + 1) * CHUNK],
                                                CT[:, 2 * q + cbl, n // 2, 32 * s4:32 * s4 + 32],
                                                HX[it % 2][:, n, 4 * cbl + s4, :], start=n == 0, stop=n == 2)
            ins_.then_inc(y_full, 1)

        def mix(it):
            if it == -1:
                bu(0)
                bu(1)
            if 0 <= it < len(S_ITS) - 2:
                bu(it + 2)
            if 1 <= it <= len(S_ITS):
                y(it - 1)

        for zu in range(1, 4):
            def beside(s, zu=zu):
                tau = SLOTS * zu + s
                if tau == B_TICK:
                    block_turns()
                mix(tau - S_TICK)
            gemm(U_AIN + zu, G_AIN + zu, "cols", extras=beside)
        for it in range(S_END, len(S_ITS) + 1):
            mix(it)

        for c in range(2):
            gemm(U_GLU, G_GLU + c, "cols", HH, HL, s0=4 * c, s1=4 * c + 4,
                 ready=lambda s, c=c: pe.wait_ge(h_ready, s + 1) if c == 0 else None)
        for c in range(4):
            gemm(U_AOUT + c // 2, G_AOUT + c, "rows", HH, HL, s0=4 * (c % 2), s1=4 * (c % 2) + 4, kt0=CB,
                 ready=lambda s, c=c: pe.wait_ge(h_ready, 4 + s + 1) if c == 0 else None)
        transposes(TR_X1, X, lambda i: pe.wait_ge(rows_ready, 1 + i // 2))

        gemm(U_KV, G_KV, "cols", ready=split_ready(TR_X1))
        gemm(U_KV + 1, G_KV + 1, "cols")
        gemm(U_KV + 2, G_KV + 2, "cols")
        pe.wait_ge(comp_dve, 2)
        for kv_ in range(2):
            for s4 in range(4):
                s = 4 * kv_ + s4
                pe.wait_ge(lo_ready, (U_KV + 3) * SLOTS + s + 1)
                for i8 in range(8):
                    i = 8 * s4 + i8
                    first, last = i == 0, i == 31
                    for n, wa in enumerate((WH, WL)):
                        w = wa[:, s % SPLIT, :, :].rearrange("p k (i e) -> p (k i) e", e=HD)[:, i8, :]
                        r = KVC[:, kv_, :, :, i:i + CSTRIDE * (NCMP - 1) + 1:CSTRIDE].rearrange("p s h n -> p n (s h)")
                        o = BK[kv_][:, 0:NCMP * 2 * (KVH + 1)].rearrange("p (n r) -> p n r", n=NCMP)
                        ins_ = nc.tensor.matmul(o, w, r, start=first and n == 0, stop=last and n == 1)
                ins_.then_inc(slot_used, 1)
        gemm(U_KV + 4, G_KV + 3, "rows")
        pe.wait_ge(kvp_in, 32)
        pe.wait_ge(comp_act, 2)
        nc.tensor.matmul(BK[0][:, 0:NCMP * KVH], W2[:, 0, :], HC[:, 0, 0:NCMP, :].rearrange("p n h -> p (n h)"),
                         start=True, stop=True)
        for h in range(KVH):
            ins_ = nc.tensor.matmul(BK[1][0:NCMP, h * HD:(h + 1) * HD], HC[:, 1, 0:NCMP, h], W2[:, 1, :],
                                    start=True, stop=True)
        ins_.then_inc(comp_full, 1)
        gemm(U_KV + 5, G_KV + 4, "cols")
        gemm(U_KV + 6, G_KV + 5, "rows")

        pe.wait_ge(gate_split, 1)
        pe.wait_ge(comp_dve, 4)
        for kt in range(KT):
            for n, (xa, wi) in enumerate(((XH, 0), (XH, 1), (XL, 0))):
                ins_ = nc.tensor.matmul(BK[3][0:GATES, 0:TOK], GWS[wi][:, kt, :], xa[:, kt, :],
                                        start=kt == 0 and n == 0, stop=kt == KT - 1 and n == 2)
        ins_.then_inc(gate_full, 1)
        gemm(U_NSA, G_NSA, "cols")
        pe.wait_ge(gate_tanh, 1)
        for t in range(NT):
            ins_ = nc.tensor.transpose(BK[2][:, t * GATES:(t + 1) * GATES], GT[0:GATES, t * P:(t + 1) * P], ID[0:GATES, 0:GATES])
        ins_.then_inc(gate_full, 1)

        def group(g, more):
            def scores(n):
                if n == 0:
                    pe.wait_ge(acc_free, g * 4 + (G_NSA + 1))
                if n >= 2:
                    pe.wait_ge(p_ready, g * 10 + (n - 1))
                bank = BK[n % 2]
                if n < 2:
                    for h in range(4):
                        ins_ = nc.tensor.matmul(bank[:, h * 16:(h + 1) * 16], QT[:, h, n * P:(n + 1) * P],
                                                KC[:, :, bass.ds(g, 1)].rearrange("p n o -> p (n o)"), start=True, stop=True)
                else:
                    h, keys = (n - 2) % 4, KS if n < 6 else KW
                    for t in range(NT):
                        lo, w = (0, P) if t == 0 else (P, TOK)
                        nc.tensor.matmul(bank[:, lo:lo + w], QT[:, h, t * P:(t + 1) * P],
                                         keys[:, bass.ds(g, 1), 0:w].rearrange("p o k -> p (o k)"), start=True, stop=False)
                        d = lo + w - P
                        ins_ = nc.tensor.matmul(bank[:, d:d + P], ID_R[:, :], CAUSAL_R[:, :], start=False, stop=True)
                ins_.then_inc(s_full, 1)

            def turn(n):
                pe.wait_ge(p_ready, g * 10 + (n + 1))
                if n:
                    pe.wait_ge(pt_ready, g * 10 + n)
                if n < 2:
                    for h in range(4):
                        ins_ = nc.tensor.transpose(BK[2][0:16, h * P:(h + 1) * P], CP[:, n, h, :], ID)
                else:
                    for b in range(3):
                        ins_ = nc.tensor.transpose(BK[2][:, b * P:(b + 1) * P], PB_[:, n % 2, b * P:(b + 1) * P], ID)
                ins_.then_inc(t_full, 1)

            def values(n):
                pe.wait_ge(pt_ready, g * 10 + (n + 1))
                if n:
                    pe.wait_ge(o_read, g * 10 + n)
                if n < 2:
                    for h in range(4):
                        ins_ = nc.tensor.matmul(BK[3][:, h * P:(h + 1) * P], PTC[:, n % 2, h * P:(h + 1) * P],
                                                VC[:, bass.ds(g, 1), :].rearrange("p o d -> p (o d)"), start=True, stop=True)
                else:
                    v = VS if n < 6 else VW
                    for b, (t, k) in enumerate(((0, 0), (1, 0), (1, 1))):
                        ins_ = nc.tensor.matmul(BK[3][:, t * P:(t + 1) * P], PTB[:, n % 2, b * P:(b + 1) * P],
                                                v[:, k, bass.ds(g * HD, HD)], start=b < 2, stop=b != 1)
                ins_.then_inc(o_full, 1)

            for j in range(3):
                def attend(s, j=j):
                    i = 8 * j + s
                    if 2 <= i < 12:
                        values(i - 2)
                    if 1 <= i < 11:
                        turn(i - 1)
                    if i < 10:
                        scores(i)
                gemm(g * 4 + (U_NSA + 1 + j), g * 4 + (G_NSA + 1 + j), "rows", extras=attend, parity=1 + j)
            if more:
                gemm(g * 4 + (U_NSA + 4), g * 4 + (G_NSA + 4), "cols", parity=0)
            pe.wait_ge(rows_ready, g + 5)
            for i in range(2):
                for j in range(2):
                    for t in range(NT):
                        h = 2 * i + j
                        ins_ = nc.tensor.transpose(BK[i][:, (j * NT + t) * P:(j * NT + t + 1) * P],
                                                   YB[:, t, h * P:(h + 1) * P], ID)
                ins_.then_inc(tr_full, 1)
            pe.wait_ge(tr_tmp, g * 2 + (TR_Y + 2))

        with pe.Fori(0, 3) as g:
            group(g, True)
        group(3, False)

        for u in range(4):
            gemm(U_BOUT + u, G_BOUT + u, "rows", HH, HL,
                 ready=(lambda s: pe.wait_ge(split_done, TR_Y + s + 1)) if u == 0 else None)
        transposes(TR_H, HN, lambda i: pe.wait_ge(rows_ready, 9 + i // 2))

        def rotate(n):
            pair = [G_QKV, G_QKV + 1, G_QKV + 6, G_QKV + 7][n] % 2
            dst = (DQ, DK)[n % 2]
            for b in range(2):
                pe.wait_ge(rot_raw, 2 * n + b + 1)
                ins_ = nc.tensor.matmul(ACC[pair][:, b, :], const("rotate"),
                                        dst[:, 2 * b:2 * b + 2, :].rearrange("p m t -> p (m t)"), start=True, stop=True)
                ins_.then_inc(rot_full, 1)

        def diff_scores(n):
            h = n % 4
            if h == 0:
                pe.wait_ge(acc_free, G_QKV + 6 * (n // 4) + 3)
            if n:
                pe.wait_ge(a_act, 2 * n)
            if n == 4:
                pe.wait_ge(f_dve, 8)
            for m in range(2):
                for t in range(NT):
                    lo, w = (0, P) if t == 0 else (P, TOK)
                    nc.tensor.matmul(BK[m][:, lo:lo + w], DQ[64 * m:64 * m + 64, h, t * P:(t + 1) * P],
                                     DK[64 * m:64 * m + 64, h, 0:w], start=True, stop=False)
                    d = lo + w - P
                    ins_ = nc.tensor.matmul(BK[m][:, d:d + P], ID_R[:, :], CAUSAL_R[:, :], start=False, stop=True)
                ins_.then_inc(a_full, 1)

        def diff_turn(n):
            pe.wait_ge(w_dve, n + 1)
            pe.wait_ge(tr_tmp, TR_MIX + 8 * (n // 4) + n % 4)
            for b in range(3):
                ins_ = nc.tensor.transpose(BK[2][:, b * P:(b + 1) * P], P1[:, n % 2, b * P:(b + 1) * P], ID)
            ins_.then_inc(b_full, 1)

        def weigh(order, cols, ready, v, h):
            pe.wait_ge(*ready)
            if order:
                pe.wait_ge(on_dve, order)
            for b, (t, k) in enumerate(((0, 0), (1, 0), (1, 1))):
                ins_ = nc.tensor.matmul(BK[3][:, t * P:(t + 1) * P], cols[:, b * P:(b + 1) * P],
                                        v[:, k, h * HD:(h + 1) * HD], start=b < 2, stop=b != 1)
            ins_.then_inc(c_full, 1)

        def head_turn(order, turned):
            pe.wait_ge(on_dve, order + 1)
            pe.wait_ge(b_act, turned)
            if order:
                pe.wait_ge(tr_tmp, TR_MIX + order)
            for t in range(NT):
                ins_ = nc.tensor.transpose(BK[2][:, t * P:(t + 1) * P], ON[:, order % 2, t, :], ID)
            ins_.then_inc(tr_full, 1)

        def sb_scores(n):
            h = n % 4
            if h == 0:
                pe.wait_ge(acc_free, G_QKV + 6 * (n // 4) + 6)
                pe.wait_ge(a_act, 8 * (n // 4) + 8)
            else:
                pe.wait_ge(f_dve, 2 * n - 1)
            nc.tensor.matmul(BK[0][:, 0:TOK], SK[:, h, 0:P], SQ[:, h, :], start=True, stop=True)
            nc.tensor.matmul(BK[0][:, TOK:TOK + P], SK[:, h, P:TOK], SQ[:, h, P:TOK], start=True, stop=True).then_inc(sb_full, 1)

        def sb_sums(n):
            pe.wait_ge(f_dve, 2 * n + 1)
            if n % 4 == 0:
                pe.wait_ge(a_act, 8 * (n // 4) + 8)
            c = SC[:, n % 2, :]
            nc.tensor.matmul(BK[1][:, 0:384], const("later"), c, start=True, stop=False, skip_group_check=True)
            nc.tensor.matmul(BK[1][:, P:TOK], const("ones"), c[:, TOK:384], start=False, stop=True,
                             skip_group_check=True).then_inc(sb_summed, 1)

        def second_stage(kind, j, i):
            for h in range(4):
                n = 4 * j + h
                order = 8 * j + (0 if kind == "diff" else 4) + h
                if kind == "diff":
                    if i == 4 * h:
                        diff_scores(n)
                    if i == 4 * h + 1:
                        diff_turn(n)
                    if i == 4 * h + 2:
                        weigh(order, PT2[:, n % 2, :], (b_act, n + 1), DV, h)
                    if i == 4 * h + 5:
                        head_turn(order, n + 1)
                else:
                    if i == 4 * h:
                        sb_scores(n)
                    if i == 4 * h + 4:
                        sb_sums(n)
                    if i == 4 * h + 6:
                        weigh(order, SA[:, n % 2, :], (f_pool, n + 1), SV, h)
                    if i == 4 * h + 9:
                        head_turn(order, 4 * j + 4)

        for n in range(12):
            j, kind = divmod(n, 6)

            def beside(s, n=n, j=j, kind=kind):
                if s == 1 and kind in (1, 2):
                    rotate(2 * j + kind - 1)
                if kind >= 3:
                    second_stage("diff", j, 8 * (kind - 3) + s)
                elif j:
                    second_stage("sb", j - 1, 8 * kind + s)
            gemm(U_QKV + n, G_QKV + n, "rows" if kind in (2, 5) else "cols",
                 ready=split_ready(TR_H) if n == 0 else None, extras=beside)
        need = [2, 4, 10, 12, 12, 12, 14, 16]
        for n, (c, k) in enumerate(OUT_ORDER):
            if k == 0:
                pe.wait_ge(acc_free, G_WOUT + c - 1)
            if c == 0:
                pe.wait_ge(split_done, TR_MIX + need[k])
            tick(SLOTS * U_WOUT + n, n % SLOTS, "rows", c % 2, 2 * k, k == 0, k == SLOTS - 1, HH, HL)
            for i in (2 * n, 2 * n + 1):
                if i < 24:
                    second_stage("sb", 1, i)
        transposes(TR_H2, HN, lambda i: pe.wait_ge(rows_ready, 13 + i // 2))

        def quarter(q, first):
            for j in range(4):
                gemm(q * 8 + (U_MLP + j), q * 8 + (G_MLP + j), "cols", parity=j,
                     ready=split_ready(TR_H2) if first and j == 0 else None)
            for j in range(4):
                gemm(q * 8 + (U_MLP + 4 + j), q * 8 + (G_MLP + 4 + j), "rows", HH, HL, parity=j,
                     ready=(lambda s: pe.wait_ge(h_ready, q * 8 + (8 + s + 1))) if j == 0 else None)

        quarter(0, True)
        with pe.Fori(1, 4) as q:
            quarter(q, False)

    SINK = 6.283185

    @block.scalar
    def _(act):
        seen = [0]

        def high(base_, n=1):
            for _ in range(n):
                p = seen[0]
                seen[0] += 1
                s = p % SLOTS
                act.wait_ge(raw_in[s], base_ * 2 + 16 * (p // SLOTS + 1))
                if not isinstance(base_, int) or base_ + p >= SPLIT:
                    act.wait_ge(slot_used, base_ + (p - SPLIT + 1))
                nc.scalar.activation(WH[:, s % SPLIT, :, :], RAW[:, s, :, :], ACT.Copy).then_inc(hi_ready, 1)

        def unit(base_=0, first=None, extras=None, ticks=SLOTS):
            for s in range(ticks):
                high(base_)
                if s == 0 and first is not None:
                    first()
                if extras is not None:
                    extras(s)

        def done(ticks, base_=0):
            act.wait_ge(slot_used, base_ + ticks)

        def squares(c):
            cols = slice(c * COLS, (c + 1) * COLS)
            for t in range(NT):
                ins_ = nc.scalar.activation(HN[:, t, cols], X[:, t, cols], ACT.Square, accum_out=CS[:, t, c:c + 1])
            ins_.then_inc(row_squares, 1)

        def turned(first, gain=None, bias=None, i0=0, i1=8):
            for i in range(i0, i1):
                m = first + i
                act.wait_ge(tr_full, m + 1)
                if not isinstance(m, int) or m >= 2:
                    act.wait_ge(split_done, m - 1)
                if gain is None:
                    nc.scalar.activation(TMP[:, i % 2, :, :], BK[i % 4].rearrange("p (j t) -> p j t", j=2)[:, :, :], ACT.Copy).then_inc(tr_tmp, 1)
                    continue
                for j in range(2):
                    kt = 2 * i + j
                    ins_ = nc.scalar.activation(TMP[:, i % 2, j, :], BK[i % 4][:, j * TOK:(j + 1) * TOK], ACT.Identity,
                                                scale=PT[:, 0, gain + kt:gain + kt + 1],
                                                bias=0.0 if bias is None else PT[:, 0, bias + kt:bias + kt + 1])
                ins_.then_inc(tr_tmp, 1)

        rows = [(PR[0:32, 1, :], ins["a_lam_re"][0].rearrange("(s w) p -> s (w p)", w=2)),
                (PR[32:64, 1, :], ins["a_lam_im"][0].rearrange("(s w) p -> s (w p)", w=2)),
                (LDT[64:96, :], ins["a_log_dt"][0].rearrange("(s w) -> s w", w=2)),
                (PR[96:128, 1, :], ins["cmp_pos_v"])]
        for dst, src in rows:
            act.dma_start(dst, src).then_inc(ssm_in, 16)
        for i, name in enumerate(("a_b_re", "a_b_im")):
            act.dma_start(BN[:, i, :, :], ins[name][0].rearrange("(s w) p c -> (w p) s c", w=2)).then_inc(bc_in, 16)
        for i, name in enumerate(("a_c_re", "a_c_im")):
            act.dma_start(CN[:, i, :, :], ins[name][0].rearrange("(k r) c p -> (r c) k p", r=8)).then_inc(bc_in, 16)

        def params_copy(n, i):
            act.wait_ge(params_full, n)
            nc.scalar.activation(PT[:, i, :], BK[0][:, 0:P], ACT.Copy).then_inc(params_done, 1)

        turned(TR_X, i0=0, i1=4)
        high(0, LEAD)
        turned(TR_X, i0=4, i1=8)
        high(0, 2)
        params_copy(1, 1)
        act.wait_ge(params_done, 1)
        nc.scalar.activation(SP[:, 0, :], PT[:, 1, 64:96], ACT.Exp).then_inc(tab_act, 1)
        high(0, 2)
        act.wait_ge(tab_dve, 1)
        nc.scalar.activation(SP[:, 1, :], SP[:, 3, :], ACT.Exp).then_inc(tab_act, 1)
        high(0)
        act.wait_ge(tab_dve, 2)
        nc.scalar.activation(SP[:, 4:8, :], SP[:, 4:8, :], ACT.Sin, scale=SINK).then_inc(tab_act, 1)
        high(0, 2)
        act.wait_ge(bc_in, 64)
        for ri, half in enumerate(("group_half", "group_minus")):
            for w in range(2):
                ins_ = nc.scalar.activation(CBLK[:, ri, :, w, :], CN[:, ri, :, :], ACT.Copy, scale=const(half)[:, w:w + 1])
        ins_.then_inc(c_ready, 1)
        high(0, 4)
        for n in range(8):
            act.wait_ge(bc_full, n + 1)
            dst = BT if n < 4 else CT
            i = 2 * (n % 4)
            nc.scalar.activation(dst[:, i:i + 2, :, :].rearrange("p c r n -> p (c r n)"), BK[n % 4][:, :], ACT.Copy).then_inc(bc_done, 1)
        params_copy(2, 0)

        def u_copy(zu):
            done(SLOTS * (zu + 1))
            nc.scalar.activation(UT[:, 4 * zu:4 * zu + 2, :].rearrange("p m t -> p (m t)"), ACC[zu][:, 0, :], ACT.Copy).then_inc(act_part, 1)

        def table(q):
            st = slice(8 * q, 8 * q + 8)
            act.wait_ge(tab_dve, 3 + q)
            nc.scalar.activation(SIN[:, st, :], SIN[:, st, :], ACT.Sin, scale=SINK)
            nc.scalar.activation(COS[:, st, :], COS[:, st, :], ACT.Sin, scale=SINK).then_inc(tab_act, 1)

        def skip_path(q):
            act.wait_ge(acc_free, q // 2 + 1)
            for cb in (2 * q, 2 * q + 1):
                ins_ = nc.scalar.activation(YT[:, cb, :], UT[:, cb, :], ACT.Copy, scale=PT[:, 0, 64 + cb:65 + cb])
            ins_.then_inc(skip_done, 1)

        def bu_copy(it):
            act.wait_ge(bu_full, it + 1)
            if it >= 2:
                act.wait_ge(g_ready, 2 * it - 2)
            for b in range(2):
                n = 2 * it + b
                dst = BU[:, it % 2, :, :, :].rearrange("p r (c h b) t -> p (r c) h b t", c=2, h=2)[:, :, :, b, :]
                nc.scalar.activation(dst, BK[n % 3].rearrange("p (a h t) -> p a h t", a=4, h=2)[:, :, :, :], ACT.Copy).then_inc(bu_evac, 1)

        def z_epilogue(zu):
            for b in range(2):
                if b == 0:
                    done(SLOTS * (zu + 3))
                nc.scalar.activation(ZT[:, 4 * zu + 2 * b:4 * zu + 2 * b + 2, :].rearrange("p m t -> p (m t)"),
                                     ACC[zu][:, b, :], ACT.Tanh, scale=0.5).then_inc(act_part, 1)

        def gelu(half):
            act.wait_ge(y_read, 8 * half + 8)
            for b in (2 * half, 2 * half + 1):
                yb = YT[:, 2 * b:2 * b + 2, :]
                nc.scalar.activation(yb, yb, ACT.Gelu_apprx_tanh).then_inc(gelu_done, 1)

        u_copy(0)
        high(0, 2)
        table(0)
        skip_path(0)
        skip_path(1)
        high(0, S_TICK + LEAD - seen[0])
        bu_copy(0)
        bu_copy(1)
        assert seen[0] == S_TICK + LEAD, seen[0]
        for it in range(len(S_ITS)):
            if it < S_END:
                high(0)
            if 1 <= it < len(S_ITS) - 1:
                bu_copy(it + 1)
            if it == 2:
                u_copy(1)
            if it == 3:
                skip_path(2)
            if it == 11:
                skip_path(3)
            if it % 4 == 2 and it < 12:
                table(it // 4 + 1)
            if it == 12:
                gelu(0)
        z_epilogue(0)
        gelu(1)
        z_epilogue(1)
        unit()
        for c in range(2):
            done(SLOTS * U_GLU + 4 * (c + 1))
            for m in range(4):
                bias = PT[:, 0, 72 + 4 * c + m:73 + 4 * c + m]
                if c == 0 and m == 0:
                    act.wait_ge(tab_dve, 6)
                nc.scalar.activation(ACC[c][:, m // 2, (m % 2) * TOK:(m % 2 + 1) * TOK], ACC[c][:, m // 2, (m % 2) * TOK:(m % 2 + 1) * TOK],
                                     ACT.Tanh, scale=0.5, bias=bias).then_inc(act_part, 1)
        unit()
        unit()
        turned(TR_X1, gain=0, bias=16)

        def half_copy(unit_, group, dst, scale=1.0):
            done(SLOTS * (unit_ + 1))
            nc.scalar.activation(dst, ACC[group % 2][:, 0, :], ACT.Copy, scale=scale).then_inc(act_part, 1)

        def flat(x):
            return x.rearrange("p m t -> p (m t)")

        def kvc_high(n):
            done(SLOTS * (U_KV + n + 1))
            for b in range(2):
                nc.scalar.activation(flat(KVC[:, n, 0, 2 * b:2 * b + 2, :]), ACC[(G_KV + n) % 2][:, b, :], ACT.Copy).then_inc(act_part, 1)

        unit()
        unit(first=lambda: kvc_high(0))
        unit(first=lambda: kvc_high(1))
        unit(first=lambda: half_copy(U_KV + 2, G_KV + 2, flat(KS[:, 0:2, :])))
        unit()
        act.wait_ge(comp_dve, 3)
        for i in range(2):
            nc.scalar.activation(HC[:, i, 0:NCMP, :], HS[:, i, :, 0:KVH], ACT.Gelu_apprx_tanh,
                                 bias=HS[:, i, 0, KVH:KVH + 1]).then_inc(comp_act, 1)
        unit(first=lambda: half_copy(U_KV + 4, G_KV + 3, VS[:, 0, :]))
        unit(first=lambda: half_copy(U_KV + 5, G_KV + 4, flat(KW[:, 0:2, :])))
        unit(first=lambda: half_copy(U_KV + 6, G_KV + 5, VW[:, 0, :]))
        act.wait_ge(gate_full, 1)
        nc.scalar.activation(GT[0:GATES, :], BK[3][0:GATES, 0:TOK], ACT.Tanh, scale=0.5).then_inc(gate_tanh, 1)

        def group(g, more, base_):
            def probs(n):
                act.wait_ge(nm_ready, g * 10 + (n + 1))
                if n >= 2:
                    act.wait_ge(t_full, g * 10 + (n - 1))
                if n < 2:
                    nc.scalar.activation(CP[:, n, :, :], CP[:, n, :, :], ACT.Exp).then_inc(p_ready, 1)
                    return
                for t in range(NT):
                    lo, w = (0, P) if t == 0 else (P, TOK)
                    ins_ = nc.scalar.activation(PB_[:, n % 2, lo:lo + w], BK[n % 2][:, lo:lo + w], ACT.Exp,
                                                bias=NM[:, n % 2, t:t + 1], accum_out=RS[:, n % 2, t:t + 1])
                ins_.then_inc(p_ready, 1)

            def turned_probs(n):
                act.wait_ge(t_full, g * 10 + (n + 1))
                if n >= 2:
                    act.wait_ge(o_full, g * 10 + (n - 1))
                if n < 2:
                    nc.scalar.activation(PTC[0:16, n, :], BK[2][0:16, :], ACT.Copy).then_inc(pt_ready, 1)
                else:
                    nc.scalar.activation(PTB[:, n % 2, :], BK[2][:, 0:384], ACT.Copy).then_inc(pt_ready, 1)

            def z_tanh_(j):
                act.wait_ge(slot_used, g * 32 + SLOTS * (U_NSA + 2 + j))
                if j:
                    act.wait_ge(z_used, g * 3 + j)
                for t in range(NT):
                    nc.scalar.activation(ZB[:, t, :], ACC[(1 + j) % 2][:, t, :], ACT.Tanh, scale=0.5).then_inc(z_tanh, 1)

            for j in range(3 + more):
                def beside(s, j=j):
                    i = 8 * j + s
                    if 1 <= i < 11:
                        turned_probs(i - 1)
                    if i < 10:
                        probs(i)
                unit(base_, first=(lambda j=j: z_tanh_(j - 1)) if j else None, extras=beside)
            if not more:
                z_tanh_(2)
            else:
                q_epilogue(g)
            for i in range(2):
                m = g * 2 + (TR_Y + i)
                act.wait_ge(tr_full, m + 1)
                act.wait_ge(split_done, m - 1)
                nc.scalar.activation(TMP[:, i, :, :], BK[i].rearrange("p (j t) -> p j t", j=2)[:, :, :], ACT.Copy).then_inc(tr_tmp, 1)

        def q_epilogue(g):
            act.wait_ge(slot_used, g * 32 + SLOTS * (U_NSA + 5))
            nc.scalar.activation(flat(QT[:, 0:2, :]), ACC[0][:, 0, :], ACT.Copy, scale=HD ** -0.5).then_inc(act_part, 1)

        done(SLOTS * (U_NSA + 1))
        nc.scalar.activation(flat(QT[:, 0:2, :]), ACC[0][:, 0, :], ACT.Copy, scale=HD ** -0.5).then_inc(act_part, 1)
        first_tick = SLOTS * (U_NSA + 1)
        assert seen[0] == first_tick + LEAD, (seen[0], first_tick)
        with act.Fori(0, 3) as g:
            seen[0] = LEAD
            group(g, True, g * 32 + first_tick)
        seen[0] = first_tick + 96 + LEAD
        group(3, False, 0)

        for u in range(4):
            unit()
        for c in range(4):
            act.wait_ge(x_rows, c + 1)
            squares(c)
        turned(TR_H, gain=32)
        act.wait_ge(lam_dve, 1)
        nc.scalar.activation(LSM[:, 0:2], LSM[:, 0:2], ACT.Exp).then_inc(lam_act, 1)

        def raw_epilogue(n):
            unit_ = U_QKV + [0, 1, 6, 7][n]
            dst = (DQ, DK)[n % 2]
            done(SLOTS * (unit_ + 1))
            if n >= 2:
                act.wait_ge(a_full, 8)
            for b in range(2):
                nc.scalar.activation(flat(dst[:, 2 * b:2 * b + 2, :]), ACC[n % 2][:, b, :], ACT.Copy,
                                     scale=64 ** -0.5 if n % 2 == 0 else 1.0).then_inc(rot_raw, 1)

        def qkv_epilogue(n):
            j, kind = divmod(n, 6)
            if kind < 2:
                raw_epilogue(2 * j + kind)
                return
            dst = {2: DV[:, 0, :], 3: flat(SQ[:, 0:2, :]), 4: flat(SK[:, 0:2, :]), 5: SV[:, 0, :]}[kind]
            if j and kind == 2:
                act.wait_ge(c_full, 4)
            if j and kind == 3:
                act.wait_ge(c_full, 8)
            half_copy(U_QKV + n, G_QKV + n, dst, HD ** -0.5 if kind == 3 else 1.0)

        def norm_squares(order):
            act.wait_ge(c_full, order + 1)
            for t in range(NT):
                ins_ = nc.scalar.activation(JUNK[:, t, :], BK[3][:, t * P:(t + 1) * P], ACT.Square,
                                            accum_out=SM[:, order % 2, 8 + t:9 + t])
            ins_.then_inc(ss_act, 1)

        def head_copy(kind, order):
            act.wait_ge(tr_full, TR_MIX + order + 1)
            act.wait_ge(split_done, TR_MIX + order - 1)
            nc.scalar.activation(TMP[:, order % 2, 0, :], BK[2][:, 0:TOK], ACT.Identity, bias=0.0,
                                 scale=HNC[:, kind:kind + 1]).then_inc(tr_tmp, 1)

        def second_stage(kind, j, i):
            for h in range(4):
                n = 4 * j + h
                order = 8 * j + (0 if kind == "diff" else 4) + h
                if kind == "diff":
                    if i == 4 * h:
                        for m in range(2):
                            dst = (P1, P2)[m]
                            act.wait_ge(a_dve, 2 * n + m + 1)
                            if n >= 2:
                                act.wait_ge(b_full, n - 1)
                            for t in range(NT):
                                lo, w = (0, P) if t == 0 else (P, TOK)
                                ins_ = nc.scalar.activation(dst[:, n % 2, lo:lo + w], BK[m][:, lo:lo + w], ACT.Exp,
                                                            bias=SM[:, n % 2, 2 * m + t:2 * m + t + 1],
                                                            accum_out=SM[:, n % 2, 4 + 2 * m + t:5 + 2 * m + t])
                            ins_.then_inc(a_act, 1)
                    if i == 4 * h + 1:
                        act.wait_ge(b_full, n + 1)
                        if n >= 2:
                            act.wait_ge(c_full, 8 * ((n - 2) // 4) + (n - 2) % 4 + 1)
                        nc.scalar.activation(PT2[:, n % 2, :], BK[2][:, 0:384], ACT.Copy).then_inc(b_act, 1)
                    if i == 4 * h + 2:
                        norm_squares(order)
                    if i == 4 * h + 5:
                        head_copy(0, order)
                else:
                    if i == 4 * h:
                        act.wait_ge(sb_abs, n + 1)
                        a = SA[:, n % 2, :]
                        nc.scalar.activation(a, a, ACT.Exp).then_inc(sb_act, 1)
                        act.wait_ge(sb_act, 3 * n + 1)
                        nc.scalar.activation(a, a, ACT.Ln, bias=1.0).then_inc(sb_act, 1)
                    if i == 4 * h + 4:
                        act.wait_ge(f_dve, 2 * n + 2)
                        nc.scalar.activation(SA[:, n % 2, :], SB[:, n % 2, :], ACT.Exp).then_inc(sb_act, 1)
                    if i == 4 * h + 6:
                        norm_squares(order)
                    if i == 4 * h + 9:
                        head_copy(1, order)

        for n in range(12):
            j, kind = divmod(n, 6)

            def beside(s, n=n, j=j, kind=kind):
                if kind >= 3:
                    second_stage("diff", j, 8 * (kind - 3) + s)
                elif j:
                    second_stage("sb", j - 1, 8 * kind + s)
            unit(first=(lambda n=n: qkv_epilogue(n - 1)) if n else None, extras=beside)
        for n in range(12):
            high(0)
            if n == 0:
                qkv_epilogue(11)
            for i in (2 * n, 2 * n + 1):
                second_stage("sb", 1, i)
        for ticks, chunks in ((8, (0, 1)), (8, (2,)), (4, (3,))):
            high(0, ticks)
            for c in chunks:
                act.wait_ge(acc_free, G_WOUT + c + 1)
                squares(c)
        turned(TR_H2, gain=48)

        def hidden(q, j):
            act.wait_ge(slot_used, q * 64 + SLOTS * (U_MLP + j + 1))
            for b in range(2):
                if j:
                    act.wait_ge(hid_dve, q * 8 + (2 * j - 1 + b))
                nc.scalar.activation(REL[:, b, :], ACC[j % 2][:, b, :], ACT.Relu).then_inc(hid_relu, 1)
            for b in range(2):
                act.wait_ge(hid_dve, q * 8 + (2 * j + b + 1))
                kt = 4 * j + 2 * b
                nc.scalar.activation(flat(HH[:, kt:kt + 2, :]), HID[:, b, :], ACT.Copy).then_inc(hid_high, 1)

        def quarter(q, base_, last):
            for j in range(8):
                ticks = SLOTS - LEAD if last and j == 7 else SLOTS
                unit(base_, first=(lambda j=j: hidden(q, j - 1)) if 1 <= j <= 4 else None, ticks=ticks)
                if last and j >= 5:
                    act.wait_ge(acc_free, G_MLP + 24 + j)
                    squares(j - 5)

        base_ = SLOTS * U_MLP
        with act.Fori(0, 3) as q:
            seen[0] = LEAD
            quarter(q, q * 64 + base_, False)
        seen[0] = base_ + 192 + LEAD
        quarter(3, 0, True)
        act.wait_ge(acc_free, G_MLP + 32)
        squares(3)

    @block.vector
    def _(v):
        steps = Steps(v, dve_steps)
        seen = [0]
        V = nc.vector

        def low(base_, n=1):
            for _ in range(n):
                p = seen[0]
                seen[0] += 1
                v.wait_ge(hi_ready, base_ + (p + 1))
                k = p % SPLIT
                V.tensor_tensor(WL[:, k, :, :], RAW[:, p % SLOTS, :, :], WH[:, k, :, :].bitcast(F32), ALU.subtract).then_inc(lo_ready, 1)

        def unit(base_=0, first=None, extras=None, ticks=SLOTS):
            for s in range(ticks):
                low(base_)
                if s == 0 and first is not None:
                    first()
                if extras is not None:
                    extras(s)

        def flat(x):
            return x.rearrange("p m t -> p (m t)")

        def f32(x):
            return x.bitcast(F32)

        parts = [0]

        def part():
            parts[0] += 1
            v.wait_ge(act_part, parts[0])

        def split(high, low_, src, sem_=None):
            V.tensor_copy(high, src).then_inc(dve_steps, 1)
            steps.n += 1
            steps.wait()
            V.tensor_tensor(low_, src, f32(high), ALU.subtract).then_inc(sem_ or split_done, 1)

        def round_turned(i0, i1):
            for i in range(i0, i1, 2):
                v.wait_ge(tr_tmp, TR_X + i + 1)
                V.tensor_copy(XH[:, 2 * i:2 * i + 2, :], TMP[:, 0, :, :]).then_inc(x_rounded, 1)
                hi_, lo_ = (x[:, 2 * i + 2:2 * i + 4, :] for x in (XH, XL))
                v.wait_ge(tr_tmp, TR_X + i + 2)
                steps.link(V.tensor_copy(hi_, TMP[:, 1, :, :]))
                v.wait_ge(x_low, i // 2 + 1)
                V.tensor_tensor(lo_, TMP[:, 1, :, :], f32(hi_), ALU.subtract).then_inc(split_done, 2)

        def split_turned(first, i0=0, i1=8):
            for i in range(i0, i1):
                v.wait_ge(tr_tmp, first + i + 1)
                split(XH[:, 2 * i:2 * i + 2, :], XL[:, 2 * i:2 * i + 2, :], TMP[:, i % 2, :, :])

        v.wait_ge(const_in, 16)
        round_turned(0, 4)
        v.wait_ge(ssm_in, 64)
        V.tensor_copy(PR[64:96, 1, :].rearrange("s (w p) -> s w p", w=2), LDT[64:96, :].unsqueeze(2).to_broadcast([32, 2, 64])).then_inc(rows_set, 1)
        low(0, LEAD)
        round_turned(4, 8)
        low(0, 2)
        v.wait_ge(tab_act, 1)
        dt, mag, theta, a_, red, w2_ = (SP[:, i, :] for i in (0, 1, 2, 3, 8, 9))
        lr, li = PT[:, 1, 0:32], PT[:, 1, 32:64]
        V.tensor_tensor(SP[:, 3, :], lr, dt, ALU.mult).then_inc(tab_dve, 1)
        low(0, 2)
        TT = lambda o, a, b, op: steps.link(V.tensor_tensor(o, a, b, op))
        TS = lambda o, a, s1, s2, o1, o2: steps.link(V.tensor_scalar(o, a, s1, s2, o1, o2))
        TT(theta, li, dt, ALU.mult)
        TS(w2_, theta, 1.0 / TWO_PI, MAGIC, ALU.mult, ALU.add)
        TS(w2_, w2_, -MAGIC, None, ALU.add, ALU.bypass)
        steps.link(V.scalar_tensor_tensor(red, w2_, -PI_A, theta, ALU.mult, ALU.add))
        steps.link(V.scalar_tensor_tensor(red, w2_, -PI_B, red, ALU.mult, ALU.add))
        steps.link(V.scalar_tensor_tensor(red, w2_, -PI_C, red, ALU.mult, ALU.add))
        low_turns = YT[:, 6:8, :].rearrange("p c (s t) -> p (c s) t", t=CHUNK)
        r_, rh, rl = SP[:, 10, :], SP[:, 12, :], SP[:, 14, :]
        TS(r_, red, 1.0 / TWO_PI, None, ALU.mult, ALU.bypass)
        TS(rh, r_, 4096.0, MAGIC, ALU.mult, ALU.add)
        TS(rh, rh, -MAGIC, 1.0 / 4096.0, ALU.add, ALU.mult)
        TT(rl, r_, rh, ALU.subtract)

        def turns(whole, high, low_, sin_, cos_, between=lambda: None):
            TS(sin_, whole, MAGIC, -MAGIC, ALU.add, ALU.add)
            between()
            TT(sin_, high, sin_, ALU.subtract)
            TT(sin_, sin_, low_, ALU.add)
            TS(cos_, whole, 0.25, MAGIC, ALU.add, ALU.add)
            TS(cos_, cos_, -MAGIC, -0.25, ALU.add, ALU.add)
            between()
            TT(cos_, high, cos_, ALU.subtract)
            TT(cos_, cos_, low_, ALU.add)
            TS(cos_, cos_, 0.5, -0.5, ALU.min, ALU.max)
            return lambda: V.tensor_scalar(sin_, sin_, 0.5, -0.5, ALU.min, ALU.max)

        TS(SP[:, 11:16:2, :], SP[:, 10:16:2, :], float(CHUNK), None, ALU.mult, ALU.bypass)
        turns(SP[:, 10:12, :], SP[:, 12:14, :], SP[:, 14:16, :], SP[:, 4:8:2, :], SP[:, 5:8:2, :])().then_inc(tab_dve, 1)
        low(0)
        cr, ci, inv, t0, t1 = (SP[:, i, :] for i in (8, 9, 11, 13, 15))
        v.wait_ge(tab_dve, 2)
        TT(t0, lr, lr, ALU.mult)
        TT(t1, li, li, ALU.mult)
        TT(t0, t0, t1, ALU.add)
        steps.link(V.reciprocal(inv, t0))
        v.wait_ge(tab_act, 3)
        TT(SP[:, 4:8, :], SP[:, 4:8, :], mag.unsqueeze(1).to_broadcast([P, 4, NST]), ALU.mult)
        ai, ar = SP[:, 4, :], SP[:, 5, :]
        TS(ar, ar, -1.0, None, ALU.add, ALU.bypass)
        TT(t0, ar, lr, ALU.mult)
        TT(t1, ai, li, ALU.mult)
        TT(t0, t0, t1, ALU.add)
        TT(cr, t0, inv, ALU.mult)
        TT(t0, ai, lr, ALU.mult)
        TT(t1, ar, li, ALU.mult)
        TT(t0, t0, t1, ALU.subtract)
        V.tensor_tensor(ci, t0, inv, ALU.mult).then_inc(coef_ready, 1)
        low(0, 2)
        v.wait_ge(coef_ready, 1)
        v.wait_ge(bc_in, 64)
        v.wait_ge(pool_steps, 1)
        for ri, op in enumerate((ALU.subtract, ALU.add)):
            if ri == 0:
                steps.inc(V.tensor_tensor(BB[:, 0, :, :], BN[:, 0, :, :], cr.unsqueeze(2).to_broadcast([P, NST, 16]), ALU.mult))
                TT(BTMP[:, 0, :, :], BN[:, 1, :, :], ci.unsqueeze(2).to_broadcast([P, NST, 16]), ALU.mult)
            else:
                v.wait_ge(b_products, 1)
            for w in range(2):
                h = slice(64 * w, 64 * w + 64)
                if (ri, w) == (1, 1):
                    steps.wait()
                ins_ = V.tensor_tensor(BBLK[h, ri, :, w, :], BB[h, ri, :, :], BTMP[h, ri, :, :], op)
                if (ri, w) == (1, 1):
                    ins_.then_inc(blk_ready, 1)
                else:
                    steps.inc(ins_)
            low(0)
        low(0, 2)
        V.tensor_copy(CAUSAL_R[:, :], const("causal")).then_inc(dve_steps, 1)
        V.tensor_copy(ID_R[:, :], const("ident")).then_inc(dve_steps, 1)
        V.memset(MHALF[:, :], -0.5).then_inc(dve_steps, 1)
        V.memset(TINY[:, :], 0.0).then_inc(dve_steps, 1)
        steps.n += 4

        def u_copy(zu):
            part()
            v.wait_ge(slot_used, SLOTS * (zu + 1))
            V.tensor_copy(flat(UT[:, 4 * zu + 2:4 * zu + 4, :]), ACC[zu][:, 1, :]).then_inc(acc_free, 1)

        def table(q, between=lambda: None):
            st = slice(8 * q, 8 * q + 8)
            wide = [P, 8, CHUNK]
            TT(COS[:, st, :], r_[:, st].unsqueeze(2).to_broadcast(wide), const("steps").unsqueeze(1).to_broadcast(wide), ALU.mult)
            v.wait_ge(tab_pool, 2 * q + 1)
            turns(COS[:, st, :], DECAY[:, st, :], low_turns, SIN[:, st, :], COS[:, st, :], between)().then_inc(tab_dve, 1)

        u_copy(0)
        table(0, lambda: low(0))
        low(0, S_TICK + LEAD - seen[0])

        def inputs(it):
            c, q = S_ITS[it]
            if c == 0:
                v.wait_ge(tab_act, 4 + q)
            v.wait_ge(bu_evac, 2 * it + 2)
            steps.inc(V.tensor_tensor(PP[it % 2][:, 0, :, :], COS[:, 8 * q:8 * q + 8, :], BU[:, it % 2, 0, :, :], ALU.mult))

        def rotated(it):
            c, q = S_ITS[it]
            st = slice(8 * q, 8 * q + 8)
            pp, qr = PP[it % 2], QP[:, it % 2, :, :, :]
            v.wait_ge(q_ready, it + 1)
            steps.wait()
            i1 = steps.inc(V.tensor_tensor(pp[:, 0, :, :], pp[:, 0, :, :], qr[:, 0, :, :], ALU.add))
            i2 = steps.inc(V.tensor_tensor(pp[:, 1, :, :], qr[:, 1, :, :], BU[:, it % 2, 1, :, :], ALU.subtract))
            if c:
                for ri in range(2):
                    steps.wait(i1 if ri == 0 else i2)
                    steps.inc(V.tensor_tensor(pp[:, ri, :, 0:1], pp[:, ri, :, 0:1], CARRY[:, q, ri, :].unsqueeze(2), ALU.add))
            else:
                v.wait_ge(tab_pool, 2 * q + 2)
            if it:
                v.wait_ge(xp_ready, it)
            for ri in range(2):
                if ri == 0:
                    steps.wait(steps.base + steps.n - 1)
                else:
                    steps.wait()
                V.tensor_tensor_scan(G[:, ri, :, :].rearrange("p s t -> p (s t)"),
                                     DECAY[:, st, :].rearrange("p s t -> p (s t)"),
                                     pp[:, ri, :, :].rearrange("p s t -> p (s t)"), 0.0, ALU.mult, ALU.add).then_inc(g_ready, 1)

        def states(it):
            c, q = S_ITS[it]
            st = slice(8 * q, 8 * q + 8)
            v.wait_ge(g_ready, 2 * it + 2)
            if it >= 2:
                v.wait_ge(y_full, it - 1)
            hx = HX[it % 2]
            steps.inc(V.tensor_tensor(hx[:, 0, :, :], COS[:, st, :], G[:, 0, :, :], ALU.mult))
            steps.inc(V.scalar_tensor_tensor(hx[:, 2, :, :], G[:, 1, :, :], -1.0, COS[:, st, :], ALU.mult, ALU.mult))
            if c < 3:
                er, ei = G[:, 0, :, CHUNK - 1:CHUNK], G[:, 1, :, CHUNK - 1:CHUNK]
                ms_, mc = (SP[:, i, st].unsqueeze(2) for i in (6, 7))
                ct = [CTMP[:, i, :].unsqueeze(2) for i in range(4)]
                for o, a, b in ((ct[0], er, mc), (ct[1], ei, ms_), (ct[2], ei, mc), (ct[3], er, ms_)):
                    steps.inc(V.tensor_tensor(o, a, b, ALU.mult))
                steps.wait()
                steps.inc(V.tensor_tensor(CARRY[:, q, 0, :].unsqueeze(2), ct[0], ct[1], ALU.add))
                steps.inc(V.tensor_tensor(CARRY[:, q, 1, :].unsqueeze(2), ct[2], ct[3], ALU.subtract))

        def state_sums(it):
            hx = HX[it % 2]
            v.wait_ge(xp_ready, it + 1)
            steps.wait()
            V.tensor_tensor(hx[:, 0:4:2, :, :], hx[:, 0:4:2, :, :], hx[:, 1:4:2, :, :], ALU.add).then_inc(hs_ready, 1)

        def y_copy(it):
            c, q = S_ITS[it]
            v.wait_ge(y_full, it + 1)
            if c == 0:
                v.wait_ge(skip_done, q + 1)
            yc = YT[:, 2 * q:2 * q + 2, c * CHUNK:(c + 1) * CHUNK]
            V.tensor_tensor(yc, yc, BK[3][:, q * 2 * CHUNK:(q * 2 + 2) * CHUNK].rearrange("p (b t) -> p b t", b=2),
                            ALU.add).then_inc(y_read, 1)

        def z_epilogue(zu):
            for b in range(2):
                part()
                zt = flat(ZT[:, 4 * zu + 2 * b:4 * zu + 2 * b + 2, :])
                ins_ = V.scalar_tensor_tensor(zt, zt, 1.0, ACC[zu][:, b, :], ALU.add, ALU.mult)
                if b:
                    ins_.then_inc(acc_free, 1)
                else:
                    steps.inc(ins_)

        assert seen[0] == S_TICK + LEAD, seen[0]
        inputs(0)
        for it in range(len(S_ITS)):
            if it >= 2:
                y_copy(it - 2)
            if it:
                state_sums(it - 1)
            rotated(it)
            if it < S_END:
                low(0)
            if it + 1 < len(S_ITS):
                inputs(it + 1)
            states(it)
            if it == 2:
                u_copy(1)
            if it % 4 == 1 and it < 12:
                table(it // 4 + 1)
            if it == 4:
                v.wait_ge(params_done, 2)
                TS(PT[:, 0, 72:80], PT[:, 0, 72:80], 0.5, None, ALU.mult, ALU.bypass)
        z_epilogue(0)
        last = len(S_ITS) - 1
        state_sums(last)
        y_copy(last - 1)
        y_copy(last)
        for b in range(4):
            v.wait_ge(gelu_done, b + 1)
            split(HH[:, 2 * b:2 * b + 2, :], HL[:, 2 * b:2 * b + 2, :], YT[:, 2 * b:2 * b + 2, :], h_ready)
        z_epilogue(1)
        unit()
        for c in range(2):
            for b in range(2):
                part()
                part()
                g_ = flat(YT[:, 4 * c + 2 * b:4 * c + 2 * b + 2, :])
                z_ = flat(ZT[:, 4 * c + 2 * b:4 * c + 2 * b + 2, :])
                ins_ = V.scalar_tensor_tensor(g_, ACC[c][:, b, :], 1.0, g_, ALU.add, ALU.mult)
                if b:
                    ins_.then_inc(acc_free, 1)
                    v.wait_ge(acc_free, G_GLU + c + 1)
                else:
                    steps.link(ins_)
                steps.link(V.scalar_tensor_tensor(g_, g_, 0.25, z_, ALU.mult, ALU.mult))
                kt = CB + 4 * c + 2 * b
                split(HH[:, kt:kt + 2, :], HL[:, kt:kt + 2, :], YT[:, 4 * c + 2 * b:4 * c + 2 * b + 2, :], h_ready)

        def residual(unit_done, pair, chunk, alpha=None):
            v.wait_ge(slot_used, unit_done)
            for t in range(NT):
                xr = X[:, t, chunk * COLS:(chunk + 1) * COLS] if isinstance(chunk, int) else None
                if alpha is None:
                    ins_ = V.tensor_tensor(xr, xr, ACC[pair][:, t, :], ALU.add)
                else:
                    ins_ = V.scalar_tensor_tensor(xr, xr, alpha, ACC[pair][:, t, :], ALU.mult, ALU.add)
                if t:
                    ins_.then_inc(acc_free, 1)
                else:
                    steps.inc(ins_)

        def chunk_stats(chunk, group):
            v.wait_ge(acc_free, group + 1)
            for t in range(NT):
                steps.inc(V.bn_stats(STATS[:, t, chunk, :], X[:, t, chunk * COLS:(chunk + 1) * COLS]))

        def whiten(n, rows_sem):
            steps.wait()
            for t in range(NT):
                steps.inc(V.bn_aggr(MV[:, t, :], STATS[:, t, :, :]))
            steps.wait()
            V.tensor_scalar(MS[:, 0:NT], MV[:, :, 1:2].rearrange("p t o -> p (t o)"), LN_EPS, None, ALU.add, ALU.bypass).then_inc(ms_rows, 1)
            v.wait_ge(rstd_rows, n)
            for c in range(4):
                xc = X[:, :, c * COLS:(c + 1) * COLS]
                gain, bias = (GB2[:, i, c * COLS:(c + 1) * COLS] for i in range(2))
                for t in range(NT):
                    if rows_sem is rows_ready:
                        ins_ = V.tensor_scalar(xc[:, t, :], xc[:, t, :], MV[:, t, 0:1], RSTD[:, t:t + 1], ALU.subtract, ALU.mult)
                    else:
                        ins_ = V.scalar_tensor_tensor(xc[:, t, :], xc[:, t, :], MV[:, t, 0:1], gain, ALU.subtract, ALU.mult)
                    if t and rows_sem is rows_ready:
                        ins_.then_inc(rows_ready, 1)
                    else:
                        steps.inc(ins_)
                if rows_sem is rows_ready:
                    continue
                steps.wait()
                for t in range(NT):
                    ins_ = V.scalar_tensor_tensor(xc[:, t, :], xc[:, t, :], RSTD[:, t:t + 1], bias, ALU.mult, ALU.add)
                    if t:
                        ins_.then_inc(x_rows, 1)
                    else:
                        steps.inc(ins_)

        v.wait_ge(x_loaded, 16)
        for c in range(4):
            if c % 2 == 0:
                low(0, SLOTS)
            residual(SLOTS * (U_AOUT + c // 2) + 4 * (c % 2) + 4, (G_AOUT + c) % 2, c, ALPHA)
            chunk_stats(c, G_AOUT + c)
        whiten(1, rows_ready)
        split_turned(TR_X1)

        def half_copy(unit_, group, dst, scale=1.0):
            part()
            v.wait_ge(slot_used, SLOTS * (unit_ + 1))
            ins_ = V.tensor_scalar(dst, ACC[group % 2][:, 1, :], scale, None, ALU.mult, ALU.bypass)
            ins_.then_inc(acc_free, 1)

        def kvc_low(n):
            for b in range(2):
                part()
                ins_ = V.tensor_tensor(flat(KVC[:, n, 1, 2 * b:2 * b + 2, :]), ACC[(G_KV + n) % 2][:, b, :],
                                       f32(flat(KVC[:, n, 0, 2 * b:2 * b + 2, :])), ALU.subtract)
                if b:
                    ins_.then_inc(acc_free, 1)
                else:
                    steps.inc(ins_)

        unit()
        unit(first=lambda: kvc_low(0))

        def positions():
            kvc_low(1)
            v.wait_ge(acc_free, G_KV + 2)
            for i, src in enumerate((PT[:, 0, 80:112], PT[:, 1, 96:128])):
                for part_ in range(2):
                    steps.inc(V.tensor_scalar(KVC[:, i, part_, KVH, :].rearrange("p (b t) -> p b t", b=2),
                                              const("ones").unsqueeze(1).to_broadcast([P, 2, P]), 0.0, None, ALU.mult, ALU.bypass))
                steps.wait()
                hi_ = KVC[:, i, 0, KVH, 0:CBLOCK]
                steps.link(V.tensor_copy(hi_, src))
                V.tensor_tensor(KVC[:, i, 1, KVH, 0:CBLOCK], src, f32(hi_), ALU.subtract).then_inc(comp_dve, 1)

        unit(first=positions)
        unit(first=lambda: half_copy(U_KV + 2, G_KV + 2, flat(KS[:, 2:4, :])))
        unit()
        v.wait_ge(slot_used, SLOTS * (U_KV + 4))
        for i in range(2):
            sums = BK[i][:, 0:NCMP * 2 * (KVH + 1)].rearrange("p (n s h) -> p n s h", n=NCMP, s=2)
            steps.link(V.tensor_copy(HS[:, i, :, :], sums[:, :, 1, :]))
            ins_ = V.tensor_tensor(HS[:, i, :, :], HS[:, i, :, :], sums[:, :, 0, :], ALU.add)
            (steps.inc if i == 0 else (lambda x: x.then_inc(comp_dve, 1)))(ins_)
        unit(first=lambda: half_copy(U_KV + 4, G_KV + 3, VS[:, 1, :]))
        steps.inc(V.memset(KC[:, NCMP:16, :], 0.0))
        steps.inc(V.memset(VC[:, :, :], 0.0))
        steps.wait()
        v.wait_ge(comp_full, 1)
        steps.inc(V.tensor_copy(KC[:, 0:NCMP, :].rearrange("p n h -> p (n h)"), BK[0][:, 0:NCMP * KVH]))
        V.tensor_copy(VC[0:NCMP, :, :].rearrange("p h d -> p (h d)"), BK[1][0:NCMP, :]).then_inc(comp_dve, 1)
        unit(first=lambda: half_copy(U_KV + 5, G_KV + 4, flat(KW[:, 2:4, :])))
        v.wait_ge(natural_done, 1)
        v.wait_ge(gw_in, 16)
        steps.link(V.tensor_copy(GWS[0][:, :, :], GW[:, :, :]))
        V.tensor_tensor(GWS[1][:, :, :], GW[:, :, :], f32(GWS[0][:, :, :]), ALU.subtract).then_inc(gate_split, 1)
        unit(first=lambda: half_copy(U_KV + 6, G_KV + 5, VW[:, 1, :]))

        steps.inc(V.memset(PTC[:, :, :], 0.0))
        v.wait_ge(gate_full, 2)
        steps.link(V.tensor_scalar(GATE[:, :, :].rearrange("p t n -> p (t n)"), BK[2][:, 0:NT * GATES], 1.0, 0.25, ALU.add, ALU.mult))
        for t in range(NT):
            steps.inc(V.tensor_scalar(GATE[:, t, 0:HEADS], GATE[:, t, 0:HEADS], const("cmp_valid")[:, 16 * t:16 * t + 1],
                                      None, ALU.mult, ALU.bypass))
        steps.wait()

        def group(g, more, base_):
            def maxima(n):
                v.wait_ge(s_full, g * 10 + (n + 1))
                if n < 2:
                    c = CP[:, n, :, :]
                    bias = const("cmp_bias")[:, 16 * n:16 * n + 16].unsqueeze(1).to_broadcast([P, 4, 16])
                    steps.link(V.tensor_tensor(c, BK[n][:, 0:64].rearrange("p (h n) -> p h n", h=4), bias, ALU.add))
                    steps.link(V.tensor_reduce(NM[:, n, 0:4], c, AX_X, ALU.max))
                    V.tensor_tensor(c, c, NM[:, n, 0:4].unsqueeze(2).to_broadcast([P, 4, 16]), ALU.subtract).then_inc(nm_ready, 1)
                    return
                for t in range(NT):
                    lo, w = (0, P) if t == 0 else (P, TOK)
                    ins_ = V.tensor_reduce(NM[:, n % 2, t:t + 1], BK[n % 2][:, lo:lo + w], AX_X, ALU.max, negate=True)
                    if t:
                        ins_.then_inc(nm_ready, 1)
                    else:
                        steps.inc(ins_)

            def scales(n):
                v.wait_ge(p_ready, g * 10 + (n + 1))
                w = 4 if n < 2 else 2
                rs, os = RS[:, n % 2, 0:w], OS[:, n % 2, 0:w]
                if n < 2:
                    steps.link(V.tensor_reduce(rs, CP[:, n, :, :], AX_X, ALU.add))
                    gate = GATE[:, n, bass.ds(g * 4, 4)]
                else:
                    branch, h = (1 if n < 6 else 2), (n - 2) % 4
                    gate = GATE[:, :, bass.ds(g * 4 + (branch * HEADS + h), 1)].rearrange("p t o -> p (t o)")
                steps.link(V.reciprocal(rs, rs))
                steps.inc(V.tensor_tensor(os, rs, gate, ALU.mult))

            def outputs(n):
                steps.wait()
                v.wait_ge(o_full, g * 10 + (n + 1))
                for m in range(4 if n < 2 else 2):
                    branch, t, h = (0, n, m) if n < 2 else (1 if n < 6 else 2, m, (n - 2) % 4)
                    ins_ = V.tensor_scalar(OB[:, branch, t, h * HD:(h + 1) * HD], BK[3][:, m * P:(m + 1) * P],
                                           OS[:, n % 2, m:m + 1], None, ALU.mult, ALU.bypass)
                    if m == (3 if n < 2 else 1):
                        ins_.then_inc(o_read, 1)
                    else:
                        steps.inc(ins_)

            def z_epilogue(j):
                v.wait_ge(o_read, g * 10 + (2, 6, 10)[j])
                for t in range(NT):
                    v.wait_ge(z_tanh, g * 6 + (2 * j + t + 1))
                    z_ = ZB[:, t, :]
                    ins_ = V.scalar_tensor_tensor(z_, z_, 1.0, ACC[(1 + j) % 2][:, t, :], ALU.add, ALU.mult)
                    if t:
                        ins_.then_inc(acc_free, 1)
                        v.wait_ge(acc_free, g * 4 + (G_NSA + 2 + j))
                    else:
                        steps.link(ins_)
                if j == 0:
                    V.tensor_tensor(YB[:, :, :], ZB[:, :, :], OB[:, 0, :, :], ALU.mult).then_inc(z_used, 1)
                    return
                steps.link(V.tensor_tensor(ZB[:, :, :], ZB[:, :, :], OB[:, j, :, :], ALU.mult))
                v.wait_ge(z_used, g * 3 + j)
                ins_ = V.tensor_tensor(YB[:, :, :], YB[:, :, :], ZB[:, :, :], ALU.add)
                ins_.then_inc(z_used, 1)
                if j == 2:
                    v.wait_ge(z_used, g * 3 + 3)
                    V.tensor_copy(TINY[:, 0:1], TINY[:, 1:2]).then_inc(rows_ready, 1)

            for j in range(3 + more):
                def beside(s, j=j):
                    i = 8 * j + s
                    if 2 <= i < 12:
                        outputs(i - 2)
                    if i < 10:
                        maxima(i)
                    if i < 10:
                        scales(i)
                unit(base_, first=(lambda j=j: z_epilogue(j - 1)) if j else None, extras=beside)
            if more:
                q_epilogue(g, g + (parts[0] + 1))
            else:
                z_epilogue(2)
            for i in range(2):
                v.wait_ge(tr_tmp, g * 2 + (TR_Y + i + 1))
                kt = bass.ds(g * 4 + 2 * i, 2)
                split(HH[:, kt, :], HL[:, kt, :], TMP[:, i, :, :])

        def q_epilogue(g, share):
            v.wait_ge(act_part, share)
            v.wait_ge(slot_used, g * 32 + SLOTS * (U_NSA + 5))
            V.tensor_scalar(flat(QT[:, 2:4, :]), ACC[0][:, 1, :], HD ** -0.5, None, ALU.mult, ALU.bypass).then_inc(acc_free, 1)

        parts[0] += 1
        q_epilogue(-1, parts[0])
        first_tick = SLOTS * (U_NSA + 1)
        assert seen[0] == first_tick + LEAD, (seen[0], first_tick)
        n0, per = steps.n, GROUP_STEPS
        with v.Fori(0, 3) as g:
            seen[0], steps.base, steps.n = LEAD, g * per + n0, 0
            group(g, True, g * 32 + first_tick)
            assert steps.n == per, steps.n
        seen[0], steps.base, steps.n = first_tick + 96 + LEAD, 0, n0 + 3 * per
        parts[0] += 3
        group(3, False, 0)

        for c in range(4):
            low(0, SLOTS)
            residual(SLOTS * (U_BOUT + c + 1), (G_BOUT + c) % 2, c, ALPHA)
            chunk_stats(c, G_BOUT + c)
        v.wait_ge(gain_in, 96)
        whiten(2, x_rows)

        def root_mean_squares(n, squares, dst):
            v.wait_ge(row_squares, squares)
            steps.link(V.tensor_reduce(MS[:, NT:2 * NT], CS[:, :, :], AX_X, ALU.add))
            V.tensor_scalar(MS[:, 0:NT], MS[:, NT:2 * NT], 1.0 / DM, NORM_EPS, ALU.mult, ALU.add).then_inc(ms_rows, 1)
            v.wait_ge(rstd_rows, n)
            if dst is None:
                for c in range(4):
                    cols = slice(c * COLS, (c + 1) * COLS)
                    for t in range(NT):
                        V.scalar_tensor_tensor(X[:, t, cols], X[:, t, cols], RSTD[:, t:t + 1], GF[:, cols],
                                               ALU.mult, ALU.mult).then_inc(out_ready, 1)
                return
            for c in range(4):
                cols = slice(c * COLS, (c + 1) * COLS)
                for t in range(NT):
                    ins_ = V.tensor_scalar(dst[:, t, cols], X[:, t, cols], RSTD[:, t:t + 1], None, ALU.mult, ALU.bypass)
                    if t:
                        ins_.then_inc(rows_ready, 1)
                    else:
                        steps.inc(ins_)

        root_mean_squares(3, 4, HN)
        split_turned(TR_H)
        v.wait_ge(lam_in, 64)
        steps.link(V.tensor_tensor(LAM4[:, 0:4:2, :], LAM4[:, 0:4:2, :], LAM4[:, 1:4:2, :], ALU.mult))
        V.tensor_reduce(LSM[:, 0:2], LAM4[:, 0:4:2, :], AX_X, ALU.add).then_inc(lam_dve, 1)
        v.wait_ge(lam_act, 1)
        steps.link(V.tensor_tensor(LSM[:, 2:3], LSM[:, 1:2], LSM[:, 0:1], ALU.subtract))
        steps.inc(V.tensor_scalar(LSM[:, 3:4], LSM[:, 2:3], -LAM_INIT, None, ALU.add, ALU.bypass))
        v.wait_ge(hn_in, 32)
        steps.link(V.tensor_scalar(HNC[:, 0:1], HNC[:, 0:1], 1.0 - LAM_INIT, None, ALU.mult, ALU.bypass))

        def rotary(n):
            group = [G_QKV, G_QKV + 1, G_QKV + 6, G_QKV + 7][n]
            dst = (DQ, DK)[n % 2]
            for b in range(2):
                v.wait_ge(rot_full, 2 * n + b + 1)
                d = dst[:, 2 * b:2 * b + 2, :]
                wide = [P, 2, TOK]
                ins_ = V.tensor_tensor(RT[:, :, :], ACC[group % 2][:, b, :].rearrange("p (m t) -> p m t", m=2),
                                       const("sin").unsqueeze(1).to_broadcast(wide), ALU.mult)
                steps.inc(ins_)
                steps.link(V.tensor_tensor(d, d, const("cos").unsqueeze(1).to_broadcast(wide), ALU.mult))
                ins_ = V.tensor_tensor(d, d, RT[:, :, :], ALU.add)
                if b:
                    ins_.then_inc(acc_free, 1)
                else:
                    steps.link(ins_)

        def qkv_epilogue(n):
            j, kind = divmod(n, 6)
            if kind < 2:
                return
            dst = {2: DV[:, 1, :], 3: flat(SQ[:, 2:4, :]), 4: flat(SK[:, 2:4, :]), 5: SV[:, 1, :]}[kind]
            half_copy(U_QKV + n, G_QKV + n, dst, HD ** -0.5 if kind == 3 else 1.0)

        def mean_square(order):
            v.wait_ge(ss_act, order + 1)
            r = order % 2
            V.tensor_scalar(SM[:, r, 18:20], SM[:, r, 8:10], 1.0 / HD, NORM_EPS, ALU.mult, ALU.add).then_inc(ms_dve, 1)

        def normed(order):
            v.wait_ge(r_pool, order + 1)
            for t in range(NT):
                ins_ = V.tensor_scalar(ON[:, order % 2, t, :], BK[3][:, t * P:(t + 1) * P],
                                       SM[:, order % 2, 20 + t:21 + t], None, ALU.mult, ALU.bypass)
                if t:
                    ins_.then_inc(on_dve, 1)
                else:
                    steps.inc(ins_)

        def head_split(order, kt):
            v.wait_ge(tr_tmp, TR_MIX + order + 1)
            split(HH[:, kt, :], HL[:, kt, :], TMP[:, order % 2, 0, :])

        def diagonal(x):
            return x.rearrange("p (b q) -> p b q", b=3)[:, 0:3:2, :]

        def second_stage(kind, j, i):
            for h in range(4):
                n = 4 * j + h
                r = n % 2
                order = 8 * j + (0 if kind == "diff" else 4) + h
                if kind == "diff":
                    if i == 4 * h:
                        for m in range(2):
                            v.wait_ge(a_full, 2 * n + m + 1)
                            for t in range(NT):
                                lo, w = (0, P) if t == 0 else (P, TOK)
                                ins_ = V.tensor_reduce(SM[:, r, 2 * m + t:2 * m + t + 1], BK[m][:, lo:lo + w], AX_X, ALU.max, negate=True)
                                if t:
                                    ins_.then_inc(a_dve, 1)
                                else:
                                    steps.inc(ins_)
                        v.wait_ge(a_act, 2 * n + 2)
                        steps.link(V.reciprocal(SM[:, r, 12:16], SM[:, r, 4:8]))
                        steps.link(V.tensor_scalar(SM[:, r, 16:18], SM[:, r, 14:16], LSM[:, 3:4], None, ALU.mult, ALU.bypass))
                        for t in range(NT):
                            lo, w = (0, P) if t == 0 else (P, TOK)
                            p1, p2 = P1[:, r, lo:lo + w], P2[:, r, lo:lo + w]
                            steps.link(V.tensor_scalar(p1, p1, SM[:, r, 12 + t:13 + t], None, ALU.mult, ALU.bypass))
                            ins_ = V.scalar_tensor_tensor(p1, p2, SM[:, r, 16 + t:17 + t], p1, ALU.mult, ALU.add)
                            if t:
                                ins_.then_inc(w_dve, 1)
                            else:
                                steps.inc(ins_)
                    if i == 4 * h + 3:
                        mean_square(order)
                    if i == 4 * h + 4:
                        normed(order)
                    if i == 4 * h + 6:
                        head_split(order, 4 * j + h)
                else:
                    if i == 4 * h:
                        v.wait_ge(sb_full, n + 1)
                        s_ = BK[0][:, 0:384]
                        a, b, c = SA[:, r, :], SB[:, r, :], SC[:, r, :]
                        steps.link(V.tensor_scalar(b, s_, 0.0, None, ALU.min, ALU.bypass))
                        V.scalar_tensor_tensor(a, b, 2.0, s_, ALU.mult, ALU.subtract).then_inc(sb_abs, 1)
                        v.wait_ge(sb_act, 3 * n + 2)
                        steps.link(V.tensor_tensor(b, b, a, ALU.subtract))
                        steps.link(V.tensor_tensor(c, b, s_, ALU.subtract))
                        V.tensor_tensor(diagonal(c), diagonal(c), const("strict").unsqueeze(1).to_broadcast([P, 2, P]),
                                        ALU.mult).then_inc(f_dve, 1)
                    if i == 4 * h + 4:
                        v.wait_ge(sb_summed, n + 1)
                        b = SB[:, r, :]
                        V.tensor_tensor(b, b, BK[1][:, 0:384], ALU.add).then_inc(f_dve, 1)
                    if i == 4 * h + 7:
                        mean_square(order)
                    if i == 4 * h + 8:
                        normed(order)
                    if i == 4 * h + 10:
                        head_split(order, 8 + 4 * j + h)

        for n in range(12):
            j, kind = divmod(n, 6)

            def beside(s, n=n, j=j, kind=kind):
                if s == 1 and kind in (1, 2):
                    rotary(2 * j + kind - 1)
                if kind >= 3:
                    second_stage("diff", j, 8 * (kind - 3) + s)
                elif j:
                    second_stage("sb", j - 1, 8 * kind + s)
            unit(first=(lambda n=n: qkv_epilogue(n - 1)) if n else None, extras=beside)
        for n in range(12):
            low(0)
            if n == 0:
                qkv_epilogue(11)
            for i in (2 * n, 2 * n + 1):
                second_stage("sb", 1, i)
        for c, ticks in enumerate((4, 0, 8, 8)):
            low(0, ticks)
            residual(SLOTS * U_WOUT + OUT_DONE[c], (G_WOUT + c) % 2, c)
        root_mean_squares(4, 8, HN)
        split_turned(TR_H2)

        def hidden(q, j):
            for b in range(2):
                v.wait_ge(hid_relu, q * 8 + (2 * j + b + 1))
                if j:
                    v.wait_ge(hid_high, q * 8 + (2 * j + b - 1))
                V.scalar_tensor_tensor(HID[:, b, :], ACC[j % 2][:, b, :], 0.0, REL[:, b, :], ALU.max, ALU.mult).then_inc(hid_dve, 1)
            v.wait_ge(hid_dve, q * 8 + (2 * j + 2))
            V.tensor_copy(TINY[:, 0:1], TINY[:, 1:2]).then_inc(acc_free, 1)
            for b in range(2):
                kt = 4 * j + 2 * b
                v.wait_ge(hid_high, q * 8 + (2 * j + b + 1))
                V.tensor_tensor(flat(HL[:, kt:kt + 2, :]), HID[:, b, :], f32(flat(HH[:, kt:kt + 2, :])), ALU.subtract).then_inc(h_ready, 1)

        def quarter(q, base_, last):
            for j in range(8):
                def first(j=j):
                    if j <= 4:
                        hidden(q, j - 1)
                    else:
                        residual(q * 64 + SLOTS * (U_MLP + j), (j - 1) % 2, j - 5)
                ticks = SLOTS - LEAD if last and j == 7 else SLOTS
                unit(base_, first=first if j else None, ticks=ticks)
            residual(q * 64 + SLOTS * (U_MLP + 8), 1, 3)

        base_ = SLOTS * U_MLP
        n0, per = steps.n, QUARTER_STEPS
        with v.Fori(0, 3) as q:
            seen[0], steps.base, steps.n = LEAD, q * per + n0, 0
            quarter(q, q * 64 + base_, False)
            assert steps.n == per, steps.n
        seen[0], steps.base, steps.n = base_ + 192 + LEAD, 0, n0 + 3 * per
        quarter(3, 0, True)
        v.wait_ge(gain_in, 112)
        root_mean_squares(5, 12, None)

    @block.gpsimd
    def _(pool):
        GP = nc.gpsimd
        steps = Steps(pool, pool_steps)
        GP.memset(BBLK[:, :, :, :, :], 0.0).then_inc(pool_steps, 1)
        GP.memset(PR[:, 0, :], 0.0).then_inc(pool_steps, 1)
        pool.wait_ge(pool_steps, 2)
        tiles = lambda w: w.rearrange("(k p) -> k p", p=P)
        rows = [(PR[0:16, 0, :], tiles(ins["ln_g"][0])), (PR[16:32, 0, :], tiles(ins["ln_b"][0])),
                (PR[32:48, 0, :], tiles(ins["ln1_2"][0])), (PR[48:64, 0, :], tiles(ins["ln2_2"][0])),
                (PR[64:72, 0, :], tiles(ins["a_d"][0])), (PR[72:80, 0, :], tiles(ins["a_b_glu"][0])),
                (PR[80:112, 0, :], ins["cmp_pos_k"])]
        assert len(rows) == PARAM_DMAS
        for dst, src in rows:
            pool.dma_start(dst, src).then_inc(params_in, 16)
        for i, name in enumerate(("diff_head_norm_2", "sb_head_norm_2")):
            pool.dma_start(HNC[:, i:i + 1], ins[name][0].rearrange("(p o) -> p o", o=1)).then_inc(hn_in, 16)

        def table_parts(q):
            st = slice(8 * q, 8 * q + 8)
            wide = [P, 8, CHUNK]
            tt = const("steps").unsqueeze(1).to_broadcast(wide)
            pool.wait_ge(tab_dve, 2 + q)
            GP.tensor_tensor(DECAY[:, st, :], SP[:, 12, st].unsqueeze(2).to_broadcast(wide), tt, ALU.mult)
            GP.tensor_tensor(YT[:, 6:8, :].rearrange("p c (s t) -> p (c s) t", t=CHUNK),
                             SP[:, 14, st].unsqueeze(2).to_broadcast(wide), tt, ALU.mult).then_inc(tab_pool, 1)

        def decay(q):
            st = slice(8 * q, 8 * q + 8)
            wide = [P, 8, CHUNK]
            pool.wait_ge(tab_dve, 3 + q)
            GP.tensor_tensor(DECAY[:, st, :], SP[:, 1, st].unsqueeze(2).to_broadcast(wide),
                             const("not_first").unsqueeze(1).to_broadcast(wide), ALU.mult).then_inc(tab_pool, 1)

        def q_products(it):
            c, q = S_ITS[it]
            st = slice(8 * q, 8 * q + 8)
            pool.wait_ge(bu_evac, 2 * it + 2)
            if c == 0:
                pool.wait_ge(tab_act, 4 + q)
            bur, bui = BU[:, it % 2, 0, :, :], BU[:, it % 2, 1, :, :]
            GP.tensor_tensor(QP[:, it % 2, 0, :, :], SIN[:, st, :], bui, ALU.mult)
            GP.tensor_tensor(QP[:, it % 2, 1, :, :], SIN[:, st, :], bur, ALU.mult)
            GP.tensor_tensor(bui, COS[:, st, :], bui, ALU.mult).then_inc(q_ready, 1)

        def x_products(it):
            c, q = S_ITS[it]
            st = slice(8 * q, 8 * q + 8)
            pool.wait_ge(g_ready, 2 * it + 2)
            if it >= 2:
                pool.wait_ge(y_full, it - 1)
            for i in range(2):
                ins_ = GP.tensor_tensor(HX[it % 2][:, 1 + 2 * i, :, :], SIN[:, st, :], G[:, 1 - i, :, :], ALU.mult)
            ins_.then_inc(xp_ready, 1)

        for i in range(0, 8, 2):
            pool.wait_ge(x_rounded, i // 2 + 1)
            hi_, lo_ = (x[:, 2 * i:2 * i + 2, :] for x in (XH, XL))
            GP.tensor_tensor(lo_, TMP[:, 0, :, :], hi_.bitcast(F32), ALU.subtract).then_inc(x_low, 1)
        pool.wait_ge(const_in, 16)
        pool.wait_ge(bc_in, 64)
        pool.wait_ge(coef_ready, 1)
        cr, ci = (SP[:, i, :].unsqueeze(2).to_broadcast([P, NST, 16]) for i in (8, 9))
        GP.tensor_tensor(BB[:, 1, :, :], BN[:, 1, :, :], cr, ALU.mult)
        GP.tensor_tensor(BTMP[:, 1, :, :], BN[:, 0, :, :], ci, ALU.mult).then_inc(b_products, 1)
        table_parts(0)
        decay(0)
        q_products(0)
        q_products(1)
        for it in range(len(S_ITS)):
            x_products(it)
            if it % 4 == 0 and it < 12:
                table_parts(it // 4 + 1)
            if it % 4 == 2 and it < 12:
                decay(it // 4 + 1)
            if it + 2 < len(S_ITS):
                q_products(it + 2)

        def rsqrt(n):
            pool.wait_ge(ms_rows, n)
            GP.tensor_tensor(RSTD[:, 0:NT], MS[:, 0:NT], MHALF[:, 0:NT], ALU.pow).then_inc(rstd_rows, 1)

        def gains(dst, name, layer, cols):
            src = ins[name][layer] if layer is not None else ins[name]
            return dst, src[cols].partition_broadcast(P)

        pool.wait_ge(h_ready, 8)
        pool.wait_ge(y_full, 16)
        for i, name in enumerate(("cmp_w2_k", "cmp_w2_v")):
            pool.dma_start(W2[:, i, :], ins[name]).then_inc(kvp_in, 16)
        for half in range(2):
            cols = slice(half * DM // 2, (half + 1) * DM // 2)
            if half:
                pool.wait_ge(pool_steps, steps.n)
            for i, name in enumerate(("ln_g", "ln_b")):
                pool.dma_start(GB[:, i, :], ins[name][0][cols].partition_broadcast(P)).then_inc(gain_in, 16)
            if half == 0:
                rsqrt(1)
                pool.wait_ge(tr_full, TR_X1 + 8)
            pool.wait_ge(gain_in, 32 * (half + 1))
            if half == 0:
                steps.n = 2
            for t in range(NT):
                steps.link(GP.tensor_tensor(X[:, t, cols], X[:, t, cols], GB[:, 0, :], ALU.mult))
                ins_ = GP.tensor_tensor(X[:, t, cols], X[:, t, cols], GB[:, 1, :], ALU.add)
                if half and t:
                    ins_.then_inc(natural_done, 1)
                else:
                    steps.inc(ins_)
        pool.wait_ge(comp_dve, 4)
        pool.dma_start(GW[:, :, :], B_IN[:, ZW * 4:ZW * 4 + GATES].rearrange("(k p) n -> p k n", p=P)).then_inc(gw_in, 16)
        pool.wait_ge(rows_ready, 8)
        pool.wait_ge(o_read, 40)
        for i, name in enumerate(("ln_g", "ln_b")):
            pool.dma_start(GB2[:, i, :], ins[name][1].partition_broadcast(P)).then_inc(gain_in, 16)
        for i, name in enumerate(("lambda_q1_2", "lambda_k1_2", "lambda_q2_2", "lambda_k2_2")):
            pool.dma_start(LAM4[:, i, :], ins[name][0].partition_broadcast(P)).then_inc(lam_in, 16)
        rsqrt(2)
        rsqrt(3)

        def head_rsqrt(order):
            pool.wait_ge(ms_dve, order + 1)
            r = order % 2
            GP.tensor_tensor(SM[:, r, 20:22], SM[:, r, 18:20], MHALF[:, 0:2], ALU.pow).then_inc(r_pool, 1)

        def second_stage(kind, j, i):
            for h in range(4):
                n = 4 * j + h
                order = 8 * j + (0 if kind == "diff" else 4) + h
                if kind == "diff":
                    if i == 4 * h + 3:
                        head_rsqrt(order)
                else:
                    if i == 4 * h + 5:
                        pool.wait_ge(sb_act, 3 * n + 3)
                        d = SA[:, n % 2, :].rearrange("p (b q) -> p b q", b=3)[:, 0:3:2, :]
                        GP.tensor_tensor(d, d, const("strict").unsqueeze(1).to_broadcast([P, 2, P]), ALU.mult).then_inc(f_pool, 1)
                    if i == 4 * h + 7:
                        head_rsqrt(order)

        for j in range(2):
            for kind in ("diff", "sb"):
                for i in range(24):
                    second_stage(kind, j, i)
        pool.wait_ge(split_done, TR_MIX + 16)
        pool.dma_start(GF[:, :], ins["ln_f_2"].partition_broadcast(P)).then_inc(gain_in, 16)
        rsqrt(4)
        rsqrt(5)

    ctx.close()


NAMES = ["x", "a_w_in", "a_lam_re", "a_lam_im", "a_log_dt", "a_b_re", "a_b_im", "a_c_re", "a_c_im", "a_d", "a_w_glu",
         "a_b_glu", "a_w_out", "kv_w", "cmp_pos_k", "cmp_w1_k", "cmp_w2_k", "cmp_pos_v", "cmp_w1_v", "cmp_w2_v",
         "b_w_in", "b_w_out", "ln_g", "ln_b", "ln1_2", "w_in_2", "lambda_q1_2", "lambda_k1_2", "lambda_q2_2",
         "lambda_k2_2", "diff_head_norm_2", "sb_head_norm_2", "w_out_2", "ln2_2", "w_mlp_in_2", "w_mlp_out_2", "ln_f_2"]


def kernel(**inputs):
    import numpy as _np
    import concourse.bacc as _bacc
    from concourse import mybir as _mybir
    from concourse.bass_utils import run_bass_kernel_spmd as _run

    nc = _bacc.Bacc("TRN2", target_bir_lowering=False, num_devices=1)
    arrays, aps = {}, {}
    for name in NAMES + ["consts"]:
        a = constants() if name == "consts" else _np.ascontiguousarray(inputs[name])
        arrays[f"in_{name}"] = a
        aps[name] = nc.dram_tensor(f"in_{name}", a.shape, _mybir.dt.from_np(a.dtype), kind="ExternalInput").ap()
    out = nc.dram_tensor("out", (1, TOK, DM), F32, kind="ExternalOutput").ap()
    build(nc, aps, out)
    r = _run(nc, [arrays], core_ids=[0])
    return r.results[0]["out"]
```
